# Optimizing a Trainium2 kernel written in Bass

```python
import jax, jax.numpy as jnp
from jax import lax
import numpy as np

D_MODEL = 1024
BATCH = 1
SEQ = 256
DEPTH = 2

N_A_LAYERS = DEPTH // 2
N_B_LAYERS = DEPTH - N_A_LAYERS
CHUNK = 128
A_EXPAND = 2
A_WIDTH = A_EXPAND * D_MODEL
A_GROUPS = 16
A_GROUP_DIM = A_WIDTH // A_GROUPS
HEAD_DIM = 64
N_Q_HEADS = D_MODEL // HEAD_DIM
N_KV_HEADS = max(1, N_Q_HEADS // 8)
Q_PER_KV = N_Q_HEADS // N_KV_HEADS
B_WIDTH = N_Q_HEADS * HEAD_DIM
KV_WIDTH = N_KV_HEADS * HEAD_DIM
WINDOW = 128
ROPE_THETA = 10000.0
EPS = 1e-5


def rms_norm(x, g):
    xf = x.astype(jnp.float32)
    y = xf * lax.rsqrt(jnp.mean(xf * xf, axis=-1, keepdims=True) + EPS) * g.astype(jnp.float32)
    return y.astype(x.dtype)

def layer_norm(x, g, b):
    xf = x.astype(jnp.float32)
    mu = jnp.mean(xf, axis=-1, keepdims=True)
    xc = xf - mu
    var = jnp.mean(xc * xc, axis=-1, keepdims=True)
    y = xc * lax.rsqrt(var + EPS) * g.astype(jnp.float32) + b.astype(jnp.float32)
    return y.astype(x.dtype)

def rotary(x, pos):
    dh = x.shape[-1]
    inv_freq = ROPE_THETA ** (-jnp.arange(0, dh, 2, dtype=jnp.float32) / dh)
    ang = pos[:, None] * inv_freq[None, :]
    cos = jnp.cos(ang)[None, :, None, :].astype(x.dtype)
    sin = jnp.sin(ang)[None, :, None, :].astype(x.dtype)
    x1, x2 = jnp.split(x, 2, axis=-1)
    return jnp.concatenate([x1 * cos - x2 * sin, x2 * cos + x1 * sin], axis=-1)

def band(t):
    b, s, h, d = t.shape
    blk = t.reshape(b, s // CHUNK, CHUNK, h, d)
    prev = jnp.concatenate([jnp.zeros_like(blk[:, :1]), blk[:, :-1]], axis=1)
    return jnp.concatenate([prev, blk], axis=2)

def gmlp_mixer(h, w_in, ln_g, ln_b, ws, bs, w_out):
    b, s, _ = h.shape
    nc = s // CHUNK
    z = h @ w_in
    u, v, g = jnp.split(z, 3, axis=-1)
    v = layer_norm(v, ln_g, ln_b)
    v = v.reshape(b, nc, CHUNK, A_GROUPS, A_GROUP_DIM)
    causal = jnp.tril(jnp.ones((CHUNK, CHUNK), dtype=bool))
    wsm = jnp.where(causal[None], ws, jnp.zeros_like(ws)).astype(v.dtype)
    sv = jnp.einsum('gts,bcsgd->bctgd', wsm, v) + bs.T[:, :, None].astype(v.dtype)
    sv = sv.reshape(b, s, A_WIDTH)
    y = u * sv * jax.nn.silu(g)
    return y @ w_out

def swa_mixer(h, k_band, v_band, pos, w_in, b_q, sinks, w_out):
    b, s, _ = h.shape
    nb = s // CHUNK
    z = h @ w_in
    q, g = jnp.split(z, 2, axis=-1)
    q = (q + b_q).reshape(b, s, N_Q_HEADS, HEAD_DIM)
    q = rotary(q, pos).reshape(b, nb, CHUNK, N_KV_HEADS, Q_PER_KV, HEAD_DIM)
    scores = jnp.einsum('bnqhrd,bnkhd->bnhrqk', q, k_band).astype(jnp.float32) * (HEAD_DIM ** -0.5)
    qi = jnp.arange(CHUNK)[:, None]
    kj = jnp.arange(2 * CHUNK)[None, :]
    rel = kj - CHUNK - qi
    in_window = (rel <= 0) & (rel > -WINDOW)
    key_valid = (jnp.arange(nb)[:, None] * CHUNK + jnp.arange(2 * CHUNK)[None, :] - CHUNK) >= 0
    mask = in_window[None] & key_valid[:, None, :]
    scores = jnp.where(mask[None, :, None, None], scores, -jnp.inf)
    sink = sinks.astype(jnp.float32).reshape(N_KV_HEADS, Q_PER_KV)[None, None, :, :, None, None]
    m = jnp.maximum(jnp.max(scores, axis=-1, keepdims=True), sink)
    p = jnp.exp(scores - m)
    denom = jnp.sum(p, axis=-1, keepdims=True) + jnp.exp(sink - m)
    p = (p / denom).astype(v_band.dtype)
    o = jnp.einsum('bnhrqk,bnkhd->bnqhrd', p, v_band).reshape(b, s, B_WIDTH)
    y = o * jax.nn.silu(g)
    return y @ w_out

def first_inputs(seed: int = 0) -> dict:
    key = jax.random.key(seed)
    ks = jax.random.split(key, 20)
    f32 = jnp.float32
    nrm = lambda k, shp, sc: jax.random.normal(k, shp, f32) * sc
    return {
        "x": nrm(ks[0], (BATCH, SEQ, D_MODEL), 1.0),
        "a_norm_g": 1.0 + nrm(ks[1], (N_A_LAYERS, D_MODEL), 0.02),
        "a_w_in": nrm(ks[2], (N_A_LAYERS, D_MODEL, 3 * A_WIDTH), D_MODEL ** -0.5),
        "a_ln_g": 1.0 + nrm(ks[3], (N_A_LAYERS, A_WIDTH), 0.02),
        "a_ln_b": nrm(ks[4], (N_A_LAYERS, A_WIDTH), 0.02),
        "a_ws": nrm(ks[5], (N_A_LAYERS, A_GROUPS, CHUNK, CHUNK), 0.5 * CHUNK ** -0.5),
        "a_bs": 1.0 + nrm(ks[6], (N_A_LAYERS, A_GROUPS, CHUNK), 0.02),
        "a_w_out": nrm(ks[7], (N_A_LAYERS, A_WIDTH, D_MODEL), 0.5 * A_WIDTH ** -0.5),
        "kv_norm_g": 1.0 + nrm(ks[8], (D_MODEL,), 0.02),
        "w_kv": nrm(ks[9], (D_MODEL, 2 * KV_WIDTH), D_MODEL ** -0.5),
        "b_kv": nrm(ks[10], (2 * KV_WIDTH,), 0.02),
        "b_norm_g": 1.0 + nrm(ks[11], (N_B_LAYERS, D_MODEL), 0.02),
        "b_w_in": nrm(ks[12], (N_B_LAYERS, D_MODEL, 2 * B_WIDTH), D_MODEL ** -0.5),
        "b_bq": nrm(ks[13], (N_B_LAYERS, B_WIDTH), 0.02),
        "b_sinks": nrm(ks[14], (N_B_LAYERS, N_Q_HEADS), 1.0),
        "b_w_out": nrm(ks[15], (N_B_LAYERS, B_WIDTH, D_MODEL), B_WIDTH ** -0.5),
        "final_norm_g": 1.0 + nrm(ks[16], (D_MODEL,), 0.02),
    }

def first_block(x, a_norm_g, a_w_in, a_ln_g, a_ln_b, a_ws, a_bs, a_w_out, kv_norm_g, w_kv, b_kv,
              b_norm_g, b_w_in, b_bq, b_sinks, b_w_out, final_norm_g):
    b, s, _ = x.shape
    pos = jnp.arange(s, dtype=jnp.float32)
    h = x
    k_band = None
    v_band = None
    for l in range(DEPTH):
        if l < N_A_LAYERS:
            i = l
            h = h + gmlp_mixer(rms_norm(h, a_norm_g[i]), a_w_in[i], a_ln_g[i], a_ln_b[i],
                               a_ws[i], a_bs[i], a_w_out[i])
        else:
            if l == N_A_LAYERS:
                kv = rms_norm(h, kv_norm_g) @ w_kv + b_kv
                k, v = jnp.split(kv, 2, axis=-1)
                k = rotary(k.reshape(b, s, N_KV_HEADS, HEAD_DIM), pos)
                v = v.reshape(b, s, N_KV_HEADS, HEAD_DIM)
                k_band = band(k)
                v_band = band(v)
            i = l - N_A_LAYERS
            h = h + swa_mixer(rms_norm(h, b_norm_g[i]), k_band, v_band, pos,
                              b_w_in[i], b_bq[i], b_sinks[i], b_w_out[i])
    return rms_norm(h, final_norm_g)


DEPTH_2 = 1

N_HEADS_NA = 8
N_HEADS_DIL = 8
D_NA = N_HEADS_NA * HEAD_DIM
D_DIL = N_HEADS_DIL * HEAD_DIM
D_MIX = D_NA + D_DIL
GRID_W = 64
NA_ROWS_MAX = 8
NA_COLS = 16
DIL_CONFIGS = ((128, 1), (512, 4), (2048, 16))
Q_BLOCK = 128
PEER_HEADS = 8
PEER_NKEYS = 128
PEER_N = PEER_NKEYS * PEER_NKEYS
PEER_DKEY = 256
PEER_TOPK = 16
PEER_TOKEN_BLOCK = 128
EPS_2 = 1e-6


def rmsnorm(x, g):
    xf = x.astype(jnp.float32)
    y = xf * lax.rsqrt(jnp.mean(xf * xf, axis=-1, keepdims=True) + EPS_2)
    return (y * g.astype(jnp.float32)).astype(x.dtype)

def alibi_slopes(n):
    return (2.0 ** (-8.0 * (np.arange(n) + 1) / n)).astype(np.float32)

def na_index(seq):
    rows = seq // GRID_W
    wr = min(NA_ROWS_MAX, rows)
    t = np.arange(seq)
    r, c = t // GRID_W, t % GRID_W
    r0 = np.clip(r - wr // 2, 0, rows - wr)
    c0 = np.clip(c - NA_COLS // 2, 0, GRID_W - NA_COLS)
    kr = r0[:, None, None] + np.arange(wr)[None, :, None]
    kc = c0[:, None, None] + np.arange(NA_COLS)[None, None, :]
    shape = (seq, wr, NA_COLS)
    idx = np.broadcast_to(kr * GRID_W + kc, shape).reshape(seq, -1)
    dr = np.broadcast_to(kr - r[:, None, None] + NA_ROWS_MAX - 1, shape).reshape(seq, -1)
    dc = np.broadcast_to(kc - c[:, None, None] + NA_COLS - 1, shape).reshape(seq, -1)
    return idx.astype(np.int32), dr.astype(np.int32), dc.astype(np.int32)

def dilated_index(seq, window, dilation):
    half = window // (2 * dilation)
    off = dilation * np.arange(-half, half + 1)
    pos = np.arange(seq)[:, None] + off[None, :]
    valid = (pos >= 0) & (pos < seq)
    idx = np.clip(pos, 0, seq - 1).astype(np.int32)
    return idx, valid, np.abs(off).astype(np.float32)

def gathered_attention(q, k, v, idx, bias, valid):
    B, H, S, hd = q.shape
    nblk = S // Q_BLOCK
    K = idx.shape[-1]
    scale = hd ** -0.5
    q_blocks = jnp.moveaxis(q.reshape(B, H, nblk, Q_BLOCK, hd), 2, 0)
    idx_blocks = idx.reshape(nblk, Q_BLOCK, K)
    bias_blocks = jnp.moveaxis(bias.reshape(H, nblk, Q_BLOCK, K), 1, 0)
    valid_blocks = valid.reshape(nblk, Q_BLOCK, K)

    def block(args):
        qb, ib, bb, mb = args
        kg = jnp.take(k, ib, axis=2)
        vg = jnp.take(v, ib, axis=2)
        s = jnp.einsum('bhqd,bhqkd->bhqk', qb, kg, preferred_element_type=jnp.float32) * scale + bb
        s = jnp.where(mb, s, -jnp.inf)
        lse = jax.nn.logsumexp(s, axis=-1)
        p = jnp.exp(s - lse[..., None])
        o = jnp.einsum('bhqk,bhqkd->bhqd', p.astype(v.dtype), vg)
        return o, lse

    o, lse = lax.map(block, (q_blocks, idx_blocks, bias_blocks, valid_blocks))
    o = jnp.moveaxis(o, 0, 2).reshape(B, H, S, hd)
    lse = jnp.moveaxis(lse, 0, 2).reshape(B, H, S)
    return o, lse

def peer(h, wq, subkeys, u_tab, v_tab):
    B, S, D = h.shape
    T = B * S
    hf = h.reshape(T, D)
    q = (hf @ wq).reshape(T, PEER_HEADS, 2, PEER_DKEY // 2)
    sc = jnp.einsum('thpd,pnd->thpn', q, subkeys, preferred_element_type=jnp.float32)
    top_v, top_i = lax.top_k(sc, PEER_TOPK)
    cand_v = (top_v[:, :, 0, :, None] + top_v[:, :, 1, None, :]).reshape(T, PEER_HEADS, -1)
    cand_id = (top_i[:, :, 0, :, None] * PEER_NKEYS + top_i[:, :, 1, None, :]).reshape(T, PEER_HEADS, -1)
    best_v, best_j = lax.top_k(cand_v, PEER_TOPK)
    ids = jnp.take_along_axis(cand_id, best_j, axis=-1)
    gates = jax.nn.softmax(best_v, axis=-1)
    E = PEER_HEADS * PEER_TOPK
    nblk = T // PEER_TOKEN_BLOCK
    x_blocks = hf.reshape(nblk, PEER_TOKEN_BLOCK, D)
    id_blocks = ids.reshape(nblk, PEER_TOKEN_BLOCK, E)
    g_blocks = gates.reshape(nblk, PEER_TOKEN_BLOCK, E)

    def block(args):
        xb, ib, gb = args
        ub = jnp.take(u_tab, ib, axis=0)
        a = jnp.einsum('td,ted->te', xb, ub, preferred_element_type=jnp.float32)
        w = gb * jax.nn.gelu(a, approximate=False)
        vb = jnp.take(v_tab, ib, axis=0)
        return jnp.einsum('te,ted->td', w.astype(vb.dtype), vb)

    y = lax.map(block, (x_blocks, id_blocks, g_blocks))
    return y.reshape(B, S, D)

def second_inputs(seed: int = 0) -> dict:
    key = jax.random.key(seed)
    ks = jax.random.split(key, 16)
    f32 = jnp.float32
    L, D = DEPTH_2, D_MODEL

    def nrm(k, shape, std):
        return jax.random.normal(k, shape, f32) * std

    return {
        "x": nrm(ks[0], (BATCH, SEQ, D), 1.0),
        "c": nrm(ks[1], (BATCH, D), 1.0),
        "ada_w": nrm(ks[2], (L, D, 6 * D), 0.5 * D ** -0.5),
        "ada_b": nrm(ks[3], (L, 6 * D), 0.01),
        "norm1_g": 1.0 + nrm(ks[4], (L, D), 0.02),
        "w_in": nrm(ks[5], (L, D, 3 * D_MIX), D ** -0.5),
        "na_rpb": nrm(ks[6], (L, N_HEADS_NA, 2 * NA_ROWS_MAX - 1, 2 * NA_COLS - 1), 0.1),
        "out_norm_na_g": 1.0 + nrm(ks[7], (L, D_NA), 0.02),
        "out_norm_dil_g": 1.0 + nrm(ks[8], (L, D_DIL), 0.02),
        "w_out": nrm(ks[9], (L, D_MIX, D), D_MIX ** -0.5),
        "norm2_g": 1.0 + nrm(ks[10], (L, D), 0.02),
        "peer_wq": nrm(ks[11], (L, D, PEER_HEADS * PEER_DKEY), D ** -0.5),
        "peer_subkeys": nrm(ks[12], (L, 2, PEER_NKEYS, PEER_DKEY // 2), (PEER_DKEY // 2) ** -0.5),
        "peer_u": nrm(ks[13], (L, PEER_N, D), D ** -0.5),
        "peer_v": nrm(ks[14], (L, PEER_N, D), 1.0),
        "final_g": 1.0 + nrm(ks[15], (D,), 0.02),
    }

def second_block(x, c, ada_w, ada_b, norm1_g, w_in, na_rpb, out_norm_na_g, out_norm_dil_g,
              w_out, norm2_g, peer_wq, peer_subkeys, peer_u, peer_v, final_g):
    B, S, D = x.shape

    na_idx_np, na_dr, na_dc = na_index(S)
    na_idx = jnp.asarray(na_idx_np)
    na_valid = jnp.ones(na_idx_np.shape, dtype=bool)
    slopes = alibi_slopes(N_HEADS_DIL)
    dil_tables = []
    for (window, dilation) in DIL_CONFIGS:
        idx_np, valid_np, dist = dilated_index(S, window, dilation)
        bias = np.broadcast_to((-slopes[:, None] * dist[None, :])[:, None, :],
                               (N_HEADS_DIL, S, idx_np.shape[1]))
        dil_tables.append((jnp.asarray(idx_np), jnp.asarray(np.ascontiguousarray(bias)), jnp.asarray(valid_np)))

    def heads(t, n):
        return t.reshape(B, S, n, HEAD_DIM).transpose(0, 2, 1, 3)

    def merge(t):
        return t.transpose(0, 2, 1, 3).reshape(B, S, -1)

    for l in range(DEPTH_2):
        mod = jax.nn.silu(c) @ ada_w[l] + ada_b[l]
        sh1, sc1, g1, sh2, sc2, g2 = jnp.split(mod[:, None, :], 6, axis=-1)

        h = rmsnorm(x, norm1_g[l]) * (1.0 + sc1) + sh1
        proj = h @ w_in[l]
        qa, ka, va, qd, kd, vd = jnp.split(
            proj, [D_NA, 2 * D_NA, 3 * D_NA, 3 * D_NA + D_DIL, 3 * D_NA + 2 * D_DIL], axis=-1)

        na_bias = na_rpb[l][:, na_dr, na_dc].astype(jnp.float32)
        o_na, _ = gathered_attention(heads(qa, N_HEADS_NA), heads(ka, N_HEADS_NA),
                                     heads(va, N_HEADS_NA), na_idx, na_bias, na_valid)

        qdh, kdh, vdh = heads(qd, N_HEADS_DIL), heads(kd, N_HEADS_DIL), heads(vd, N_HEADS_DIL)
        outs, lses = [], []
        for (idx_d, bias_d, valid_d) in dil_tables:
            o_i, lse_i = gathered_attention(qdh, kdh, vdh, idx_d, bias_d, valid_d)
            outs.append(o_i.astype(jnp.float32))
            lses.append(lse_i)
        alpha = jax.nn.softmax(jnp.stack(lses, 0), axis=0)
        o_dil = jnp.einsum('nbhs,nbhsd->bhsd', alpha, jnp.stack(outs, 0)).astype(x.dtype)

        y = jnp.concatenate([rmsnorm(merge(o_na), out_norm_na_g[l]),
                             rmsnorm(merge(o_dil), out_norm_dil_g[l])], axis=-1) @ w_out[l]
        x = x + g1 * y

        h2 = rmsnorm(x, norm2_g[l]) * (1.0 + sc2) + sh2
        x = x + g2 * peer(h2, peer_wq[l], peer_subkeys[l], peer_u[l], peer_v[l])

    return rmsnorm(x, final_g)


def setup_inputs(seed=0):
    out = dict(first_inputs(seed))
    for name, value in second_inputs(seed + 1).items():
        if name != "x":
            out[name + "_2"] = value
    return out


def reference(
    x, a_norm_g, a_w_in, a_ln_g, a_ln_b, a_ws, a_bs, a_w_out, kv_norm_g, w_kv, b_kv, b_norm_g,
    b_w_in, b_bq, b_sinks, b_w_out, final_norm_g, c_2, ada_w_2, ada_b_2, norm1_g_2, w_in_2,
    na_rpb_2, out_norm_na_g_2, out_norm_dil_g_2, w_out_2, norm2_g_2, peer_wq_2, peer_subkeys_2,
    peer_u_2, peer_v_2, final_g_2,
):
    x = first_block(
        x, a_norm_g, a_w_in, a_ln_g, a_ln_b, a_ws, a_bs, a_w_out, kv_norm_g, w_kv, b_kv,
        b_norm_g, b_w_in, b_bq, b_sinks, b_w_out, final_norm_g,
    )
    return second_block(
        x, c_2, ada_w_2, ada_b_2, norm1_g_2, w_in_2, na_rpb_2, out_norm_na_g_2,
        out_norm_dil_g_2, w_out_2, norm2_g_2, peer_wq_2, peer_subkeys_2, peer_u_2, peer_v_2,
        final_g_2,
    )


_drawn_inputs = setup_inputs


def setup_inputs(seed=0):
    import zlib

    import numpy as np

    out = dict(_drawn_inputs(seed))
    spreads = {}
    factors = {'a_norm_g': 2.884,
     'a_ln_g': 7.664,
     'a_ln_b': 7.675,
     'a_bs': 3.901,
     'kv_norm_g': 5.844,
     'b_kv': 2.689,
     'b_norm_g': 5.599,
     'b_bq': 6.683,
     'b_sinks': 2.951,
     'norm1_g_2': 3.843,
     'na_rpb_2': 2.723,
     'out_norm_na_g_2': 60.495,
     'out_norm_dil_g_2': 57.524,
     'final_g_2': 22.632,
     'norm2_g_2': 15.012}
    for name, (base, spread) in spreads.items():
        noise = np.random.default_rng([zlib.crc32(name.encode()), seed]).standard_normal(out[name].shape)
        drawn = base * np.exp(spread * noise) if base else spread * noise
        out[name] = __import__('jax').numpy.asarray(drawn.astype(out[name].dtype))
    for name, factor in factors.items():
        out[name] = (out[name] * factor).astype(out[name].dtype)
    return out
```

```python
from contextlib import ExitStack

import numpy as np

import concourse.bass as bass
from concourse import mybir

F32 = mybir.dt.float32
F32R = mybir.dt.float32r
U32 = mybir.dt.uint32
ALU = mybir.AluOpType
ACT = mybir.ActivationFunctionType
AX_X = mybir.AxisListType.X

P = 128
T = 256
NT = T // P
D = 1024
KC = D // P
CW = KC * P
AW = 2048
AG = AW // P
HD = 64
NPAIR = 8
NMOD = 6 * D // P
NK = 128
PH = 8
TOPK = 16
NEG = -1e30
EPS_A = 1e-5
EPS_B = 1e-6

RING = 4
C_V, C_UG = 0, AG
C_AOUT = C_UG + 2 * AG
C_KV = C_AOUT + 2 * KC
C_QG = C_KV + 2
C_BOUT = C_QG + 2 * NPAIR
C_V2 = C_BOUT + KC
C_QK = C_V2 + KC
C_COUT = C_QK + 2 * NPAIR
C_WQ = C_COUT + KC
C_UV = C_WQ + 2 * PH
NCHUNK = C_UV + 2 * NK

V_AG, V_KG, V_BG, V_BQ, V_BK, V_N1, V_N2 = 0, 8, 16, 24, 32, 33, 41
V_ADAB, V_OG = 49, 49 + NMOD
V_FG = V_OG + 8
NVEC = V_FG + 8

ROWS = [TOPK // (a + 1) for a in range(TOPK)]
STARTS = [sum(ROWS[:a]) for a in range(TOPK)]
NCAND = sum(ROWS)


class Chain:

    def __init__(self, eng, sem):
        self.eng, self.sem, self.n = eng, sem, 0

    def __call__(self, ins):
        self.n += 1
        ins.then_inc(self.sem, 1)
        self.eng.wait_ge(self.sem, self.n)


def up(c, g=None, per=1):
    return c if g is None else g * per + c


def tiles(view, c, g=None, per=1, width=1):
    if g is None:
        return view[:, c:c + width]
    n = view.shape[1] // per * per
    grouped = view[:, 0:n].rearrange("p (g j) n -> p g j n", j=per)
    return grouped[:, bass.ds(g + c // per, 1), c % per:c % per + width].rearrange("p a j n -> p (a j) n")


def column(view, c, g=None, per=1):
    if g is None:
        return view[:, c:c + 1]
    n = view.shape[1] // per * per
    return view[:, 0:n].rearrange("p (g j) -> p g j", j=per)[:, bass.ds(g + c // per, 1), c % per]


def two_block_kernel(nc, stream, xT, vecs, cI, cB, rows, wsT, adaT, att_bias, skT, spill, out):
    with ExitStack() as ctx:
        def sb(name, shape, dt=F32):
            return ctx.enter_context(nc.sbuf_tensor(name, shape, dt))

        def sem(name):
            return ctx.enter_context(nc.semaphore(name))

        raw = sb("raw", [P, RING, CW])
        WH = sb("WH", [P, RING, CW], F32R)
        WL = sb("WL", [P, RING, CW], F32R)
        X1H = sb("X1H", [P, KC, T], F32R)
        X1L = sb("X1L", [P, KC, T], F32R)
        idio = sb("idio", [P, 2 * P])
        ident, iota = idio[:, 0:P], idio[:, P:2 * P]
        ones = sb("ones", [P, P])
        vec = sb("vec", [P, NVEC])
        small = sb("small", [P, 168])
        tmp = [sb(f"tmp{i}", [P, T]) for i in range(6)]
        base_wv = nc.sbuf_base
        wvH = sb("wvH", [P, 2, T], F32R)
        wvL = sb("wvL", [P, 2, T], F32R)
        base = nc.sbuf_base
        G = sb("G", [P, T, NK])
        assert nc.lookup_mloc(G).addr == base and nc.lookup_mloc(wvH).addr == base_wv
        O1 = nc.alloc_sbuf_tensor_at("O1", [P, 4, NK], F32, offset=base_wv)
        O2 = nc.alloc_sbuf_tensor_at("O2", [P, 4, NK], F32, offset=base_wv + 4 * NK * 4)

        def at(name, kib, shape, dt=F32):
            off = int(kib * 1024)
            assert off + int(np.prod(shape[1:])) * 4 <= T * NK * 4, name
            return nc.alloc_sbuf_tensor_at(name, shape, dt, offset=base + off)

        x = at("x", 0, [P, KC, T])
        X2H = at("X2H", 8, [P, KC, T], F32R)
        X2L = at("X2L", 16, [P, KC, T], F32R)
        YH = at("YH", 24, [P, AG, T], F32R)
        YL = at("YL", 40, [P, AG, T], F32R)
        ada = at("ada", 56, [P, 2, D])
        cb = at("cb", 64, [P, D])
        V = at("V", 68, [P, NT, AW])
        sq0 = at("sq0", 68, [P, KC, T])
        xg0 = at("xg0", 76, [P, KC, T])
        lng = at("lng", 84, [P, AG, P])
        lnb = at("lnb", 92, [P, AG, P])
        ws = at("ws", 100, [P, AG, P])
        bsb = at("bsb", 108, [P, AG, P])
        cBt = at("cBt", 116, [P, 9 * P])
        perm, cosT, sinT = cBt[:, 0:P], cBt[:, P:3 * P], cBt[:, 3 * P:5 * P]
        mask = cBt[:, 5 * P:9 * P]
        R = at("R", 120.5, [P, 2, T])
        nm = at("nm", 122.5, [P, T])
        nt = at("nt", 123.5, [P, T])
        vst = at("vst", 124.5, [P, NT, 8, 6])
        sinkb = at("sinkb", 125, [P, NPAIR, 4])
        bvb = at("bvb", 125.25, [P, P])
        vs = at("vs", 125.75, [P, 2, T])
        sgate = at("sgate", 68, [P, NPAIR, T])
        oT = at("oT", 68, [P, NPAIR, T])
        s = at("s", 76, [P, 4, T])
        pr = at("pr", 80, [P, 4, T])
        pT = at("pT", 84, [P, 2, 4, P])
        qs = at("qs", 88, [P, 2, T])
        qb = at("qb", 90, [P, 2, T])
        ks = at("ks", 92, [P, 2, T])
        vB = at("vB", 94, [P, NT, P])
        on = at("on", 95, [P, NT, P])
        t3 = at("t3", 96, [P, 2, T])
        gr2 = at("gr2", 98, [P, 2, T])
        bias = at("bias", 100, [P, 2, 4 * T])
        vC = at("vC", 108, [P, NT, D])
        eq = at("eq", 24, [P, PH * TOPK, NCAND])
        qt = at("qt", 68, [P, 2, T])
        sc = at("sc", 70, [P, 2, NT, NK])
        v16 = at("v16", 72, [P, NT, 2 * PH, TOPK])
        i16 = at("i16", 74, [P, NT, 2 * PH, TOPK])
        cand = at("cand", 76, [P, NT * PH, NCAND])
        cid = at("cid", 79.5, [P, NT * PH, NCAND])
        best = at("best", 83, [P, NT * PH, TOPK])
        pos = at("pos", 84, [P, NT * PH, TOPK], U32)
        posf = at("posf", 85, [P, NT * PH, TOPK])
        sid = at("sid", 86, [P, NT * PH, TOPK])
        i1 = at("i1", 87, [P, NT * PH, TOPK])
        i2 = at("i2", 88, [P, NT * PH, TOPK])
        sk = at("sk", 99, [P, 2, NK])
        sc2 = at("sc2", 90, [P, NK])
        ix8 = at("ix8", 90.5, [P, TOPK], U32)
        g2b = at("g2b", 92, [P, D])
        diags = at("diags", 100, [P, KC, P])
        zsum = at("zsum", 91.5, [P, NT * PH])
        posi = at("posi", 104, [P, NT * PH, TOPK], U32)
        xtok = at("xtok", 108, [P, NT, D])
        xt2 = at("xt2", 0, [P, NT, D])
        g2r = at("g2r", 8, [P, D])
        fgr = at("fgr", 12, [P, D])
        yo = at("yo", 16, [P, NT, D])
        sqf = at("sqf", 24, [P, NT, D])

        modT, mod = small[:, 0:NMOD], small[:, NMOD:2 * NMOD]
        s1, s2 = small[:, 96:104], small[:, 104:112]
        rtok = small[:, 112:116]
        mx, negm, dsk = small[:, 116:120], small[:, 120:124], small[:, 124:128]
        small_es = small[:, 128:136].rearrange("p (a k) -> p a k", a=2)
        small_den = small[:, 136:144].rearrange("p (a k) -> p a k", a=2)
        small_rc = small[:, 144:152].rearrange("p (a k) -> p a k", a=2)
        mv = small[:, 152:156]
        rstd, st0, st1 = small[:, 156:158], small[:, 158:160], small[:, 160:162]
        st2, fsum = small[:, 162:163], small[:, 164:166]

        ps = ctx.enter_context(nc.psum_tensor("ps", [P, 8, 512], F32))

        raw_in = [sem(f"raw_in{i}") for i in range(RING)]
        h_done, l_done, chunk_done = sem("h_done"), sem("l_done"), sem("chunk_done")
        x_in, c_in, a_in, b_in, sk_in = sem("x_in"), sem("c_in"), sem("a_in"), sem("b_in"), sem("sk_in")
        ada_in = [sem(f"ada_in{i}") for i in range(2)]
        bias_in = [sem(f"bias_in{i}") for i in range(2)]
        ada_used = sem("ada_used")
        dve_link, act_link = sem("dve_link"), sem("act_link")
        sum_ready, psn_ready, m_ready, root_ready, r_ready = (
            sem("sum_ready"), sem("psn_ready"), sem("m_ready"), sem("root_ready"), sem("r_ready"))
        rt_ready, rtok_ready = sem("rt_ready"), sem("rtok_ready")
        ones_ready, cb_ready = sem("ones_ready"), sem("cb_ready")
        sq_ready, sacc_done, x_ready = sem("sq_ready"), sem("sacc_done"), sem("x_ready")
        xg_ready, xh_ready, xl_ready = sem("xg_ready"), sem("xh_ready"), sem("xl_ready")
        yf_ready, yh_ready, yl_ready = sem("yf_ready"), sem("yh_ready"), sem("yl_ready")
        v_mm, v_out, st_done = sem("v_mm"), sem("v_out"), sem("st_done")
        ln_m, ln_root, xhat_ready = sem("ln_m"), sem("ln_root"), sem("xhat_ready")
        ws_ready, vs_ready, sv_mm = sem("ws_ready"), sem("vs_ready"), sem("sv_mm")
        gr_ready, sg_ready, svb_ready, m_gate = sem("gr_ready"), sem("sg_ready"), sem("svb_ready"), sem("m_gate")
        pool_link = sem("pool_link")
        kv_mm, k_ready, v_ready = sem("kv_mm"), sem("k_ready"), sem("v_ready")
        qb_ready, rope_mm, rope_s, rope_c, q_ready, q_add = (
            sem("qb_ready"), sem("rope_mm"), sem("rope_s"), sem("rope_c"), sem("q_ready"), sem("q_add"))
        s_mm, s_ready, mx_ready, negm_ready, dsk_ready = (
            sem("s_mm"), sem("s_ready"), sem("mx_ready"), sem("negm_ready"), sem("dsk_ready"))
        p_ready, es_ready, den_ready, rc_ready = sem("p_ready"), sem("es_ready"), sem("den_ready"), sem("rc_ready")
        pt_mm, pt_ready, o_mm, on_ready, ot_mm, ot_done = (
            sem("pt_mm"), sem("pt_ready"), sem("o_mm"), sem("on_ready"), sem("ot_mm"), sem("ot_done"))
        g_ready, gate_ready = sem("g_ready"), sem("gate_ready")
        qt_ready, sc_mm, sc_ready, sc_used = sem("qt_ready"), sem("sc_mm"), sem("sc_ready"), sem("sc_used")
        tr_mm, tr_ready, spill_done = sem("tr_mm"), sem("tr_ready"), sem("spill_done")
        lists_ready, lt_mm, lt_ready, exp_in, exp_ready = (
            sem("lists_ready"), sem("lt_mm"), sem("lt_ready"), sem("exp_in"), sem("exp_ready"))
        hot_ready, gate_mm, gate_out = sem("hot_ready"), sem("gate_mm"), sem("gate_out")
        gelu_ready, w_ready, wh_ready, wl_ready = (
            sem("gelu_ready"), sem("w_ready"), sem("wh_ready"), sem("wl_ready"))
        fin_in, fy_ready, fsum_ready, out_ready, out_done = (
            sem("fin_in"), sem("fy_ready"), sem("fsum_ready"), sem("out_ready"), sem("out_done"))

        ada_sum, ln_r, t_ready, mxs_ready, mt_ready = (
            sem("ada_sum"), sem("ln_r"), sem("t_ready"), sem("mxs_ready"), sem("mt_ready"))
        vg_ready, mg_ready, acc_clear, diag_ready = (
            sem("vg_ready"), sem("mg_ready"), sem("acc_clear"), sem("diag_ready"))

        block = ctx.enter_context(nc.Block())

        @block.sync
        def _(sp):
            def load(c, g=None, group=None, j=0):
                if g is not None or c >= RING:
                    sp.wait_ge(l_done, up(c - RING + 1, g, RING))
                slot = c % RING
                if g is None:
                    sp.dma_start(raw[:, slot, :], stream[c]).then_inc(raw_in[slot], 16)
                else:
                    sp.dma_start(raw[:, slot:slot + 1, :], group[j][:, bass.ds(g, 1), :]).then_inc(raw_in[slot], 16)

            def groups(c, n):
                return stream[c:c + RING * n].rearrange("(g j) p n -> j p g n", j=RING)

            def load_ada(n, g=None, group=None):
                if g is not None or n >= 2:
                    sp.wait_ge(ada_used, up(n - 1, g, 2))
                if g is None:
                    sp.dma_start(ada[:, n % 2, :], adaT[n]).then_inc(ada_in[n % 2], 16)
                else:
                    sp.dma_start(ada[:, n % 2:n % 2 + 1, :], group[n % 2][:, bass.ds(g, 1), :]).then_inc(ada_in[n % 2], 16)

            def ada_groups(n, k):
                return adaT[n:n + 2 * k].rearrange("(g j) p n -> j p g n", j=2)

            def row(lo, n):
                return rows[lo:lo + n].partition_broadcast(P)

            sp.dma_start(x[:, :, :], xT).then_inc(x_in, 16)
            sp.dma_start(vec[:, :], vecs).then_inc(x_in, 16)
            load(0)
            load(1)
            sp.dma_start(idio[:, :], cI).then_inc(c_in, 16)
            sp.dma_start(cb[:, :], row(0, D)).then_inc(c_in, 16)
            load(2)
            load(3)
            load_ada(0)
            load_ada(1)
            sp.dma_start(ws[:, :, :], wsT).then_inc(a_in, 16)
            sp.dma_start(lng[:, :, :].rearrange("p g n -> p (g n)"), row(D, AW)).then_inc(a_in, 16)
            sp.dma_start(lnb[:, :, :].rearrange("p g n -> p (g n)"), row(D + AW, AW)).then_inc(a_in, 16)
            sp.dma_start(bsb[:, :, :].rearrange("p g n -> p (g n)"), row(D + 2 * AW, AW)).then_inc(a_in, 16)
            sp.dma_start(cBt[:, :], cB).then_inc(b_in, 16)
            sp.dma_start(bvb[:, :], row(D + 3 * AW, P)).then_inc(b_in, 16)
            sp.dma_start(sinkb[:, :, :].rearrange("p m k -> p (m k)"), row(D + 3 * AW + P, 32)).then_inc(b_in, 16)
            cs, an = groups(RING, 16), ada_groups(2, 16)
            with sp.Fori(0, 16) as g:
                for j in range(RING):
                    load(RING + j, g, cs, j)
                    if j % 2:
                        load_ada(2 + j // 2, g, an)
            load(68)
            load(69)
            cs, an = groups(70, 4), ada_groups(34, 4)
            with sp.Fori(0, 4) as g:
                for j in range(RING):
                    load(70 + j, g, cs, j)
                    if j % 2:
                        load_ada(34 + j // 2, g, an)
            cs = groups(86, 4)
            with sp.Fori(0, 4) as g:
                for j in range(RING):
                    load(86 + j, g, cs, j)
            for m in range(2):
                sp.dma_start(bias[:, m, :], att_bias[m]).then_inc(bias_in[m], 16)
            cs, an = groups(102, 3), ada_groups(42, 3)
            bs = att_bias[2:8].rearrange("(g j) p n -> j p g n", j=2)
            with sp.Fori(0, 3) as g:
                for j in range(RING):
                    load(102 + j, g, cs, j)
                    if j % 2:
                        load_ada(42 + j // 2, g, an)
                        k = j // 2
                        sp.wait_ge(s_ready, up(8 + k + 1, g, 2))
                        sp.dma_start(bias[:, k:k + 1, :], bs[k][:, bass.ds(g, 1), :]).then_inc(bias_in[k], 16)
            sp.dma_start(sk[:, :, :], skT).then_inc(sk_in, 16)
            rest = (NCHUNK - 114) // RING
            cs = groups(114, rest)
            with sp.Fori(0, rest) as g:
                for j in range(RING):
                    load(114 + j, g, cs, j)
            sp.wait_ge(w_ready, NK)
            sp.wait_ge(spill_done, 32)
            sp.dma_start(xt2[:, :, :].rearrange("p t n -> p (t n)"), spill[:, 0:NT * D]).then_inc(fin_in, 16)
            sp.dma_start(g2r[:, :], spill[:, NT * D:NT * D + D]).then_inc(fin_in, 16)
            sp.dma_start(fgr[:, :], row(D + 3 * AW + P + 32, D)).then_inc(fin_in, 16)
            for t in range(NT):
                sp.wait_ge(out_ready, t + 1)
                sp.dma_start(out[t * P:(t + 1) * P, :], yo[:, t, :]).then_inc(out_done, 16)
            sp.wait_ge(out_done, 16 * NT)

        @block.scalar
        def _(act):
            link = Chain(act, act_link)

            def hi(c, g=None):
                slot = c % RING
                act.wait_ge(raw_in[slot], up((c // RING + 1) * 16, g, 16))
                if g is not None or c >= RING:
                    act.wait_ge(chunk_done, up(c - RING + 1, g, RING))
                act.activation(WH[:, slot, :], raw[:, slot, :], ACT.Copy).then_inc(h_done, 1)

            def root(k):
                act.wait_ge(m_ready, k + 1)
                act.activation(nt[:, :], nm[:, :], ACT.Sqrt).then_inc(root_ready, 1)

            act.wait_ge(x_in, 32)
            act.activation(sq0[:, :, :], x[:, :, :], ACT.Square).then_inc(sq_ready, 1)
            for kc in range(KC):
                act.wait_ge(xg_ready, kc + 1)
                act.activation(X1H[:, kc, :], xg0[:, kc, :], ACT.Copy).then_inc(xh_ready, 1)
            for c in range(3):
                hi(c)
            root(0)
            act.wait_ge(c_in, 32)
            act.activation(cb[:, :], cb[:, :], ACT.Silu).then_inc(cb_ready, 1)

            def v_step(q, g=None):
                hi(2 * q + 3, g)
                act.wait_ge(chunk_done, up(2 * q + 2, g, 4))
                act.wait_ge(rtok_ready, 1)
                for t in range(NT):
                    act.activation(tiles(V[:, t, :].rearrange("p (q n) -> p q n", n=T), q, g, 2),
                                   ps[:, q % 2 * 2 + t:q % 2 * 2 + t + 1, 0:T], ACT.Copy,
                                   scale=rtok[:, t:t + 1]).then_inc(v_out, 1)
                hi(2 * q + 4, g)

            for q in range(2):
                v_step(q)
            with act.Fori(1, 4) as g:
                for q in range(2):
                    v_step(q, g)
            act.wait_ge(ln_m, 1)
            act.activation(st1, st0, ACT.Sqrt).then_inc(ln_root, 1)

            def ug_step(n, g):
                hi(19 + 2 * n, g)
                act.wait_ge(gr_ready, up(n + 1, g, 2))
                act.activation(tmp[n % 2][:, :], tmp[n % 2][:, :], ACT.Silu).then_inc(sg_ready, 1)
                hi(20 + 2 * n, g)
                act.wait_ge(yf_ready, up(n + 1, g, 2))
                act.activation(tiles(YH, n, g, 2), tmp[4 + n % 2][:, :].unsqueeze(1), ACT.Copy).then_inc(yh_ready, 1)

            with act.Fori(0, AG // 2) as g:
                for n in range(2):
                    ug_step(n, g)

            def sq_tile(k, src, ready, value, n, g, per):
                act.wait_ge(ready, up(value, g, per))
                if not (g is None and k == 0):
                    act.wait_ge(sacc_done, up(k, g, per))
                act.activation(tmp[4][:, :].unsqueeze(1), tiles(src, n, g, per), ACT.Square).then_inc(sq_ready, 1)

            def aout_step(n, g=None):
                hi(51 + 2 * n, g)
                hi(52 + 2 * n, g)
                sq_tile(n, x, x_ready, n + 1, n, g, 2)
                for i, XH in enumerate((X1H, X2H)):
                    act.wait_ge(xg_ready, up(KC + 2 * n + i + 1, g, 4))
                    act.activation(tiles(XH, n, g, 2), tmp[2 * i + n % 2][:, :].unsqueeze(1),
                                   ACT.Copy).then_inc(xh_ready, 1)

            for n in range(2):
                aout_step(n)
            with act.Fori(1, 4) as g:
                for n in range(2):
                    aout_step(n, g)
            hi(67)
            root(1)
            hi(68)

            def exps(p, g, sinks):
                par = p % 2
                act.wait_ge(dsk_ready if sinks else negm_ready, up(p + 1, g, 2))
                if g is not None or p >= 1:
                    act.wait_ge(pt_mm, up(p, g, 2))
                if g is not None or p >= 2:
                    act.wait_ge(rc_ready, up(p - 1, g, 2))
                for k in range(4):
                    act.activation(pr[:, k, :], s[:, k, :], ACT.Exp, bias=negm[:, k:k + 1],
                                   accum_out=small_den[:, par, k:k + 1]).then_inc(p_ready, 1)
                if sinks:
                    act.activation(small_es[:, par, :], dsk, ACT.Exp).then_inc(es_ready, 1)

            def pt_out(p, g):
                act.wait_ge(pt_mm, up(p + 1, g, 2))
                if g is not None or p >= 1:
                    act.wait_ge(o_mm, up(p, g, 2))
                for h in range(2):
                    act.activation(pT[:, h, :, :].rearrange("p k t -> p (k t)"), ps[:, 6 + h, :],
                                   ACT.Copy).then_inc(pt_ready, 1)

            def swa_step(m, g=None):
                if m < 8:
                    hi(69 + 2 * m, g)
                if 1 <= m <= 8:
                    exps(m - 1, g, True)
                if m < 8:
                    hi(70 + 2 * m, g)
                    act.wait_ge(gr_ready, up(AG + m + 1, g, 2))
                    act.activation(tiles(sgate, m, g, 2), gr2[:, m % 2:m % 2 + 1, :], ACT.Silu).then_inc(gate_ready, 1)
                if 1 <= m <= 8:
                    pt_out(m - 1, g)
                if m >= 2:
                    act.wait_ge(yf_ready, up(AG + m - 1, g, 2))
                    act.activation(tiles(YH, m - 2, g, 2), tmp[4 + m % 2][:, :].unsqueeze(1),
                                   ACT.Copy).then_inc(yh_ready, 1)

            def steps(eng, step):
                for m in range(4):
                    step(m)
                with eng.Fori(1, 3) as g:
                    step(2, g)
                    step(3, g)
                step(8)
                step(9)

            steps(act, swa_step)

            def bout_step(n, g):
                hi(85 + n, g)
                sq_tile(8 + n, x, x_ready, 8 + n + 1, n, g, 4)

            with act.Fori(0, 2) as g:
                for n in range(4):
                    bout_step(n, g)
            root(2)
            with act.Fori(0, 4) as g:
                for n in range(2):
                    sq_tile(16 + n, x, x_ready, 16 + n + 1, n, g, 2)
            root(3)

            def x1_high(n0, g):
                for j in range(2):
                    act.wait_ge(xg_ready, up(n0 + j + 1, g, 2))
                    act.activation(tiles(X1H, j, g, 2), tmp[j][:, :].unsqueeze(1), ACT.Copy).then_inc(xh_ready, 1)

            with act.Fori(0, 4) as g:
                x1_high(3 * KC, g)

            def v2_step(q, g):
                hi(C_V2 + 2 * q + 3, g)
                act.wait_ge(chunk_done, up(C_V2 + 2 * q + 2, g, 4))
                for t in range(NT):
                    act.activation(tiles(vC[:, t, :].rearrange("p (q n) -> p q n", n=T), q, g, 2),
                                   ps[:, q % 2 * 2 + t:q % 2 * 2 + t + 1, 0:T], ACT.Copy).then_inc(v_out, 1)
                hi(C_V2 + 2 * q + 4, g)

            with act.Fori(0, 2) as g:
                for q in range(2):
                    v2_step(q, g)

            def mix_step(m, g=None):
                if m < 8:
                    hi(C_QK + 2 * m + 3, g)
                    act.wait_ge(chunk_done, up(C_QK + 2 * m + 1, g, 4))
                    act.wait_ge(s_mm, up(8 + m - 1, g, 2))
                    act.activation(qs[:, m % 2, :], ps[:, m % 2, 0:T], ACT.Copy).then_inc(qt_ready, 1)
                if 1 <= m <= 8:
                    exps(8 + m - 1, g, False)
                if m < 8:
                    hi(C_QK + 2 * m + 4, g)
                if 1 <= m <= 8:
                    pt_out(8 + m - 1, g)
                if m >= 2:
                    sq_tile(24 + m - 2, oT, ot_done, m - 1, m - 2, g, 2)

            steps(act, mix_step)
            for k in range(2):
                root(4 + k)
                with act.Fori(0, 2) as g:
                    for j in range(2):
                        n = 4 * k + j
                        act.wait_ge(yf_ready, up(AG + 8 + n + 1, g, 2))
                        act.activation(tiles(YH, n, g, 2), tmp[j][:, :].unsqueeze(1), ACT.Copy).then_inc(yh_ready, 1)

            def cout_step(n, g):
                hi(117 + n, g)
                sq_tile(32 + n, x, x_ready, 24 + n + 1, n, g, 4)

            with act.Fori(0, 2) as g:
                for n in range(4):
                    cout_step(n, g)
            root(6)
            with act.Fori(0, 4) as g:
                x1_high(4 * KC, g)
            act.wait_ge(tr_mm, 1)
            for i in range(4):
                link(act.activation(xtok[:, i // 2, i % 2 * 512:i % 2 * 512 + 512], ps[:, 4 + i, :], ACT.Copy))
            act.dma_start(spill[:, 0:NT * D], xtok[:, :, :].rearrange("p t n -> p (t n)")).then_inc(spill_done, 16)
            act.wait_ge(tr_mm, 2)
            for i in range(2):
                link(act.activation(g2b[:, i * 512:i * 512 + 512], ps[:, 6 + i, :], ACT.Copy))
            act.dma_start(spill[:, NT * D:NT * D + D], g2b[:, :]).then_inc(spill_done, 16)

            def wq_step(n, g=None):
                hi(125 + n, g)
                act.wait_ge(chunk_done, up(123 + n, g, 4))
                if g is not None or n >= 2:
                    act.wait_ge(sc_mm, up(n - 1, g, 4))
                act.activation(qt[:, n % 2, :], ps[:, n % 2, 0:T], ACT.Copy).then_inc(qt_ready, 1)
                act.wait_ge(sc_mm, up(n + 1, g, 4))
                if g is not None or n >= 2:
                    act.wait_ge(sc_used, up(n - 1, g, 4))
                act.activation(sc[:, n % 2, :, :].rearrange("p t n -> p (t n)"), ps[:, 2 + n % 2, 0:T],
                               ACT.Copy).then_inc(sc_ready, 1)

            for n in range(4):
                wq_step(n)
            with act.Fori(1, 4) as g:
                for n in range(4):
                    wq_step(n, g)
            act.wait_ge(exp_in, 1)
            act.activation(best[:, :, :], best[:, :, :], ACT.Exp).then_inc(exp_ready, 1)
            act.wait_ge(lt_mm, 1)
            for i in range(3):
                act.activation(tmp[i][:, :], ps[:, 4 + i, 0:T], ACT.Copy).then_inc(lt_ready, 1)
            act.wait_ge(spill_done, 32)

            def gate_step(n, g):
                act.wait_ge(gate_mm, up(4 * n + 4, g, 8))
                act.activation(tiles(G[:, :, :].rearrange("p (q t) n -> p q (t n)", t=4), n, g, 2),
                               ps[:, n:n + 1, :], ACT.Copy).then_inc(gate_out, 1)

            with act.Fori(0, T // 8) as g:
                for n in range(2):
                    gate_step(n, g)

            def gelu(j, g=None):
                act.wait_ge(chunk_done, C_UV + 1 if j == 0 else up(C_UV + 2 * j, g, 4))
                if g is not None or j >= 2:
                    act.wait_ge(wl_ready, up(j - 1, g, 2))
                act.activation(tmp[j % 2][:, :], ps[:, j % 2, 0:T], ACT.Gelu).then_inc(gelu_ready, 1)

            def w_high(j, g=None):
                act.wait_ge(w_ready, up(j + 1, g, 2))
                if g is not None or j >= 2:
                    act.wait_ge(chunk_done, up(C_UV + 2 * j - 1, g, 4))
                act.activation(wvH[:, j % 2, :], tmp[2 + j % 2][:, :], ACT.Copy).then_inc(wh_ready, 1)

            hi(141)
            gelu(0)
            w_high(0)
            hi(142)
            hi(143)
            def column_step(j, g=None):
                gelu(j, g)
                w_high(j, g)
                hi(C_UV + 4 + 2 * j, g)
                hi(C_UV + 5 + 2 * j, g)

            column_step(1)
            column_step(2)
            with act.Fori(1, (NK - 4) // 2) as g:
                column_step(1, g)
                column_step(2, g)
            for j in (NK - 3, NK - 2, NK - 1):
                gelu(j)
                w_high(j)
                if j == NK - 3:
                    hi(142 + 2 * j)
                    hi(143 + 2 * j)
            for t in range(NT):
                act.wait_ge(fy_ready, t + 1)
                act.activation(sqf[:, t, :], yo[:, t, :], ACT.Square, accum_out=fsum[:, t:t + 1]).then_inc(fsum_ready, 1)
            act.wait_ge(ln_m, 2)
            act.activation(st1, st0, ACT.Sqrt).then_inc(ln_root, 1)

        @block.vector
        def _(dve):
            link = Chain(dve, dve_link)

            def lo(c, g=None):
                slot = c % RING
                dve.wait_ge(h_done, up(c + 1, g, RING))
                if g is not None or c >= RING:
                    dve.wait_ge(chunk_done, up(c - RING + 1, g, RING))
                dve.tensor_tensor(WL[:, slot, :], raw[:, slot, :], WH[:, slot, :].bitcast(F32),
                                  ALU.subtract).then_inc(l_done, 1)

            def ada_tile(n, g=None):
                dve.wait_ge(ada_in[n % 2], up((n // 2 + 1) * 16, g, 16))
                if g is not None or n >= 1:
                    dve.wait_ge(ada_used, up(n, g, 2))
                dve.tensor_tensor_reduce(ada[:, n % 2, :], ada[:, n % 2, :], cb[:, :], 1.0, 0.0,
                                         ALU.mult, ALU.add, st2).then_inc(ada_sum, 1)
                dve.wait_ge(ada_sum, up(n + 1, g, 2))
                dve.tensor_copy(column(modT, n, g, 2), st2).then_inc(ada_used, 1)

            def newton(y, m, t, last):
                link(dve.tensor_tensor(t, y, y, ALU.mult))
                link(dve.tensor_tensor(t, t, m, ALU.mult))
                link(dve.tensor_scalar(t, t, -0.5, 1.5, ALU.mult, ALU.add))
                dve.tensor_tensor(y, y, t, ALU.mult).then_inc(last, 1)

            def rms(k, width, eps):
                dve.wait_ge(psn_ready, k + 1)
                dve.tensor_scalar(nm[:, :], ps[:, 7, 0:T], 1.0 / width, eps, ALU.mult, ALU.add).then_inc(m_ready, 1)
                dve.wait_ge(root_ready, k + 1)
                link(dve.reciprocal(R[:, k % 2, :], nt[:, :]))
                newton(R[:, k % 2, :], nm[:, :], nt[:, :], r_ready)
                dve.wait_ge(r_ready, k + 1)

            def rms_tokens(k):
                dve.wait_ge(rt_ready, k + 1)
                dve.tensor_copy(rtok[:, 2 * k:2 * k + 2],
                                ps[:, 7, T:2 * T].rearrange("p (t c) -> p t c", c=P)[:, :, 0]).then_inc(rtok_ready, 1)

            dve.memset(ones[:, :], 1.0).then_inc(ones_ready, 1)
            dve.wait_ge(x_in, 32)
            for kc in range(KC):
                dve.tensor_scalar(xg0[:, kc, :], x[:, kc, :], vec[:, V_AG + kc:V_AG + kc + 1], None,
                                  ALU.mult).then_inc(xg_ready, 1)
            dve.wait_ge(sq_ready, 1)
            dve.tensor_reduce(tmp[5][:, :], sq0[:, :, :].rearrange("p k t -> p t k"), AX_X, ALU.add).then_inc(sum_ready, 1)
            for kc in range(KC):
                dve.wait_ge(xh_ready, kc + 1)
                dve.tensor_tensor(X1L[:, kc, :], xg0[:, kc, :], X1H[:, kc, :].bitcast(F32),
                                  ALU.subtract).then_inc(xl_ready, 1)
            for c in range(3):
                lo(c)
            rms(0, D, EPS_A)
            dve.wait_ge(cb_ready, 1)

            def v_step(q, g=None):
                lo(2 * q + 3, g)
                ada_tile(q, g)
                if g is None and q == 0:
                    rms_tokens(0)
                lo(2 * q + 4, g)
                for t in range(NT):
                    dve.wait_ge(v_out, up(2 * q + t + 1, g, 4))
                    dve.bn_stats(tiles(vst[:, t, :, :], q, g, 2),
                                 tiles(V[:, t, :].rearrange("p (q n) -> p q n", n=T), q, g, 2)).then_inc(st_done, 1)

            for q in range(2):
                v_step(q)
            with dve.Fori(1, 4) as g:
                for q in range(2):
                    v_step(q, g)
            dve.wait_ge(st_done, 16)
            for t in range(NT):
                link(dve.bn_aggr(mv[:, 2 * t:2 * t + 2], vst[:, t, :, :]))
            dve.tensor_scalar(st0, mv[:, 1:4:2], 1.0, EPS_A, ALU.mult, ALU.add).then_inc(ln_m, 1)
            dve.wait_ge(ln_root, 1)
            link(dve.reciprocal(rstd, st1))
            newton(rstd, st0, st1, ln_r)
            dve.wait_ge(ln_r, 1)
            for t in range(NT):
                dve.tensor_scalar(V[:, t, :], V[:, t, :], mv[:, 2 * t:2 * t + 1], rstd[:, t:t + 1],
                                  ALU.subtract, ALU.mult).then_inc(xhat_ready, 1)

            def y_low(n, count, src, g, per):
                dve.wait_ge(yh_ready, up(count + 1, g, per))
                dve.tensor_tensor(tiles(YL, n, g, per), src, tiles(YH, n, g, per).bitcast(F32),
                                  ALU.subtract).then_inc(yl_ready, 1)

            def ug_step(n, g):
                lo(19 + 2 * n, g)
                dve.wait_ge(chunk_done, up(18 + 2 * n, g, 4))
                dve.tensor_tensor(tmp[n % 2][:, :], ps[:, 2 + n % 2, 0:T], R[:, 0, :], ALU.mult).then_inc(gr_ready, 1)
                ada_tile(8 + n, g)
                lo(20 + 2 * n, g)
                dve.wait_ge(sv_mm, up(n + 1, g, 2))
                dve.tensor_tensor(tmp[2 + n % 2][:, :].rearrange("p (c t) -> p c t", c=NT),
                                  ps[:, 4 + n % 2, 0:T].rearrange("p (c t) -> p c t", c=NT),
                                  tiles(bsb, n, g, 2).broadcast_to([P, NT, P]), ALU.add).then_inc(svb_ready, 1)
                dve.wait_ge(m_gate, up(n + 1, g, 2))
                dve.tensor_tensor(tmp[4 + n % 2][:, :], ps[:, n % 2, 0:T], tmp[4 + n % 2][:, :],
                                  ALU.mult).then_inc(yf_ready, 1)
                y_low(n, n, tmp[4 + n % 2][:, :].unsqueeze(1), g, 2)

            with dve.Fori(0, AG // 2) as g:
                for n in range(2):
                    ug_step(n, g)

            def x_low(XL, XH, n, count, src, g, per, cper):
                dve.wait_ge(xh_ready, up(count + 1, g, cper))
                dve.tensor_tensor(tiles(XL, n, g, per), src, tiles(XH, n, g, per).bitcast(F32),
                                  ALU.subtract).then_inc(xl_ready, 1)

            def aout_step(n, g=None):
                lo(51 + 2 * n, g)
                lo(52 + 2 * n, g)
                dve.wait_ge(chunk_done, up(50 + 2 * n, g, 4))
                dve.tensor_tensor(tiles(x, n, g, 2), tiles(x, n, g, 2), ps[:, n % 2:n % 2 + 1, 0:T],
                                  ALU.add).then_inc(x_ready, 1)
                ada_tile(24 + n, g)
                dve.wait_ge(x_ready, up(n + 1, g, 2))
                for i, gain in enumerate((V_KG, V_BG)):
                    dve.tensor_scalar(tmp[2 * i + n % 2][:, :].unsqueeze(1), tiles(x, n, g, 2),
                                      column(vec[:, gain:gain + 8], n, g, 2), None, ALU.mult).then_inc(xg_ready, 1)
                for i, (XH, XL) in enumerate(((X1H, X1L), (X2H, X2L))):
                    x_low(XL, XH, n, KC + 2 * n + i, tmp[2 * i + n % 2][:, :].unsqueeze(1), g, 2, 4)

            for n in range(2):
                aout_step(n)
            with dve.Fori(1, 4) as g:
                for n in range(2):
                    aout_step(n, g)
            dve.wait_ge(ada_used, 32)
            link(dve.tensor_tensor(mod[:, 0:32], modT[:, 0:32], vec[:, V_ADAB:V_ADAB + 32], ALU.add))
            link(dve.tensor_scalar(s1, mod[:, 8:16], 1.0, None, ALU.add))
            link(dve.tensor_tensor(s1, s1, vec[:, V_N1:V_N1 + 8], ALU.mult))
            lo(67)
            rms(1, D, EPS_A)

            def rope_in(i, bank, bcol, g=None):
                dve.tensor_tensor(tmp[0][:, :], ps[:, bank, 0:T], R[:, 1, :], ALU.mult).then_inc(t_ready, 1)
                dve.wait_ge(t_ready, up(i + 1, g, 2))
                if g is not None or i >= 2:
                    dve.wait_ge(q_ready, up(i - 1, g, 2))
                dve.tensor_scalar(qb[:, i % 2, :], tmp[0][:, :], bcol, None, ALU.add).then_inc(qb_ready, 1)

            def rope_out(i, bank, g=None):
                dve.wait_ge(rope_mm, up(i + 1, g, 2))
                if g is not None or i >= 2:
                    dve.wait_ge(q_ready, up(i - 1, g, 2))
                dve.tensor_tensor(tmp[2 + i % 2][:, :], ps[:, bank, T:2 * T], sinT, ALU.mult).then_inc(rope_s, 1)

            dve.wait_ge(b_in, 48)
            dve.wait_ge(chunk_done, C_KV + 1)
            rope_in(0, 6, vec[:, V_BK:V_BK + 1])
            lo(68)
            rope_out(0, 6)
            rms_tokens(1)
            dve.wait_ge(rtok_ready, 2)
            dve.wait_ge(chunk_done, C_KV + 2)
            for t in range(NT):
                dve.scalar_tensor_tensor(out=vB[:, t, :], in0=ps[:, 5, t * P:(t + 1) * P],
                                         scalar=rtok[:, 2 + t:3 + t], in1=bvb[:, :],
                                         op0=ALU.mult, op1=ALU.add).then_inc(v_ready, 1)

            def soft_in(p, g, sinks):
                dve.wait_ge(s_mm, up(p + 1, g, 2))
                if g is not None or p >= 1:
                    dve.wait_ge(p_ready, up(4 * p, g, 8))
                if sinks:
                    if g is not None or p >= 1:
                        dve.wait_ge(es_ready, up(p, g, 2))
                    b = mask.unsqueeze(1).broadcast_to([P, 2, 2 * T])
                else:
                    dve.wait_ge(bias_in[p % 2], up(((p - 8) // 2 + 1) * 16, g, 16))
                    b = bias[:, p % 2, :].rearrange("p (h n) -> p h n", h=2)
                ins = dve.scalar_tensor_tensor(out=s[:, :, :].rearrange("p (h t) k -> p h (t k)", h=2),
                                               in0=ps[:, 4:6, :], scalar=HD ** -0.5, in1=b,
                                               op0=ALU.mult, op1=ALU.add)
                ins.then_inc(s_ready, 1)
                dve.wait_ge(s_ready, up(p + 1, g, 2))
                dve.tensor_reduce(mx, s[:, :, :], AX_X, ALU.max).then_inc(mx_ready, 1)
                dve.wait_ge(mx_ready, up(p + 1, g, 2))
                if sinks:
                    sink = tiles(sinkb, p, g, 2)
                    dve.tensor_tensor(mx.unsqueeze(1), mx.unsqueeze(1), sink, ALU.max).then_inc(mxs_ready, 1)
                    dve.wait_ge(mxs_ready, up(p + 1, g, 2))
                dve.tensor_scalar(negm, mx, -1.0, None, ALU.mult).then_inc(negm_ready, 1)
                dve.wait_ge(negm_ready, up(p + 1, g, 2))
                if sinks:
                    dve.tensor_tensor(dsk.unsqueeze(1), negm.unsqueeze(1), sink, ALU.add).then_inc(dsk_ready, 1)

            def soft_sum(p, g, sinks):
                par = p % 2
                dve.wait_ge(p_ready, up(4 * p + 4, g, 8))
                if sinks:
                    dve.wait_ge(es_ready, up(p + 1, g, 2))
                    dve.tensor_tensor(small_den[:, par, :], small_den[:, par, :], small_es[:, par, :],
                                      ALU.add).then_inc(den_ready, 1)
                    dve.wait_ge(den_ready, up(p + 1, g, 2))
                dve.reciprocal(small_rc[:, par, :], small_den[:, par, :]).then_inc(rc_ready, 1)

            def o_out(p, g):
                dve.wait_ge(o_mm, up(p + 1, g, 2))
                dve.wait_ge(rc_ready, up(p + 1, g, 2))
                if g is not None or p >= 1:
                    dve.wait_ge(ot_mm, up(p, g, 2))
                r = small_rc[:, p % 2, :].rearrange("p (h t) -> p t h", h=2).unsqueeze(3).broadcast_to([P, NT, 2, HD])
                dve.tensor_tensor(on[:, :, :].rearrange("p t (h d) -> p t h d", h=2),
                                  ps[:, 2 + (p + 1) % 2, T:2 * T].rearrange("p (t h d) -> p t h d", t=NT, h=2),
                                  r, ALU.mult).then_inc(on_ready, 1)

            def swa_step(m, g=None):
                if m < 8:
                    lo(69 + 2 * m, g)
                    dve.wait_ge(chunk_done, up(67 + 2 * m, g, 4))
                    rope_in(m + 1, m % 2, column(vec[:, V_BQ:V_BQ + 8], m, g, 2), g)
                if 1 <= m <= 8:
                    soft_in(m - 1, g, True)
                if m >= 2:
                    o_out(m - 2, g)
                if m < 8:
                    ada_tile(32 + m, g)
                    lo(70 + 2 * m, g)
                    dve.wait_ge(chunk_done, up(68 + 2 * m, g, 4))
                    if g is not None or m >= 2:
                        dve.wait_ge(gate_ready, up(m - 1, g, 2))
                    dve.tensor_tensor(gr2[:, m % 2, :], ps[:, 2 + m % 2, 0:T], R[:, 1, :], ALU.mult).then_inc(gr_ready, 1)
                    rope_out(m + 1, m % 2, g)
                if 1 <= m <= 8:
                    soft_sum(m - 1, g, True)
                if m >= 2:
                    dve.wait_ge(ot_mm, up(m - 1, g, 2))
                    dve.wait_ge(gate_ready, up(m - 1, g, 2))
                    y = tmp[4 + m % 2][:, :].unsqueeze(1)
                    dve.tensor_tensor(y, ps[:, 2 + (m + 1) % 2:3 + (m + 1) % 2, T:2 * T], tiles(sgate, m - 2, g, 2),
                                      ALU.mult).then_inc(yf_ready, 1)
                    y_low(m - 2, AG + m - 2, y, g, 2)

            def steps(eng, step):
                for m in range(4):
                    step(m)
                with eng.Fori(1, 3) as g:
                    step(2, g)
                    step(3, g)
                step(8)
                step(9)

            steps(dve, swa_step)

            def bout_step(n, g):
                lo(85 + n, g)
                dve.wait_ge(chunk_done, up(C_BOUT + n + 1, g, 4))
                dve.tensor_tensor(tiles(x, n, g, 4), tiles(x, n, g, 4), ps[:, n % 2:n % 2 + 1, 0:T],
                                  ALU.add).then_inc(x_ready, 1)

            with dve.Fori(0, 2) as g:
                for n in range(4):
                    bout_step(n, g)
            rms(2, D, EPS_A)
            with dve.Fori(0, 4) as g:
                for n in range(2):
                    dve.scalar_tensor_tensor(out=tiles(x, n, g, 2), in0=tiles(x, n, g, 2),
                                             scalar=column(vec[:, V_FG:V_FG + 8], n, g, 2), in1=R[:, 0:1, :],
                                             op0=ALU.mult, op1=ALU.mult).then_inc(x_ready, 1)
            rms(3, D, EPS_B)
            dve.wait_ge(x_ready, 24)

            def modulated(k, gains, shifts):
                with dve.Fori(0, 4) as g:
                    for j in range(2):
                        t = tmp[j][:, :].unsqueeze(1)
                        dve.wait_ge(xl_ready, up((3 + k) * KC + j - 1, g, 2))
                        dve.scalar_tensor_tensor(out=t, in0=tiles(x, j, g, 2), scalar=column(gains, j, g, 2),
                                                 in1=R[:, 1 - k:2 - k, :],
                                                 op0=ALU.mult, op1=ALU.mult).then_inc(mt_ready, 1)
                        dve.wait_ge(mt_ready, up(k * KC + j + 1, g, 2))
                        dve.tensor_scalar(t, t, column(shifts, j, g, 2), None, ALU.add).then_inc(xg_ready, 1)
                        x_low(X1L, X1H, j, (3 + k) * KC + j, t, g, 2, 2)

            modulated(0, s1, mod[:, 0:8])

            def v2_step(q, g):
                lo(C_V2 + 2 * q + 3, g)
                lo(C_V2 + 2 * q + 4, g)

            with dve.Fori(0, 2) as g:
                for q in range(2):
                    v2_step(q, g)

            def mix_step(m, g=None):
                if m < 8:
                    lo(C_QK + 2 * m + 3, g)
                if 1 <= m <= 8:
                    soft_in(8 + m - 1, g, False)
                if m >= 2:
                    o_out(8 + m - 2, g)
                if m < 8:
                    ada_tile(40 + m, g)
                    lo(C_QK + 2 * m + 4, g)
                    dve.wait_ge(chunk_done, up(C_QK + 2 * m + 2, g, 4))
                    if g is not None or m >= 2:
                        dve.wait_ge(s_mm, up(8 + m - 1, g, 2))
                    dve.tensor_copy(ks[:, m % 2, :], ps[:, 2 + m % 2, 0:T]).then_inc(k_ready, 1)
                if 1 <= m <= 8:
                    soft_sum(8 + m - 1, g, False)
                if m >= 2:
                    dve.wait_ge(ot_mm, up(8 + m - 1, g, 2))
                    dve.tensor_copy(tiles(oT, m - 2, g, 2),
                                    ps[:, 2 + (m + 1) % 2:3 + (m + 1) % 2, T:2 * T]).then_inc(ot_done, 1)

            steps(dve, mix_step)
            dve.wait_ge(ada_used, NMOD)
            link(dve.tensor_tensor(mod[:, 32:48], modT[:, 32:48], vec[:, V_ADAB + 32:V_ADAB + 48], ALU.add))
            link(dve.tensor_scalar(s2, mod[:, 32:40], 1.0, None, ALU.add))
            link(dve.tensor_tensor(s2, s2, vec[:, V_N2:V_N2 + 8], ALU.mult))
            dve.wait_ge(ot_done, NPAIR)
            for k in range(2):
                rms(4 + k, D // 2, EPS_B)
                with dve.Fori(0, 2) as g:
                    for j in range(2):
                        n = 4 * k + j
                        y = tmp[j][:, :].unsqueeze(1)
                        dve.wait_ge(yl_ready, up(AG + 8 + n - 1, g, 2))
                        dve.scalar_tensor_tensor(out=y, in0=tiles(oT, n, g, 2),
                                                 scalar=column(vec[:, V_OG:V_OG + 8], n, g, 2),
                                                 in1=R[:, k:k + 1, :],
                                                 op0=ALU.mult, op1=ALU.mult).then_inc(yf_ready, 1)
                        dve.wait_ge(yf_ready, up(AG + 8 + n + 1, g, 2))
                        y_low(n, AG + 8 + n, y, g, 2)

            def cout_step(n, g):
                lo(117 + n, g)
                dve.wait_ge(chunk_done, up(C_COUT + n + 1, g, 4))
                dve.scalar_tensor_tensor(out=tiles(x, n, g, 4), in0=ps[:, n % 2:n % 2 + 1, 0:T],
                                         scalar=column(mod[:, 16:24], n, g, 4), in1=tiles(x, n, g, 4),
                                         op0=ALU.mult, op1=ALU.add).then_inc(x_ready, 1)

            with dve.Fori(0, 2) as g:
                for n in range(4):
                    cout_step(n, g)
            rms(6, D, EPS_B)
            modulated(1, s2, mod[:, 24:32])
            dve.wait_ge(c_in, 32)
            dve.wait_ge(yl_ready, AG + 16)
            dve.tensor_tensor(diags[:, :, :], ident.unsqueeze(1).broadcast_to([P, KC, P]),
                              mod[:, 40:48].unsqueeze(2).broadcast_to([P, KC, P]), ALU.mult).then_inc(diag_ready, 1)

            for n in range(2 * PH):
                lo(125 + n)
                dve.wait_ge(sc_ready, n + 1)
                for t in range(NT):
                    row, b8 = sc[:, n % 2, t, :], v16[:, t, n, :]
                    link(dve.max(b8[:, 0:8], row))
                    link(dve.max_index(ix8[:, 0:8], b8[:, 0:8], row))
                    link(dve.match_replace(sc2[:, :], b8[:, 0:8], row, NEG))
                    link(dve.max(b8[:, 8:16], sc2[:, :]))
                    link(dve.max_index(ix8[:, 8:16], b8[:, 8:16], sc2[:, :]))
                    ins = dve.tensor_copy(i16[:, t, n, :], ix8[:, :])
                    if t == NT - 1:
                        ins.then_inc(sc_used, 1)
                        dve.wait_ge(sc_used, n + 1)
                    else:
                        link(ins)

            vr = v16[:, :, :, :].rearrange("p t (h q) k -> p (t h) q k", q=2)
            ir = i16[:, :, :, :].rearrange("p t (h q) k -> p (t h) q k", q=2)
            steps_ = [(a, a + 1, ROWS[a], STARTS[a]) for a in range(8)] + [(8, TOPK, 1, STARTS[8])]
            R16 = NT * PH
            for a, b, n, at0 in steps_:
                w = n * (b - a)
                va, ia = vr[:, :, 0, a:b], ir[:, :, 0, a:b]
                vb, ib = vr[:, :, 1, 0:n], ir[:, :, 1, 0:n]
                if n > 1:
                    va, ia = va.broadcast_to([P, R16, n]), ia.broadcast_to([P, R16, n])
                elif b - a > 1:
                    vb, ib = vb.broadcast_to([P, R16, b - a]), ib.broadcast_to([P, R16, b - a])
                link(dve.tensor_tensor(cand[:, :, at0:at0 + w], va, vb, ALU.add))
                link(dve.scalar_tensor_tensor(out=cid[:, :, at0:at0 + w], in0=ia, scalar=float(NK), in1=ib,
                                              op0=ALU.mult, op1=ALU.add))
            for r in range(R16):
                row, b8, c2 = cand[:, r, :], best[:, r, :], sc2[:, 0:NCAND]
                link(dve.max(b8[:, 0:8], row))
                link(dve.max_index(pos[:, r, 0:8], b8[:, 0:8], row))
                link(dve.match_replace(c2, b8[:, 0:8], row, NEG))
                link(dve.max(b8[:, 8:16], c2))
                link(dve.max_index(pos[:, r, 8:16], b8[:, 8:16], c2))
            link(dve.tensor_copy(zsum[:, :], best[:, :, 0]))
            dve.tensor_tensor(best[:, :, :], best[:, :, :], zsum[:, :].unsqueeze(2).broadcast_to([P, R16, TOPK]),
                              ALU.subtract).then_inc(exp_in, 1)
            link(dve.tensor_copy(posf[:, :, :], pos[:, :, :]))
            for t in range(NT):
                rs = slice(t * PH, (t + 1) * PH)
                link(dve.tensor_tensor(eq[:, :, :],
                                       posf[:, rs, :].rearrange("p h k -> p (h k)").unsqueeze(2)
                                       .broadcast_to([P, PH * TOPK, NCAND]),
                                       iota[:, 0:NCAND].unsqueeze(1).broadcast_to([P, PH * TOPK, NCAND]), ALU.is_equal))
                eq4 = eq[:, :, :].rearrange("p (h k) c -> p h k c", h=PH)
                link(dve.tensor_tensor(eq4, eq4, cid[:, rs, :].unsqueeze(2).broadcast_to([P, PH, TOPK, NCAND]), ALU.mult))
                link(dve.tensor_reduce(sid[:, rs, :].rearrange("p h k -> p (h k)"), eq[:, :, :], AX_X, ALU.add))
            link(dve.tensor_copy(pos[:, :, :], sid[:, :, :]))
            link(dve.tensor_scalar(posi[:, :, :], pos[:, :, :], 7, None, ALU.logical_shift_right))
            link(dve.tensor_scalar(pos[:, :, :], pos[:, :, :], NK - 1, None, ALU.bitwise_and))
            link(dve.tensor_copy(i1[:, :, :], posi[:, :, :]))
            link(dve.tensor_copy(i2[:, :, :], pos[:, :, :]))
            dve.wait_ge(exp_ready, 1)
            link(dve.tensor_reduce(zsum[:, :], best[:, :, :], AX_X, ALU.add))
            link(dve.reciprocal(zsum[:, :], zsum[:, :]))
            dve.tensor_tensor(best[:, :, :], best[:, :, :], zsum[:, :].unsqueeze(2).broadcast_to([P, R16, TOPK]),
                              ALU.mult).then_inc(lists_ready, 1)
            dve.wait_ge(lt_ready, 3)

            def hot_step(n, g=None):
                if g is not None or n >= 4:
                    dve.wait_ge(gate_mm, up(n - 3, g, 8))
                k = n % 4
                dve.tensor_scalar(O1[:, k, :], iota, column(tmp[1], n, g, 8), column(tmp[0], n, g, 8),
                                  ALU.is_equal, ALU.mult)
                dve.tensor_scalar(O2[:, k, :], iota, column(tmp[2], n, g, 8), None,
                                  ALU.is_equal).then_inc(hot_ready, 1)

            for n in range(8):
                hot_step(n)
            with dve.Fori(1, T // 8) as g:
                for n in range(8):
                    hot_step(n, g)

            def gated(j, g=None):
                dve.wait_ge(gelu_ready, up(j + 1, g, 2))
                if g is not None or j >= 2:
                    dve.wait_ge(wl_ready, up(j - 1, g, 2))
                gj = G[:, :, j:j + 1] if g is None else \
                    G[:, :, 1:NK - 1].rearrange("p t (g j) -> p j t g", j=2)[:, j - 1, :, bass.ds(g, 1)]
                dve.tensor_tensor(tmp[2 + j % 2][:, :].unsqueeze(2), tmp[j % 2][:, :].unsqueeze(2), gj,
                                  ALU.mult).then_inc(w_ready, 1)

            def w_low(j, g=None):
                dve.wait_ge(wh_ready, up(j + 1, g, 2))
                if g is not None or j >= 2:
                    dve.wait_ge(chunk_done, up(C_UV + 2 * j - 1, g, 4))
                dve.tensor_tensor(wvL[:, j % 2, :], tmp[2 + j % 2][:, :], wvH[:, j % 2, :].bitcast(F32),
                                  ALU.subtract).then_inc(wl_ready, 1)

            dve.wait_ge(gate_out, T // 4)
            lo(141)
            gated(0)
            w_low(0)
            lo(142)
            lo(143)
            def column_step(j, g=None):
                gated(j, g)
                w_low(j, g)
                lo(C_UV + 4 + 2 * j, g)
                lo(C_UV + 5 + 2 * j, g)

            column_step(1)
            column_step(2)
            with dve.Fori(1, (NK - 4) // 2) as g:
                column_step(1, g)
                column_step(2, g)
            for j in (NK - 3, NK - 2, NK - 1):
                gated(j)
                w_low(j)
                if j == NK - 3:
                    lo(142 + 2 * j)
                    lo(143 + 2 * j)

            dve.wait_ge(fin_in, 48)
            dve.wait_ge(chunk_done, NCHUNK)
            for t in range(NT):
                for h in range(2):
                    cols = slice(h * 512, h * 512 + 512)
                    link(dve.tensor_tensor(yo[:, t, cols], ps[:, 4 + 2 * t + h, :], g2r[:, cols], ALU.mult))
                dve.tensor_tensor(yo[:, t, :], yo[:, t, :], xt2[:, t, :], ALU.add).then_inc(fy_ready, 1)
            dve.wait_ge(fsum_ready, NT)
            dve.tensor_scalar(st0, fsum, 1.0 / D, EPS_B, ALU.mult, ALU.add).then_inc(ln_m, 1)
            dve.wait_ge(ln_root, 2)
            link(dve.reciprocal(rstd, st1))
            newton(rstd, st0, st1, ln_r)
            dve.wait_ge(ln_r, 2)
            for t in range(NT):
                dve.scalar_tensor_tensor(out=yo[:, t, :], in0=yo[:, t, :], scalar=rstd[:, t:t + 1],
                                         in1=fgr[:, :], op0=ALU.mult, op1=ALU.mult).then_inc(out_ready, 1)

        @block.gpsimd
        def _(pool):
            pool.wait_ge(a_in, 64)
            pool.affine_select(out=ws[:, :, :], in_=ws[:, :, :], compare_op=ALU.is_ge, fill=0.0, base=0,
                               pattern=[[0, AG], [1, P]], channel_multiplier=-1).then_inc(ws_ready, 1)
            pool.wait_ge(xhat_ready, 2)
            Vg = V[:, :, :].rearrange("p c (n d) -> p n c d", d=P)

            def v_affine(n, g=None):
                if g is not None or n >= 2:
                    pool.wait_ge(sv_mm, up(n - 1, g, 2))
                src = Vg[:, n] if g is None else \
                    Vg.rearrange("p (g j) c d -> p j g c d", j=2)[:, n % 2, bass.ds(g + n // 2, 1)].rearrange(
                        "p a c d -> p (a c) d")
                dst = vs[:, n % 2, :].rearrange("p (c d) -> p c d", c=NT)
                pool.tensor_tensor(dst, src, tiles(lng, n, g, 2).broadcast_to([P, NT, P]), ALU.mult)\
                    .then_inc(vg_ready, 1)
                pool.wait_ge(vg_ready, up(n + 1, g, 2))
                pool.tensor_tensor(dst, dst, tiles(lnb, n, g, 2).broadcast_to([P, NT, P]), ALU.add)\
                    .then_inc(vs_ready, 1)

            def gate_product(n, g=None):
                m = tmp[4 + n % 2][:, :]
                pool.wait_ge(sg_ready, up(n + 1, g, 2))
                pool.wait_ge(svb_ready, up(n + 1, g, 2))
                if g is not None or n >= 2:
                    pool.wait_ge(yl_ready, up(n - 1, g, 2))
                pool.tensor_tensor(m, tmp[n % 2][:, :], tmp[2 + n % 2][:, :], ALU.mult).then_inc(mg_ready, 1)
                pool.wait_ge(mg_ready, up(n + 1, g, 2))
                pool.tensor_tensor(m, m, R[:, 0, :], ALU.mult).then_inc(m_gate, 1)

            v_affine(0)
            v_affine(1)
            for n in range(2):
                gate_product(n)
                v_affine(n + 2)
            with pool.Fori(1, 7) as g:
                for n in range(2):
                    gate_product(n, g)
                    v_affine(n + 2, g)
            for n in range(14, 16):
                gate_product(n)

            pool.wait_ge(yl_ready, AG)
            pool.memset(tmp[5][:, :], 0.0).then_inc(acc_clear, 1)
            pool.wait_ge(acc_clear, 1)

            def add_square(k, acc, g=None):
                pool.wait_ge(sq_ready, up(k + 2, g, 1))
                if g is not None or k >= 1:
                    pool.wait_ge(sacc_done, up(k, g, 1))
                pool.tensor_tensor(acc, acc, tmp[4][:, :], ALU.add).then_inc(sacc_done, 1)

            add_square(0, tmp[5][:, :])
            with pool.Fori(0, KC - 1) as g:
                add_square(1, tmp[5][:, :], g)

            def rope(i, dst, waits, g=None):
                k = i % 2
                pool.wait_ge(qb_ready, up(i + 1, g, 2))
                pool.tensor_tensor(t3[:, k, :], qb[:, k, :], cosT, ALU.mult).then_inc(rope_c, 1)
                pool.wait_ge(rope_c, up(i + 1, g, 2))
                pool.wait_ge(rope_s, up(i + 1, g, 2))
                if waits is not None:
                    pool.wait_ge(s_mm, waits)
                pool.tensor_tensor(dst, t3[:, k, :], tmp[2 + k][:, :], ALU.add).then_inc(q_ready, 1)

            rope(0, ks[:, 0, :], None)
            for m in range(2):
                rope(m + 1, qs[:, m, :], None)
            with pool.Fori(0, 3) as g:
                for m in range(2, 4):
                    rope(m + 1, qs[:, m % 2, :], up(m - 1, g, 2), g)

            def clear(acc, n):
                pool.memset(acc, 0.0).then_inc(acc_clear, 1)
                pool.wait_ge(acc_clear, n)

            pool.wait_ge(yl_ready, AG + 8)
            clear(tmp[5][:, :], 2)
            with pool.Fori(0, KC) as g:
                add_square(8, tmp[5][:, :], g)
            pool.wait_ge(psn_ready, 3)
            clear(tmp[5][:, :], 3)
            with pool.Fori(0, KC) as g:
                add_square(16, tmp[5][:, :], g)
            pool.wait_ge(psn_ready, 4)
            clear(tmp[5][:, :], 4)
            with pool.Fori(0, 4) as g:
                add_square(24, tmp[5][:, :], g)
            clear(qb[:, 0, :], 5)
            with pool.Fori(0, 4) as g:
                add_square(28, qb[:, 0, :], g)
            pool.wait_ge(psn_ready, 6)
            clear(tmp[5][:, :], 6)
            with pool.Fori(0, KC) as g:
                add_square(32, tmp[5][:, :], g)

        @block.tensor
        def _(pe):
            pe.wait_ge(ones_ready, 1)
            pe.wait_ge(c_in, 32)

            def product(out_ap, stat, mov, k0=0, first=True, last=True):
                sH, sL, mH, mL = (*stat, *mov)
                for kc in range(KC):
                    for i, (a, b) in enumerate(((sH, mH), (sH, mL), (sL, mH))):
                        mm = pe.matmul(out_ap, a(kc), b(kc), start=(first and kc == 0 and i == 0),
                                       stop=(last and kc == KC - 1 and i == 2))
                return mm

            def weight(W, slot, n=1):
                if n == 1:
                    return lambda kc: W[:, slot, kc * P:(kc + 1) * P]
                return lambda kc: W[:, slot:slot + n, kc * P:(kc + 1) * P]

            def acts(X, k0=0):
                return lambda kc: X[:, k0 + kc, :]

            def feature_tile(c, g, bank, XH, XL, k0=0, first=True, last=True):
                pe.wait_ge(l_done, up(c + 1, g, RING))
                mm = product(ps[:, bank, 0:T], (weight(WH, c % RING), weight(WL, c % RING)),
                             (acts(XH, k0), acts(XL, k0)), first=first, last=last)
                mm.then_inc(chunk_done, 1)

            def token_tiles(c, g, bank, XH, XL, n):
                pe.wait_ge(l_done, up(c + n, g, RING))
                for t in range(NT):
                    def x_tile(X):
                        return lambda kc: X[:, kc, t * P:(t + 1) * P]
                    o = ps[:, bank + t, 0:n * P] if n > 1 else ps[:, bank, t * P:(t + 1) * P]
                    if n > 1:
                        o = o.rearrange("p (a n) -> p a n", a=n)
                    mm = product(o, (x_tile(XH), x_tile(XL)),
                                 (weight(WH, c % RING, n), weight(WL, c % RING, n)))
                mm.then_inc(chunk_done, n)

            def spread(k, ready, count, acc):
                pe.wait_ge(ready, count)
                pe.matmul(ps[:, 7, 0:T], ones[:, :], acc, start=True, stop=True).then_inc(psn_ready, 1)

            def turn_rms(k):
                pe.wait_ge(r_ready, k + 1)
                for t in range(NT):
                    mm = pe.transpose(ps[:, 7, T + t * P:T + (t + 1) * P], R[:, k % 2, t * P:(t + 1) * P], ident)
                mm.then_inc(rt_ready, 1)

            spread(0, sum_ready, 1, tmp[5][:, :])
            pe.wait_ge(xl_ready, KC)
            for q in range(2):
                token_tiles(2 * q, None, 2 * q, X1H, X1L, 2)
                if q == 0:
                    turn_rms(0)
            with pe.Fori(1, 4) as g:
                for q in range(2):
                    pe.wait_ge(v_out, up(2 * q - 2, g, 4))
                    token_tiles(2 * q, g, 2 * q, X1H, X1L, 2)
            pe.wait_ge(v_out, 16)

            def ug_step(n, g=None):
                if g is not None or n >= 2:
                    pe.wait_ge(yf_ready, up(n - 1, g, 2))
                feature_tile(16 + 2 * n, g, n % 2, X1H, X1L)
                feature_tile(17 + 2 * n, g, 2 + n % 2, X1H, X1L)
                pe.wait_ge(vs_ready, up(n + 1, g, 2))
                pe.wait_ge(ws_ready, 1)
                w = tiles(ws, n, g, 2)
                for c in range(NT):
                    mm = pe.matmul(ps[:, 4 + n % 2, c * P:(c + 1) * P], vs[:, n % 2, c * P:(c + 1) * P],
                                   w.rearrange("p a t -> p (a t)"), start=True, stop=True)
                mm.then_inc(sv_mm, 1)

            ug_step(0)
            ug_step(1)
            with pe.Fori(1, AG // 2) as g:
                for n in range(2):
                    ug_step(n, g)
            pe.wait_ge(yl_ready, AG)

            def aout_step(n, g=None):
                if g is not None or n >= 2:
                    pe.wait_ge(x_ready, up(n - 1, g, 2))
                feature_tile(C_AOUT + 2 * n, g, n % 2, YH, YL, 0, True, False)
                feature_tile(C_AOUT + 2 * n + 1, g, n % 2, YH, YL, KC, False, True)

            aout_step(0)
            aout_step(1)
            with pe.Fori(1, 4) as g:
                for n in range(2):
                    aout_step(n, g)
            pe.wait_ge(xl_ready, 3 * KC)
            feature_tile(C_KV, None, 6, X1H, X1L)
            spread(1, sacc_done, KC, tmp[5][:, :])
            token_tiles(C_KV + 1, None, 5, X1H, X1L, 1)
            pe.wait_ge(b_in, 48)

            def rope_turn(i, bank, g=None):
                pe.wait_ge(qb_ready, up(i + 1, g, 2))
                pe.matmul(ps[:, bank, T:2 * T], perm, qb[:, i % 2, :], start=True, stop=True).then_inc(rope_mm, 1)

            def scores(p, g, kslot):
                for h in range(2):
                    hs = slice(h * HD, (h + 1) * HD)
                    for t in range(NT):
                        mm = pe.matmul(ps[:, 4 + h, t * T:(t + 1) * T], qs[hs, p % 2, t * P:(t + 1) * P],
                                       ks[hs, kslot, :], start=True, stop=True)
                mm.then_inc(s_mm, 1)

            def turn_probs(p, g):
                pe.wait_ge(p_ready, up(4 * p + 4, g, 8))
                if g is not None or p >= 1:
                    pe.wait_ge(pt_ready, up(2 * p, g, 4))
                for h in range(2):
                    for kt in range(NT):
                        for t in range(NT):
                            k = kt * NT + t
                            mm = pe.transpose(ps[:, 6 + h, k * P:(k + 1) * P],
                                              pr[:, 2 * h + t, kt * P:(kt + 1) * P], ident)
                mm.then_inc(pt_mm, 1)

            def values(p, g, v_of):
                pe.wait_ge(pt_ready, up(2 * p + 2, g, 4))
                for t in range(NT):
                    for h in range(2):
                        for kt in range(NT):
                            mm = pe.matmul(ps[:, 2 + (p + 1) % 2, T + t * P + h * HD:T + t * P + (h + 1) * HD],
                                           pT[:, h, kt * NT + t, :], v_of(kt, h),
                                           start=(kt == 0), stop=(kt == NT - 1))
                mm.then_inc(o_mm, 1)

            def turn_out(p, g):
                pe.wait_ge(on_ready, up(p + 1, g, 2))
                for t in range(NT):
                    mm = pe.transpose(ps[:, 2 + (p + 1) % 2, T + t * P:T + (t + 1) * P], on[:, t, :], ident)
                mm.then_inc(ot_mm, 1)

            rope_turn(0, 6)
            turn_rms(1)
            pe.wait_ge(v_ready, 2)

            def swa_step(m, g=None):
                if m < 8:
                    if g is not None or m >= 2:
                        pe.wait_ge(rope_s, up(m, g, 2))
                    feature_tile(C_QG + 2 * m, g, m % 2, X2H, X2L)
                if 1 <= m <= 8:
                    pe.wait_ge(q_ready, up(m + 1, g, 2))
                    if g is not None or m >= 2:
                        pe.wait_ge(s_ready, up(m - 1, g, 2))
                    scores(m - 1, g, 0)
                if m >= 2:
                    pe.wait_ge(gr_ready, up(AG + min(m, 8), g, 2))
                    if m == 9:
                        pe.wait_ge(yf_ready, AG + 6)
                    values(m - 2, g, lambda kt, h: vB[:, kt, h * HD:(h + 1) * HD])
                if m < 8:
                    if g is not None or m >= 3:
                        pe.wait_ge(yf_ready, up(AG + m - 2, g, 2))
                    feature_tile(C_QG + 2 * m + 1, g, 2 + m % 2, X2H, X2L)
                    rope_turn(m + 1, m % 2, g)
                if 1 <= m <= 8:
                    turn_probs(m - 1, g)
                if m >= 2:
                    turn_out(m - 2, g)

            def steps(eng, step):
                for m in range(4):
                    step(m)
                with eng.Fori(1, 3) as g:
                    step(2, g)
                    step(3, g)
                step(8)
                step(9)

            steps(pe, swa_step)

            def out_steps(c, count, x0):
                pe.wait_ge(yl_ready, count)
                with pe.Fori(0, 2) as g:
                    for n in range(4):
                        pe.wait_ge(x_ready, up(x0 + n - 1, g, 4))
                        feature_tile(c + n, g, n % 2, YH, YL)

            out_steps(C_BOUT, AG + 8, 8)
            spread(2, sacc_done, 16, tmp[5][:, :])
            spread(3, sacc_done, 24, tmp[5][:, :])
            pe.wait_ge(xl_ready, 4 * KC)
            with pe.Fori(0, 2) as g:
                for q in range(2):
                    pe.wait_ge(v_out, up(16 + 2 * q - 2, g, 4))
                    token_tiles(C_V2 + 2 * q, g, 2 * q, X1H, X1L, 2)
            vCv = vC[:, :, :].rearrange("p t (m n) -> p t m n", n=P)

            def mix_step(m, g=None):
                if m < 8:
                    pe.wait_ge(v_out, 24) if g is None and m < 2 else pe.wait_ge(qt_ready, up(m - 1, g, 2))
                    feature_tile(C_QK + 2 * m, g, m % 2, X1H, X1L)
                if 1 <= m <= 8:
                    p = m - 1
                    pe.wait_ge(qt_ready, up(p + 1, g, 2))
                    pe.wait_ge(k_ready, up(p + 1, g, 2))
                    pe.wait_ge(s_ready, up(8 + p, g, 2))
                    scores(8 + p, g, p % 2)
                if m >= 2:
                    p = m - 2
                    pe.wait_ge(k_ready, up(min(m, 8), g, 2))
                    if m == 9:
                        pe.wait_ge(ot_done, 6)

                    def v_of(kt, h):
                        v = tiles(vCv[:, kt], p, g, 2)[:, :, h * HD:(h + 1) * HD]
                        return v.rearrange("p a n -> p (a n)")
                    values(8 + p, g, v_of)
                if m < 8:
                    if g is not None or m >= 3:
                        pe.wait_ge(ot_done, up(m - 2, g, 2))
                    feature_tile(C_QK + 2 * m + 1, g, 2 + m % 2, X1H, X1L)
                if 1 <= m <= 8:
                    turn_probs(8 + m - 1, g)
                if m >= 2:
                    turn_out(8 + m - 2, g)

            steps(pe, mix_step)
            spread(4, sacc_done, 28, tmp[5][:, :])
            pe.wait_ge(m_ready, 5)
            spread(5, sacc_done, 32, qb[:, 0, :])
            out_steps(C_COUT, AG + 16, 24)
            spread(6, sacc_done, 40, tmp[5][:, :])
            pe.wait_ge(m_ready, 7)
            for t in range(NT):
                for kc in range(KC):
                    mm = pe.transpose(ps[:, 4 + 2 * t + kc // 4, kc % 4 * P:(kc % 4 + 1) * P],
                                      x[:, kc, t * P:(t + 1) * P], ident)
            mm.then_inc(tr_mm, 1)
            pe.wait_ge(diag_ready, 1)
            pe.wait_ge(act_link, 4)
            for i in range(2):
                mm = pe.matmul(ps[:, 6 + i, :], ones[:, :],
                               diags[:, 4 * i:4 * i + 4, :].rearrange("p k n -> p (k n)"), start=True, stop=True)
            mm.then_inc(tr_mm, 1)
            pe.wait_ge(xl_ready, 5 * KC)
            pe.wait_ge(sk_in, 16)

            def wq_step(n, g=None):
                pe.wait_ge(qt_ready, up(8 + n - 1, g, 4))
                feature_tile(C_WQ + n, g, n % 2, X1H, X1L)
                pe.wait_ge(qt_ready, up(8 + n + 1, g, 4))
                if g is not None or n >= 2:
                    pe.wait_ge(sc_ready, up(n - 1, g, 4))
                for t in range(NT):
                    mm = pe.matmul(ps[:, 2 + n % 2, t * P:(t + 1) * P], qt[:, n % 2, t * P:(t + 1) * P],
                                   sk[:, n % 2, :], start=True, stop=True)
                mm.then_inc(sc_mm, 1)

            for n in range(4):
                wq_step(n)
            with pe.Fori(1, 4) as g:
                for n in range(4):
                    wq_step(n, g)
            pe.wait_ge(lists_ready, 1)
            pe.wait_ge(act_link, 6)
            for i, src in enumerate((best, i1, i2)):
                for t in range(NT):
                    mm = pe.transpose(ps[:, 4 + i, t * P:(t + 1) * P],
                                      src[:, t * PH:(t + 1) * PH, :].rearrange("p h k -> p (h k)"), ident)
            mm.then_inc(lt_mm, 1)

            def gate_step(n, g=None):
                if n % 4 == 0 and (g is not None or n >= 8):
                    pe.wait_ge(gate_out, up(n // 4 - 1, g, 2))
                pe.wait_ge(hot_ready, up(n + 1, g, 8))
                k = n % 4
                pe.matmul(ps[:, n // 4, k * P:(k + 1) * P], O1[:, k, :], O2[:, k, :],
                          start=True, stop=True).then_inc(gate_mm, 1)

            for n in range(8):
                gate_step(n)
            with pe.Fori(1, T // 8) as g:
                for n in range(8):
                    gate_step(n, g)

            def down(j, c, g=None, first=False, last=False):
                pe.wait_ge(l_done, up(c + 1, g, RING))
                pe.wait_ge(wl_ready, up(j + 1, g, 2))
                slot = c % RING
                for t in range(NT):
                    ts_ = slice(t * P, (t + 1) * P)
                    for h in range(2):
                        hs = slice(h * 512, (h + 1) * 512)
                        for i, (a, b) in enumerate(((wvH, WH), (wvH, WL), (wvL, WH))):
                            mm = pe.matmul(ps[:, 4 + 2 * t + h, :], a[:, j % 2, ts_], b[:, slot, hs],
                                           start=(first and i == 0), stop=(last and i == 2),
                                           skip_group_check=True)
                mm.then_inc(chunk_done, 1)

            def up_tile(j, c, g=None):
                if g is not None or j >= 2:
                    pe.wait_ge(gelu_ready, up(j - 1, g, 2))
                feature_tile(c, g, j % 2, X1H, X1L)

            pe.wait_ge(gate_out, T // 4)
            pe.wait_ge(lt_ready, 3)
            up_tile(0, C_UV)
            up_tile(1, C_UV + 1)
            down(0, C_UV + 2, first=True)
            with pe.Fori(0, (NK - 2) // 2) as g:
                for j in (1, 2):
                    up_tile(j + 1, C_UV + 1 + 2 * j, g)
                    down(j, C_UV + 2 + 2 * j, g)
            down(NK - 1, NCHUNK - 1, last=True)


def _constants():
    ident = np.eye(P, dtype=np.float32)
    iota = np.tile(np.arange(P, dtype=np.float32), (P, 1))
    half = HD // 2
    perm = np.zeros((P, P), np.float32)
    for f in range(P):
        if f % HD < half:
            perm[f + half, f] = -1.0
        else:
            perm[f - half, f] = 1.0
    inv = np.float32(10000.0) ** (-np.arange(0, HD, 2, dtype=np.float32) / np.float32(HD))
    ang = np.arange(T, dtype=np.float32)[:, None] * inv[None, :]
    f = np.arange(P) % half
    cosT, sinT = np.cos(ang).astype(np.float32).T[f], np.sin(ang).astype(np.float32).T[f]
    q, k = np.arange(T)[:, None], np.arange(T)[None, :]
    window = np.where((k <= q) & (k > q - 128), 0.0, NEG).astype(np.float32)
    mask = window.reshape(NT, P, T).transpose(1, 0, 2).reshape(P, NT * T)
    d = np.abs(q - k)
    count = np.zeros((T, T))
    for span, step in ((128, 1), (512, 4), (2048, 16)):
        count += (d % step == 0) & (d <= span // 2)
    slopes = 2.0 ** (-8.0 * (np.arange(8) + 1) / 8)
    logc = np.where(count > 0, np.log(np.maximum(count, 1)), NEG)
    dil = (-slopes[:, None, None] * d[None] + logc[None]).astype(np.float32)
    return np.concatenate([ident, iota], 1), np.concatenate([perm, cosT, sinT, mask], 1), dil


def _window_index():
    grid, wr, wc = 64, 4, 16
    t = np.arange(T)
    r, c = t // grid, t % grid
    c0 = np.clip(c - wc // 2, 0, grid - wc)
    dr = r[None, :] - r[:, None] + 7
    dc = c[None, :] - c[:, None] + 15
    near = (c[None, :] >= c0[:, None]) & (c[None, :] < c0[:, None] + wc)
    assert T // grid == wr
    return dr, np.clip(dc, 0, 30), near


def kernel(**inputs):
    import concourse.bacc as _bacc
    from concourse.bass_utils import run_bass_kernel_spmd as _run

    a = {k: np.asarray(v) for k, v in inputs.items()}
    cI, cB, dil = _constants()

    def tiles_of(w):
        k, n = w.shape
        return w.reshape(k // D, KC, P, n // P, P).transpose(3, 0, 2, 1, 4).reshape(-1, P, CW)

    def weave(x, y):
        return np.stack([x, y], 1).reshape(-1, P, CW)

    pair = np.arange(D).reshape(2, 8, HD).transpose(1, 0, 2).reshape(-1)
    w = a["a_w_in"][0]
    parts = [tiles_of(w[:, AW:2 * AW]), weave(tiles_of(w[:, 0:AW]), tiles_of(w[:, 2 * AW:])),
             tiles_of(a["a_w_out"][0]), tiles_of(a["w_kv"])]
    w = a["b_w_in"][0]
    parts += [weave(tiles_of(w[:, 0:D][:, pair]), tiles_of(w[:, D:][:, pair])), tiles_of(a["b_w_out"][0][pair])]
    w = tiles_of(a["w_in_2"][0])
    parts += [w[8:12], w[20:24], weave(w[0:4], w[4:8]), weave(w[12:16], w[16:20]),
              tiles_of(a["w_out_2"][0]), tiles_of(a["peer_wq_2"][0])]
    u = a["peer_u_2"][0].reshape(NK, NK, KC, P).transpose(1, 3, 2, 0).reshape(NK, P, CW)
    v = a["peer_v_2"][0].reshape(NK, NK, D).transpose(1, 0, 2)
    parts += [u[0:1], weave(u[1:], v[:-1]), v[-1:]]
    stream = np.concatenate(parts)
    assert stream.shape == (NCHUNK, P, CW)

    def cols(x):
        return x.reshape(-1, P).T

    vecs = np.concatenate([cols(x) for x in (
        a["a_norm_g"][0], a["kv_norm_g"], a["b_norm_g"][0], a["b_bq"][0][pair], a["b_kv"][0:P],
        a["norm1_g_2"][0], a["norm2_g_2"][0], a["ada_b_2"][0], a["out_norm_na_g_2"][0], a["out_norm_dil_g_2"][0],
        a["final_norm_g"])], 1)
    sinks = np.repeat(a["b_sinks"][0].reshape(2, 8).T.reshape(-1), NT)
    rows = np.concatenate([a["c_2"][0], a["a_ln_g"][0], a["a_ln_b"][0], a["a_bs"][0].reshape(-1), a["b_kv"][P:],
                           sinks, a["final_g_2"]])
    dr, dc, near = _window_index()
    na = np.where(near[None], a["na_rpb_2"][0][:, dr, dc], np.float32(NEG))
    bias = np.concatenate([na, dil]).reshape(NPAIR, 2, NT, P, T).transpose(0, 3, 1, 2, 4).reshape(NPAIR, P, 4 * T)
    arrays = {
        "stream": stream,
        "xT": a["x"][0].T.reshape(KC, P, T).transpose(1, 0, 2),
        "vecs": vecs, "cI": cI, "cB": cB, "rows": rows,
        "wsT": a["a_ws"][0].transpose(2, 0, 1),
        "adaT": a["ada_w_2"][0].T.reshape(NMOD, P, D),
        "att_bias": bias,
        "skT": a["peer_subkeys_2"][0].transpose(2, 0, 1),
    }
    arrays = {k: np.ascontiguousarray(x) for k, x in arrays.items()}
    nc = _bacc.Bacc("TRN2", target_bir_lowering=False, num_devices=1)
    aps = [nc.dram_tensor(k, x.shape, F32, kind="ExternalInput").ap() for k, x in arrays.items()]
    spill = nc.dram_tensor("spill", [P, 3 * D], F32, kind="Internal").ap()
    out = nc.dram_tensor("out", [T, D], F32, kind="ExternalOutput").ap()
    two_block_kernel(nc, *aps, spill, out)
    got = _run(nc, [arrays], core_ids=[0]).results[0]["out"]
    return got.reshape(1, T, D)
```

```python
from contextlib import ExitStack

import numpy as np

import concourse.bass as bass
from concourse import mybir

F32 = mybir.dt.float32
F32R = mybir.dt.float32r
U32 = mybir.dt.uint32
ALU = mybir.AluOpType
ACT = mybir.ActivationFunctionType
AX_X = mybir.AxisListType.X

P = 128
T = 256
NT = T // P
D = 1024
KC = D // P
CW = KC * P
AW = 2048
AG = AW // P
HD = 64
NPAIR = 8
NMOD = 6 * D // P
NK = 128
PH = 8
TOPK = 16
NEG = -1e30
EPS_A = 1e-5
EPS_B = 1e-6

RING = 4
C_V, C_UG = 0, AG
C_AOUT = C_UG + 2 * AG
C_KV = C_AOUT + 2 * KC
C_QG = C_KV + 2
C_BOUT = C_QG + 2 * NPAIR
C_V2 = C_BOUT + KC
C_QK = C_V2 + KC
C_COUT = C_QK + 2 * NPAIR
C_WQ = C_COUT + KC
C_UV = C_WQ + 2 * PH
NCHUNK = C_UV + 2 * NK

V_AG, V_KG, V_BG, V_BQ, V_BK, V_N1, V_N2 = 0, 8, 16, 24, 32, 33, 41
V_ADAB, V_OG = 49, 49 + NMOD
V_FG = V_OG + 8
NVEC = V_FG + 8

ROWS = [TOPK // (a + 1) for a in range(TOPK)]
STARTS = [sum(ROWS[:a]) for a in range(TOPK)]
NCAND = sum(ROWS)
POOL_ROWS = 10


class Chain:

    def __init__(self, eng, sem):
        self.eng, self.sem, self.n = eng, sem, 0

    def __call__(self, ins):
        self.n += 1
        ins.then_inc(self.sem, 1)
        self.eng.wait_ge(self.sem, self.n)


def up(c, g=None, per=1):
    return c if g is None else g * per + c


def tiles(view, c, g=None, per=1, width=1):
    if g is None:
        return view[:, c:c + width]
    n = view.shape[1] // per * per
    grouped = view[:, 0:n].rearrange("p (g j) n -> p g j n", j=per)
    return grouped[:, bass.ds(g + c // per, 1), c % per:c % per + width].rearrange("p a j n -> p (a j) n")


def column(view, c, g=None, per=1):
    if g is None:
        return view[:, c:c + 1]
    n = view.shape[1] // per * per
    return view[:, 0:n].rearrange("p (g j) -> p g j", j=per)[:, bass.ds(g + c // per, 1), c % per]


def two_block_kernel(nc, stream, xT, vecs, cI, cB, rows, wsT, adaT, att_bias, skT, spill, out):
    with ExitStack() as ctx:
        def sb(name, shape, dt=F32):
            return ctx.enter_context(nc.sbuf_tensor(name, shape, dt))

        def sem(name):
            return ctx.enter_context(nc.semaphore(name))

        raw = sb("raw", [P, RING, CW])
        WH = sb("WH", [P, RING, CW], F32R)
        WL = sb("WL", [P, RING, CW], F32R)
        X1H = sb("X1H", [P, KC, T], F32R)
        X1L = sb("X1L", [P, KC, T], F32R)
        idio = sb("idio", [P, 2 * P])
        ident, iota = idio[:, 0:P], idio[:, P:2 * P]
        ones = sb("ones", [P, P])
        vec = sb("vec", [P, NVEC])
        small = sb("small", [P, 168])
        tmp = [sb(f"tmp{i}", [P, T]) for i in range(6)]
        base_wv = nc.sbuf_base
        wvH = sb("wvH", [P, 2, T], F32R)
        wvL = sb("wvL", [P, 2, T], F32R)
        base = nc.sbuf_base
        G = sb("G", [P, T, NK])
        assert nc.lookup_mloc(G).addr == base and nc.lookup_mloc(wvH).addr == base_wv
        base_hot = nc.lookup_mloc(tmp[3]).addr
        free_slot = (C_UV + 3) % RING * CW * 4
        O1 = nc.alloc_sbuf_tensor_at("O1", [P, 8, NK], F32, offset=nc.lookup_mloc(WH).addr + free_slot)
        O2 = [nc.alloc_sbuf_tensor_at("O2a", [P, 2, 4, NK], F32, offset=base_hot),
              nc.alloc_sbuf_tensor_at("O2b", [P, 2, 4, NK], F32, offset=nc.lookup_mloc(WL).addr + free_slot)]
        assert base_hot + 8 * NK * 4 <= base

        def at(name, kib, shape, dt=F32):
            off = int(kib * 1024)
            assert off + int(np.prod(shape[1:])) * 4 <= T * NK * 4, name
            return nc.alloc_sbuf_tensor_at(name, shape, dt, offset=base + off)

        x = at("x", 0, [P, KC, T])
        uR = at("uR", 8, [P, 2, T])
        X2H = at("X2H", 8, [P, KC, T], F32R)
        X2L = at("X2L", 16, [P, KC, T], F32R)
        YH = at("YH", 24, [P, AG, T], F32R)
        YL = at("YL", 40, [P, AG, T], F32R)
        ada = at("ada", 56, [P, 2, D])
        cb = at("cb", 64, [P, D])
        V = at("V", 68, [P, NT, AW])
        sq0 = at("sq0", 68, [P, KC, T])
        xg0 = at("xg0", 76, [P, KC, T])
        lng = at("lng", 84, [P, AG, P])
        lnb = at("lnb", 92, [P, AG, P])
        ws = at("ws", 100, [P, AG, P])
        bsb = at("bsb", 108, [P, AG, P])
        cBt = at("cBt", 116, [P, 9 * P])
        perm, cosT, sinT = cBt[:, 0:P], cBt[:, P:3 * P], cBt[:, 3 * P:5 * P]
        mask = cBt[:, 5 * P:9 * P]
        R = at("R", 120.5, [P, 2, T])
        nm = at("nm", 122.5, [P, T])
        nt = at("nt", 123.5, [P, T])
        vst = at("vst", 124.5, [P, NT, 8, 6])
        sinkb = at("sinkb", 125, [P, NPAIR, 4])
        bvb = at("bvb", 125.25, [P, P])
        vs = at("vs", 125.75, [P, 2, T])
        sgate = at("sgate", 68, [P, NPAIR, T])
        oT = at("oT", 68, [P, NPAIR, T])
        s = at("s", 76, [P, 4, T])
        pr = at("pr", 80, [P, 4, T])
        pT = at("pT", 84, [P, 2, 4, P])
        qs = at("qs", 88, [P, 2, T])
        qb = at("qb", 90, [P, 2, T])
        ks = at("ks", 92, [P, 2, T])
        vB = at("vB", 94, [P, NT, P])
        on = at("on", 95, [P, NT, P])
        t3 = at("t3", 96, [P, 2, T])
        gr2 = at("gr2", 98, [P, 2, T])
        th = at("th", 100, [P, 2, T])
        F = at("F", 68, [P, KC, T])
        FY = at("FY", 76, [P, KC, T])
        bias = at("bias", 100, [P, 2, 4 * T])
        vC = at("vC", 108, [P, NT, D])
        eq = at("eq", 8, [P, NT * PH, TOPK, NCAND])
        qt = at("qt", 68, [P, 2, T])
        sc = at("sc", 70, [P, 2, NT, NK])
        v16 = at("v16", 72, [P, NT, 2 * PH, TOPK])
        i16 = at("i16", 74, [P, NT, 2 * PH, TOPK])
        cand = at("cand", 76, [P, NT * PH, NCAND])
        cid = at("cid", 79.5, [P, NT * PH, NCAND])
        best = at("best", 83, [P, NT * PH, TOPK])
        pos = at("pos", 84, [P, NT * PH, TOPK], U32)
        posf = at("posf", 85, [P, NT * PH, TOPK])
        sid = at("sid", 86, [P, NT * PH, TOPK])
        i1 = at("i1", 87, [P, NT * PH, TOPK])
        i2 = at("i2", 88, [P, NT * PH, TOPK])
        sk = at("sk", 99, [P, 2, NK])
        sc2 = at("sc2", 90, [P, NK])
        ix8 = at("ix8", 90.5, [P, TOPK], U32)
        g2b = at("g2b", 92, [P, D])
        diags = at("diags", 100, [P, KC, P])
        zsum = at("zsum", 91.5, [P, NT * PH])
        posi = at("posi", 104, [P, NT * PH, TOPK], U32)
        xtok = at("xtok", 108, [P, NT, D])
        xt2 = at("xt2", 0, [P, NT, D])
        g2r = at("g2r", 8, [P, D])
        fgr = at("fgr", 12, [P, D])
        yo = at("yo", 16, [P, NT, D])
        sqf = at("sqf", 24, [P, NT, D])

        modT, mod = small[:, 0:NMOD], small[:, NMOD:2 * NMOD]
        s1, s2 = small[:, 96:104], small[:, 104:112]
        rtok = small[:, 112:116]
        mx, negm, dsk = small[:, 116:120], small[:, 120:124], small[:, 124:128]
        small_es = small[:, 128:136].rearrange("p (a k) -> p a k", a=2)
        small_den = small[:, 136:144].rearrange("p (a k) -> p a k", a=2)
        small_rc = small[:, 144:152].rearrange("p (a k) -> p a k", a=2)
        mv = small[:, 152:156]
        rstd, st0, st1 = small[:, 156:158], small[:, 158:160], small[:, 160:162]
        st2, fsum = small[:, 162:163], small[:, 164:166]

        ps = ctx.enter_context(nc.psum_tensor("ps", [P, 8, 512], F32))

        raw_in = [sem(f"raw_in{i}") for i in range(RING)]
        h_done, l_done, chunk_done = sem("h_done"), sem("l_done"), sem("chunk_done")
        x_in, c_in, a_in, b_in, sk_in = sem("x_in"), sem("c_in"), sem("a_in"), sem("b_in"), sem("sk_in")
        ada_in = [sem(f"ada_in{i}") for i in range(2)]
        bias_in = [sem(f"bias_in{i}") for i in range(2)]
        ada_used = sem("ada_used")
        dve_link, act_link = sem("dve_link"), sem("act_link")
        sum_ready, psn_ready, m_ready, root_ready, r_ready = (
            sem("sum_ready"), sem("psn_ready"), sem("m_ready"), sem("root_ready"), sem("r_ready"))
        rt_ready, rtok_ready = sem("rt_ready"), sem("rtok_ready")
        ones_ready, cb_ready = sem("ones_ready"), sem("cb_ready")
        sq_ready, sacc_done, x_ready = sem("sq_ready"), sem("sacc_done"), sem("x_ready")
        xg_ready, xh_ready, xl_ready = sem("xg_ready"), sem("xh_ready"), sem("xl_ready")
        yf_ready, yh_ready, yl_ready = sem("yf_ready"), sem("yh_ready"), sem("yl_ready")
        v_mm, v_out, st_done = sem("v_mm"), sem("v_out"), sem("st_done")
        ln_m, ln_root, xhat_ready = sem("ln_m"), sem("ln_root"), sem("xhat_ready")
        ws_ready, vs_ready, sv_mm = sem("ws_ready"), sem("vs_ready"), sem("sv_mm")
        ur_ready, th_ready = sem("ur_ready"), sem("th_ready")
        gr_ready, sg_ready, svb_ready = sem("gr_ready"), sem("sg_ready"), sem("svb_ready")
        pool_link = sem("pool_link")
        kv_mm, k_ready, v_ready = sem("kv_mm"), sem("k_ready"), sem("v_ready")
        qb_ready, rope_mm, rope_s, rope_c, q_ready, q_add = (
            sem("qb_ready"), sem("rope_mm"), sem("rope_s"), sem("rope_c"), sem("q_ready"), sem("q_add"))
        s_mm, s_ready, mx_ready, negm_ready, dsk_ready = (
            sem("s_mm"), sem("s_ready"), sem("mx_ready"), sem("negm_ready"), sem("dsk_ready"))
        p_ready, es_ready, den_ready, rc_ready = sem("p_ready"), sem("es_ready"), sem("den_ready"), sem("rc_ready")
        pt_mm, pt_ready, o_mm, on_ready, ot_mm, ot_done = (
            sem("pt_mm"), sem("pt_ready"), sem("o_mm"), sem("on_ready"), sem("ot_mm"), sem("ot_done"))
        g_ready, gate_ready = sem("g_ready"), sem("gate_ready")
        qt_ready, sc_mm, sc_ready, sc_used = sem("qt_ready"), sem("sc_mm"), sem("sc_ready"), sem("sc_used")
        tr_mm, tr_ready, spill_done = sem("tr_mm"), sem("tr_ready"), sem("spill_done")
        lists_ready, lt_mm, lt_ready, exp_in, exp_ready = (
            sem("lists_ready"), sem("lt_mm"), sem("lt_ready"), sem("exp_in"), sem("exp_ready"))
        hot2_ready = [sem(f"hot2_ready{i}") for i in range(2)]
        pos_ready, part_ready, dist_ready, dist2_ready = (
            sem("pos_ready"), sem("part_ready"), sem("dist_ready"), sem("dist2_ready"))
        hot_ready, gate_mm, gate_out = sem("hot_ready"), sem("gate_mm"), sem("gate_out")
        gelu_ready, w_ready, wh_ready, wl_ready = (
            sem("gelu_ready"), sem("w_ready"), sem("wh_ready"), sem("wl_ready"))
        fin_in, fy_ready, fsum_ready, out_ready, out_done = (
            sem("fin_in"), sem("fy_ready"), sem("fsum_ready"), sem("out_ready"), sem("out_done"))

        ada_sum, ln_r, t_ready, mxs_ready, mt_ready = (
            sem("ada_sum"), sem("ln_r"), sem("t_ready"), sem("mxs_ready"), sem("mt_ready"))
        vg_ready, mg_ready, acc_clear, diag_ready = (
            sem("vg_ready"), sem("mg_ready"), sem("acc_clear"), sem("diag_ready"))

        block = ctx.enter_context(nc.Block())

        @block.sync
        def _(sp):
            def load(c, g=None, group=None, j=0):
                if g is not None or c >= RING:
                    sp.wait_ge(l_done, up(c - RING + 1, g, RING))
                slot = c % RING
                if g is None:
                    sp.dma_start(raw[:, slot, :], stream[c]).then_inc(raw_in[slot], 16)
                else:
                    sp.dma_start(raw[:, slot:slot + 1, :], group[j][:, bass.ds(g, 1), :]).then_inc(raw_in[slot], 16)

            def groups(c, n):
                return stream[c:c + RING * n].rearrange("(g j) p n -> j p g n", j=RING)

            def row(lo, n):
                return rows[lo:lo + n].partition_broadcast(P)

            sp.dma_start(x[:, :, :], xT).then_inc(x_in, 16)
            sp.dma_start(vec[:, :], vecs).then_inc(x_in, 16)
            load(0)
            load(1)
            sp.dma_start(idio[:, :], cI).then_inc(c_in, 16)
            sp.dma_start(cb[:, :], row(0, D)).then_inc(c_in, 16)
            load(2)
            load(3)
            sp.dma_start(ada[:, 0, :], adaT[0]).then_inc(ada_in[0], 16)
            sp.dma_start(ws[:, :, :], wsT).then_inc(a_in, 16)
            sp.dma_start(lng[:, :, :].rearrange("p g n -> p (g n)"), row(D, AW)).then_inc(a_in, 16)
            sp.dma_start(lnb[:, :, :].rearrange("p g n -> p (g n)"), row(D + AW, AW)).then_inc(a_in, 16)
            sp.dma_start(bsb[:, :, :].rearrange("p g n -> p (g n)"), row(D + 2 * AW, AW)).then_inc(a_in, 16)
            sp.dma_start(cBt[:, :], cB).then_inc(b_in, 16)
            sp.dma_start(bvb[:, :], row(D + 3 * AW, P)).then_inc(b_in, 16)
            sp.dma_start(sinkb[:, :, :].rearrange("p m k -> p (m k)"), row(D + 3 * AW + P, 32)).then_inc(b_in, 16)
            rounds = NCHUNK // RING
            cs = groups(RING, rounds - 1)
            with sp.Fori(0, rounds - 1) as g:
                for j in range(RING):
                    load(RING + j, g, cs, j)
            for c in range(RING * rounds, NCHUNK):
                load(c)
            sp.wait_ge(w_ready, NK)
            sp.wait_ge(spill_done, 32)
            sp.dma_start(xt2[:, :, :].rearrange("p t n -> p (t n)"), spill[:, 0:NT * D]).then_inc(fin_in, 16)
            sp.dma_start(g2r[:, :], spill[:, NT * D:NT * D + D]).then_inc(fin_in, 16)
            sp.dma_start(fgr[:, :], row(D + 3 * AW + P + 32, D)).then_inc(fin_in, 16)
            for t in range(NT):
                sp.wait_ge(out_ready, t + 1)
                sp.dma_start(out[t * P:(t + 1) * P, :], yo[:, t, :]).then_inc(out_done, 16)
            sp.wait_ge(out_done, 16 * NT)

        def spot(eng, rs):
            n = rs.stop - rs.start
            return eng.tensor_tensor(eq[:, rs, :, :].rearrange("p r k c -> p (r k) c"),
                                     posf[:, rs, :].rearrange("p r k -> p (r k)").unsqueeze(2)
                                     .broadcast_to([P, n * TOPK, NCAND]),
                                     iota[:, 0:NCAND].unsqueeze(1).broadcast_to([P, n * TOPK, NCAND]), ALU.is_equal)

        def number(eng, rs):
            n = rs.stop - rs.start
            return eng.tensor_tensor(eq[:, rs, :, :], eq[:, rs, :, :],
                                     cid[:, rs, :].unsqueeze(2).broadcast_to([P, n, TOPK, NCAND]), ALU.mult)

        def hot2_in(e, half, g=None):
            i2s = tmp[2][:, :].rearrange("p (g j) -> p g j", j=4)
            k = 2 * e + half
            i2s = i2s[:, k] if g is None else \
                i2s.rearrange("p (g k) j -> p k g j", k=4)[:, k, bass.ds(g, 1), :].rearrange("p a j -> p (a j)")
            return iota.unsqueeze(1).broadcast_to([P, 4, NK]), i2s.unsqueeze(2).broadcast_to([P, 4, NK])

        def rounds(eng, step):
            step(0)
            step(1)
            with eng.Fori(1, T // 16) as g:
                step(0, g)
                step(1, g)

        @block.scalar
        def _(act):
            link = Chain(act, act_link)
            ada_pairs = adaT.rearrange("(g j) p n -> j p g n", j=2)
            bias_pairs = att_bias.rearrange("(g j) p n -> j p g n", j=2)

            def load_ada(n, g=None):
                act.wait_ge(ada_used, up(n - 1, g, 2))
                src = adaT[n:n + 1].rearrange("a p n -> p a n") if g is None else ada_pairs[n % 2][:, bass.ds(g + n // 2, 1), :]
                act.dma_start(ada[:, n % 2:n % 2 + 1, :], src).then_inc(ada_in[n % 2], 16)

            def load_bias(m, g=None):
                act.wait_ge(s_ready, up(8 + m - 1, g, 2))
                src = att_bias[m:m + 1].rearrange("a p n -> p a n") if g is None else bias_pairs[m % 2][:, bass.ds(g + m // 2, 1), :]
                act.dma_start(bias[:, m % 2:m % 2 + 1, :], src).then_inc(bias_in[m % 2], 16)

            def hi(c, g=None):
                slot = c % RING
                act.wait_ge(raw_in[slot], up((c // RING + 1) * 16, g, 16))
                if g is not None or c >= RING:
                    act.wait_ge(chunk_done, up(c - RING + 1, g, RING))
                act.activation(WH[:, slot, :], raw[:, slot, :], ACT.Copy).then_inc(h_done, 1)

            def root(k):
                act.wait_ge(m_ready, k + 1)
                act.activation(nt[:, :], nm[:, :], ACT.Sqrt).then_inc(root_ready, 1)

            act.wait_ge(x_in, 32)
            act.activation(sq0[:, :, :], x[:, :, :], ACT.Square).then_inc(sq_ready, 1)
            for kc in range(KC):
                act.wait_ge(xg_ready, kc + 1)
                act.activation(X1H[:, kc, :], xg0[:, kc, :], ACT.Copy).then_inc(xh_ready, 1)
            for c in range(3):
                hi(c)
            root(0)
            act.wait_ge(c_in, 32)
            act.activation(cb[:, :], cb[:, :], ACT.Silu).then_inc(cb_ready, 1)

            def v_step(q, g=None):
                hi(2 * q + 3, g)
                act.wait_ge(chunk_done, up(2 * q + 2, g, 4))
                act.wait_ge(rtok_ready, 1)
                for t in range(NT):
                    act.activation(tiles(V[:, t, :].rearrange("p (q n) -> p q n", n=T), q, g, 2),
                                   ps[:, q % 2 * 2 + t:q % 2 * 2 + t + 1, 0:T], ACT.Copy,
                                   scale=rtok[:, t:t + 1]).then_inc(v_out, 1)
                if g is None and q == 0:
                    act.dma_start(ada[:, 1, :], adaT[1]).then_inc(ada_in[1], 16)
                else:
                    load_ada(q + 1, g)
                hi(2 * q + 4, g)

            for q in range(2):
                v_step(q)
            with act.Fori(1, 4) as g:
                for q in range(2):
                    v_step(q, g)
            act.wait_ge(ln_m, 1)
            act.activation(st1, st0, ACT.Sqrt).then_inc(ln_root, 1)
            act.activation(small[:, 166:167], vec[:, 0:1], ACT.Silu).then_inc(act_link, 1)

            def y_high(n, g=None):
                act.wait_ge(yf_ready, up(n + 1, g, 2))
                act.activation(tiles(YH, n, g, 2), tmp[4 + n % 2][:, :].unsqueeze(1), ACT.Copy).then_inc(yh_ready, 1)

            def ug_step(n, g=None):
                hi(19 + 2 * n, g)
                act.wait_ge(gr_ready, up(n + 1, g, 2))
                act.activation(tmp[n % 2][:, :], tmp[n % 2][:, :], ACT.Silu).then_inc(sg_ready, 1)
                load_ada(9 + n, g)
                hi(20 + 2 * n, g)
                if g is not None or n >= 1:
                    y_high(n - 1, g)

            for n in range(2):
                ug_step(n)
            with act.Fori(1, AG // 2) as g:
                for n in range(2):
                    ug_step(n, g)
            y_high(AG - 1)

            def sq_gained(n, g):
                act.wait_ge(x_ready, up(8 + n + 1, g, 4))
                act.wait_ge(sacc_done, up(8 + 2 * n - 1, g, 8))
                act.activation(tmp[4][:, :].unsqueeze(1), tiles(x, n, g, 4), ACT.Square).then_inc(sq_ready, 1)
                act.wait_ge(sacc_done, up(8 + 2 * n, g, 8))
                act.activation(tmp[3][:, :].unsqueeze(1), tiles(x, n, g, 4), ACT.Square,
                               scale=column(vec[:, V_FG:V_FG + 8], n, g, 4)).then_inc(sq_ready, 1)

            def sq_tile(k, src, ready, value, n, g, per):
                act.wait_ge(ready, up(value, g, per))
                if not (g is None and k == 0):
                    act.wait_ge(sacc_done, up(k, g, per))
                act.activation(tmp[4][:, :].unsqueeze(1), tiles(src, n, g, per), ACT.Square).then_inc(sq_ready, 1)

            def aout_step(n, g=None):
                hi(51 + 2 * n, g)
                load_ada(25 + n, g)
                hi(52 + 2 * n, g)
                sq_tile(n, x, x_ready, n + 1, n, g, 2)
                for i, XH in enumerate((X1H, X2H)):
                    act.wait_ge(xg_ready, up(KC + 2 * n + i + 1, g, 4))
                    act.activation(tiles(XH, n, g, 2), tmp[2 * i + n % 2][:, :].unsqueeze(1),
                                   ACT.Copy).then_inc(xh_ready, 1)

            for n in range(2):
                aout_step(n)
            with act.Fori(1, 4) as g:
                for n in range(2):
                    aout_step(n, g)
            hi(67)
            root(1)
            hi(68)

            def exps(p, g, sinks):
                par = p % 2
                act.wait_ge(dsk_ready if sinks else negm_ready, up(p + 1, g, 2))
                if g is not None or p >= 1:
                    act.wait_ge(pt_mm, up(p, g, 2))
                if g is not None or p >= 2:
                    act.wait_ge(rc_ready, up(p - 1, g, 2))
                for k in range(4):
                    act.activation(pr[:, k, :], s[:, k, :], ACT.Exp, bias=negm[:, k:k + 1],
                                   accum_out=small_den[:, par, k:k + 1]).then_inc(p_ready, 1)
                if sinks:
                    act.activation(small_es[:, par, :], dsk, ACT.Exp).then_inc(es_ready, 1)

            def pt_out(p, g):
                act.wait_ge(pt_mm, up(p + 1, g, 2))
                if g is not None or p >= 1:
                    act.wait_ge(o_mm, up(p, g, 2))
                for h in range(2):
                    act.activation(pT[:, h, :, :].rearrange("p k t -> p (k t)"), ps[:, 6 + h, :],
                                   ACT.Copy).then_inc(pt_ready, 1)

            def swa_step(m, g=None):
                if m < 8:
                    hi(69 + 2 * m, g)
                if 1 <= m <= 8:
                    exps(m - 1, g, True)
                if m < 8:
                    load_ada(33 + m, g)
                    hi(70 + 2 * m, g)
                    act.wait_ge(gr_ready, up(AG + m + 1, g, 2))
                    if g is not None or m >= 2:
                        act.wait_ge(th_ready, up(m - 1, g, 2))
                    act.activation(th[:, m % 2, :], gr2[:, m % 2, :], ACT.Tanh).then_inc(gate_ready, 1)
                if 1 <= m <= 8:
                    pt_out(m - 1, g)
                if m >= 2:
                    act.wait_ge(yf_ready, up(AG + m - 1, g, 2))
                    act.activation(tiles(YH, m - 2, g, 2), tmp[4 + m % 2][:, :].unsqueeze(1),
                                   ACT.Copy).then_inc(yh_ready, 1)

            def steps(eng, step):
                for m in range(4):
                    step(m)
                with eng.Fori(1, 3) as g:
                    step(2, g)
                    step(3, g)
                step(8)
                step(9)

            steps(act, swa_step)

            def bout_step(n, g):
                hi(85 + n, g)
                sq_gained(n, g)

            with act.Fori(0, 2) as g:
                for n in range(4):
                    bout_step(n, g)
            root(2)
            root(3)

            def x1_high(n0):
                for kc in range(KC):
                    act.wait_ge(xg_ready, n0 + kc + 1)
                    act.activation(X1H[:, kc, :], F[:, kc, :], ACT.Copy).then_inc(xh_ready, 1)

            x1_high(3 * KC)

            act.wait_ge(th_ready, NPAIR)
            for m in range(2):
                act.dma_start(bias[:, m:m + 1, :], att_bias[m:m + 1].rearrange("a p n -> p a n")).then_inc(bias_in[m], 16)
            act.dma_start(sk[:, :, :], skT).then_inc(sk_in, 16)

            def v2_step(q, g):
                hi(C_V2 + 2 * q + 3, g)
                act.wait_ge(chunk_done, up(C_V2 + 2 * q + 2, g, 4))
                for t in range(NT):
                    act.activation(tiles(vC[:, t, :].rearrange("p (q n) -> p q n", n=T), q, g, 2),
                                   ps[:, q % 2 * 2 + t:q % 2 * 2 + t + 1, 0:T], ACT.Copy).then_inc(v_out, 1)
                hi(C_V2 + 2 * q + 4, g)

            with act.Fori(0, 2) as g:
                for q in range(2):
                    v2_step(q, g)

            def mix_step(m, g=None):
                if m < 8:
                    hi(C_QK + 2 * m + 3, g)
                    act.wait_ge(chunk_done, up(C_QK + 2 * m + 1, g, 4))
                    act.wait_ge(s_mm, up(8 + m - 1, g, 2))
                    act.activation(qs[:, m % 2, :], ps[:, m % 2, 0:T], ACT.Copy).then_inc(qt_ready, 1)
                if 1 <= m <= 8:
                    exps(8 + m - 1, g, False)
                if m < 8:
                    load_ada(41 + m, g)
                    hi(C_QK + 2 * m + 4, g)
                if 1 <= m <= 8:
                    pt_out(8 + m - 1, g)
                    if m < 8:
                        load_bias(m + 1, g)
                if m == 8:
                    root(4)
                if m >= 2:
                    sq_tile(24 + m - 2, oT, ot_done, m - 1, m - 2, g, 2)

            steps(act, mix_step)
            def norm_high(k):
                for n in range(4 * k, 4 * k + 4):
                    act.wait_ge(yf_ready, AG + 8 + n + 1)
                    act.activation(YH[:, n, :], FY[:, n, :], ACT.Copy).then_inc(yh_ready, 1)

            norm_high(0)
            root(5)
            norm_high(1)

            def cout_step(n, g):
                hi(117 + n, g)
                sq_tile(32 + n, x, x_ready, 24 + n + 1, n, g, 4)

            with act.Fori(0, 2) as g:
                for n in range(4):
                    cout_step(n, g)
            root(6)
            x1_high(4 * KC)
            act.wait_ge(tr_mm, 1)
            act.wait_ge(act_link, 1)
            link.n = 1
            for i in range(4):
                link(act.activation(xtok[:, i // 2, i % 2 * 512:i % 2 * 512 + 512], ps[:, 4 + i, :], ACT.Copy))
            act.dma_start(spill[:, 0:NT * D], xtok[:, :, :].rearrange("p t n -> p (t n)")).then_inc(spill_done, 16)
            act.wait_ge(tr_mm, 2)
            for i in range(2):
                link(act.activation(g2b[:, i * 512:i * 512 + 512], ps[:, 6 + i, :], ACT.Copy))
            act.dma_start(spill[:, NT * D:NT * D + D], g2b[:, :]).then_inc(spill_done, 16)

            def wq_step(n, g=None):
                hi(125 + n, g)
                act.wait_ge(chunk_done, up(123 + n, g, 4))
                if g is not None or n >= 2:
                    act.wait_ge(sc_mm, up(n - 1, g, 4))
                act.activation(qt[:, n % 2, :], ps[:, n % 2, 0:T], ACT.Copy).then_inc(qt_ready, 1)
                act.wait_ge(sc_mm, up(n + 1, g, 4))
                if g is not None or n >= 2:
                    act.wait_ge(sc_used, up(n - 1, g, 4))
                act.activation(sc[:, n % 2, :, :].rearrange("p t n -> p (t n)"), ps[:, 2 + n % 2, 0:T],
                               ACT.Copy).then_inc(sc_ready, 1)

            for n in range(4):
                wq_step(n)
            with act.Fori(1, 4) as g:
                for n in range(4):
                    wq_step(n, g)
            act.wait_ge(exp_in, 1)
            act.activation(best[:, :, :], best[:, :, :], ACT.Exp).then_inc(exp_ready, 1)
            act.wait_ge(lt_mm, 1)
            for i in range(3):
                act.activation(tmp[i][:, :], ps[:, 4 + i, 0:T], ACT.Copy).then_inc(lt_ready, 1)
            act.wait_ge(spill_done, 32)

            def eight_step(e, g=None):
                o = O2[1][:, e, :, :].rearrange("p k n -> p (k n)")
                act.wait_ge(dist_ready, up(e + 1, g, 2))
                act.activation(o, o, ACT.Square).then_inc(dist2_ready, 1)
                act.wait_ge(dist2_ready, up(e + 1, g, 2))
                act.activation(o, o, ACT.Relu, bias=ones[:, 0:1], scale=-1.0).then_inc(hot2_ready[1], 1)
                if g is not None or e >= 1:
                    gates_out(e - 1, g)

            def gates_out(e, g=None):
                for n in range(2):
                    act.wait_ge(gate_mm, up(8 * e + 4 * n + 4, g, 16))
                    act.activation(tiles(G[:, :, :].rearrange("p (q t) n -> p q (t n)", t=4), 2 * e + n, g, 4),
                                   ps[:, 2 * (e % 2) + n:2 * (e % 2) + n + 1, :], ACT.Copy).then_inc(gate_out, 1)

            rounds(act, eight_step)
            gates_out(T // 8 - 1)

            def gelu(j, g=None):
                act.wait_ge(chunk_done, C_UV + 1 if j == 0 else up(C_UV + 2 * j, g, 4))
                if g is not None or j >= 2:
                    act.wait_ge(wl_ready, up(j - 1, g, 2))
                act.activation(tmp[j % 2][:, :], ps[:, j % 2, 0:T], ACT.Gelu).then_inc(gelu_ready, 1)

            def w_high(j, g=None):
                act.wait_ge(w_ready, up(j + 1, g, 2))
                if g is not None or j >= 2:
                    act.wait_ge(chunk_done, up(C_UV + 2 * j - 1, g, 4))
                act.activation(wvH[:, j % 2, :], tmp[2 + j % 2][:, :], ACT.Copy).then_inc(wh_ready, 1)

            hi(141)
            gelu(0)
            w_high(0)
            hi(142)
            hi(143)
            def column_step(j, g=None):
                gelu(j, g)
                w_high(j, g)
                hi(C_UV + 4 + 2 * j, g)
                hi(C_UV + 5 + 2 * j, g)

            column_step(1)
            column_step(2)
            with act.Fori(1, (NK - 4) // 2) as g:
                column_step(1, g)
                column_step(2, g)
            for j in (NK - 3, NK - 2, NK - 1):
                gelu(j)
                w_high(j)
                if j == NK - 3:
                    hi(142 + 2 * j)
                    hi(143 + 2 * j)
            for t in range(NT):
                act.wait_ge(fy_ready, t + 1)
                act.activation(sqf[:, t, :], yo[:, t, :], ACT.Square, accum_out=fsum[:, t:t + 1]).then_inc(fsum_ready, 1)
            act.wait_ge(ln_m, 2)
            act.activation(st1, st0, ACT.Sqrt).then_inc(ln_root, 1)

        @block.vector
        def _(dve):
            link = Chain(dve, dve_link)

            def lo(c, g=None):
                slot = c % RING
                dve.wait_ge(h_done, up(c + 1, g, RING))
                if g is not None or c >= RING:
                    dve.wait_ge(chunk_done, up(c - RING + 1, g, RING))
                dve.tensor_tensor(WL[:, slot, :], raw[:, slot, :], WH[:, slot, :].bitcast(F32),
                                  ALU.subtract).then_inc(l_done, 1)

            def ada_tile(n, g=None):
                dve.wait_ge(ada_in[n % 2], up((n // 2 + 1) * 16, g, 16))
                if g is not None or n >= 1:
                    dve.wait_ge(ada_used, up(n, g, 2))
                dve.tensor_tensor_reduce(ada[:, n % 2, :], ada[:, n % 2, :], cb[:, :], 1.0, 0.0,
                                         ALU.mult, ALU.add, st2).then_inc(ada_sum, 1)
                dve.wait_ge(ada_sum, up(n + 1, g, 2))
                dve.tensor_copy(column(modT, n, g, 2), st2).then_inc(ada_used, 1)

            def newton(y, m, t, last):
                link(dve.tensor_tensor(t, y, y, ALU.mult))
                link(dve.tensor_tensor(t, t, m, ALU.mult))
                link(dve.tensor_scalar(t, t, -0.5, 1.5, ALU.mult, ALU.add))
                dve.tensor_tensor(y, y, t, ALU.mult).then_inc(last, 1)

            def rms(k, width, eps, sums):
                dve.wait_ge(psn_ready, k + 1)
                dve.tensor_scalar(nm[:, :], sums, 1.0 / width, eps, ALU.mult, ALU.add).then_inc(m_ready, 1)
                dve.wait_ge(root_ready, k + 1)
                link(dve.reciprocal(R[:, k % 2, :], nt[:, :]))
                newton(R[:, k % 2, :], nm[:, :], nt[:, :], r_ready)
                dve.wait_ge(r_ready, k + 1)

            def rms_tokens(k):
                dve.wait_ge(rt_ready, k + 1)
                dve.tensor_copy(rtok[:, 2 * k:2 * k + 2],
                                ps[:, 7, T:2 * T].rearrange("p (t c) -> p t c", c=P)[:, :, 0]).then_inc(rtok_ready, 1)

            dve.memset(ones[:, :], 1.0).then_inc(ones_ready, 1)
            dve.wait_ge(x_in, 32)
            for kc in range(KC):
                dve.tensor_scalar(xg0[:, kc, :], x[:, kc, :], vec[:, V_AG + kc:V_AG + kc + 1], None,
                                  ALU.mult).then_inc(xg_ready, 1)
            dve.wait_ge(sq_ready, 1)
            dve.tensor_reduce(tmp[5][:, :], sq0[:, :, :].rearrange("p k t -> p t k"), AX_X, ALU.add).then_inc(sum_ready, 1)
            for kc in range(KC):
                dve.wait_ge(xh_ready, kc + 1)
                dve.tensor_tensor(X1L[:, kc, :], xg0[:, kc, :], X1H[:, kc, :].bitcast(F32),
                                  ALU.subtract).then_inc(xl_ready, 1)
            for c in range(3):
                lo(c)
            rms(0, D, EPS_A, ps[:, 7, 0:T])
            dve.wait_ge(cb_ready, 1)

            def v_step(q, g=None):
                lo(2 * q + 3, g)
                ada_tile(q, g)
                if g is None and q == 0:
                    rms_tokens(0)
                lo(2 * q + 4, g)
                for t in range(NT):
                    dve.wait_ge(v_out, up(2 * q + t + 1, g, 4))
                    dve.bn_stats(tiles(vst[:, t, :, :], q, g, 2),
                                 tiles(V[:, t, :].rearrange("p (q n) -> p q n", n=T), q, g, 2)).then_inc(st_done, 1)

            for q in range(2):
                v_step(q)
            with dve.Fori(1, 4) as g:
                for q in range(2):
                    v_step(q, g)
            dve.wait_ge(st_done, 16)
            for t in range(NT):
                link(dve.bn_aggr(mv[:, 2 * t:2 * t + 2], vst[:, t, :, :]))
            dve.tensor_scalar(st0, mv[:, 1:4:2], 1.0, EPS_A, ALU.mult, ALU.add).then_inc(ln_m, 1)
            dve.wait_ge(ln_root, 1)
            link(dve.reciprocal(rstd, st1))
            newton(rstd, st0, st1, ln_r)
            dve.wait_ge(ln_r, 1)
            for t in range(NT):
                dve.tensor_scalar(V[:, t, :], V[:, t, :], mv[:, 2 * t:2 * t + 1], rstd[:, t:t + 1],
                                  ALU.subtract, ALU.mult).then_inc(xhat_ready, 1)

            def y_low(n, count, src, g, per):
                dve.wait_ge(yh_ready, up(count + 1, g, per))
                dve.tensor_tensor(tiles(YL, n, g, per), src, tiles(YH, n, g, per).bitcast(F32),
                                  ALU.subtract).then_inc(yl_ready, 1)

            def ug_step(n, g=None):
                lo(19 + 2 * n, g)
                dve.wait_ge(chunk_done, up(17 + 2 * n, g, 4))
                if g is not None or n >= 2:
                    dve.wait_ge(yf_ready, up(n - 1, g, 2))
                dve.tensor_tensor(uR[:, n % 2, :], ps[:, n % 2, 0:T], R[:, 0, :], ALU.mult).then_inc(ur_ready, 1)
                dve.wait_ge(chunk_done, up(18 + 2 * n, g, 4))
                dve.tensor_tensor(tmp[n % 2][:, :], ps[:, 2 + n % 2, 0:T], R[:, 0, :], ALU.mult).then_inc(gr_ready, 1)
                lo(20 + 2 * n, g)
                ada_tile(8 + n, g)
                dve.wait_ge(sv_mm, up(n + 1, g, 2))
                dve.tensor_tensor(tmp[2 + n % 2][:, :].rearrange("p (c t) -> p c t", c=NT),
                                  ps[:, 4 + n % 2, 0:T].rearrange("p (c t) -> p c t", c=NT),
                                  tiles(bsb, n, g, 2).broadcast_to([P, NT, P]), ALU.add).then_inc(svb_ready, 1)
                if g is not None or n >= 1:
                    y_low(n - 1, n - 1, tmp[4 + (n - 1) % 2][:, :].unsqueeze(1), g, 2)

            for n in range(2):
                ug_step(n)
            with dve.Fori(1, AG // 2) as g:
                for n in range(2):
                    ug_step(n, g)
            y_low(AG - 1, AG - 1, tmp[5][:, :].unsqueeze(1), None, 2)

            def x_low(XL, XH, n, count, src, g, per, cper):
                dve.wait_ge(xh_ready, up(count + 1, g, cper))
                dve.tensor_tensor(tiles(XL, n, g, per), src, tiles(XH, n, g, per).bitcast(F32),
                                  ALU.subtract).then_inc(xl_ready, 1)

            def aout_step(n, g=None):
                lo(51 + 2 * n, g)
                lo(52 + 2 * n, g)
                dve.wait_ge(chunk_done, up(50 + 2 * n, g, 4))
                dve.tensor_tensor(tiles(x, n, g, 2), tiles(x, n, g, 2), ps[:, n % 2:n % 2 + 1, 0:T],
                                  ALU.add).then_inc(x_ready, 1)
                ada_tile(24 + n, g)
                dve.wait_ge(x_ready, up(n + 1, g, 2))
                for i, gain in enumerate((V_KG, V_BG)):
                    dve.tensor_scalar(tmp[2 * i + n % 2][:, :].unsqueeze(1), tiles(x, n, g, 2),
                                      column(vec[:, gain:gain + 8], n, g, 2), None, ALU.mult).then_inc(xg_ready, 1)
                for i, (XH, XL) in enumerate(((X1H, X1L), (X2H, X2L))):
                    x_low(XL, XH, n, KC + 2 * n + i, tmp[2 * i + n % 2][:, :].unsqueeze(1), g, 2, 4)

            for n in range(2):
                aout_step(n)
            with dve.Fori(1, 4) as g:
                for n in range(2):
                    aout_step(n, g)
            dve.wait_ge(ada_used, 32)
            link(dve.tensor_tensor(mod[:, 0:32], modT[:, 0:32], vec[:, V_ADAB:V_ADAB + 32], ALU.add))
            link(dve.tensor_scalar(s1, mod[:, 8:16], 1.0, None, ALU.add))
            link(dve.tensor_tensor(s1, s1, vec[:, V_N1:V_N1 + 8], ALU.mult))
            lo(67)
            rms(1, D, EPS_A, ps[:, 7, 0:T])

            def rope_in(i, bank, bcol, g=None):
                dve.tensor_tensor(tmp[0][:, :], ps[:, bank, 0:T], R[:, 1, :], ALU.mult).then_inc(t_ready, 1)
                dve.wait_ge(t_ready, up(i + 1, g, 2))
                if g is not None or i >= 2:
                    dve.wait_ge(q_ready, up(i - 1, g, 2))
                dve.tensor_scalar(qb[:, i % 2, :], tmp[0][:, :], bcol, None, ALU.add).then_inc(qb_ready, 1)

            def rope_out(i, bank, g=None):
                dve.wait_ge(rope_mm, up(i + 1, g, 2))
                if g is not None or i >= 2:
                    dve.wait_ge(q_ready, up(i - 1, g, 2))
                dve.tensor_tensor(tmp[2 + i % 2][:, :], ps[:, bank, T:2 * T], sinT, ALU.mult).then_inc(rope_s, 1)

            dve.wait_ge(b_in, 48)
            dve.wait_ge(chunk_done, C_KV + 1)
            rope_in(0, 6, vec[:, V_BK:V_BK + 1])
            lo(68)
            rope_out(0, 6)
            rms_tokens(1)
            dve.wait_ge(rtok_ready, 2)
            dve.wait_ge(chunk_done, C_KV + 2)
            for t in range(NT):
                dve.scalar_tensor_tensor(out=vB[:, t, :], in0=ps[:, 5, t * P:(t + 1) * P],
                                         scalar=rtok[:, 2 + t:3 + t], in1=bvb[:, :],
                                         op0=ALU.mult, op1=ALU.add).then_inc(v_ready, 1)

            def soft_in(p, g, sinks):
                dve.wait_ge(s_mm, up(p + 1, g, 2))
                if g is not None or p >= 1:
                    dve.wait_ge(p_ready, up(4 * p, g, 8))
                if sinks:
                    if g is not None or p >= 1:
                        dve.wait_ge(es_ready, up(p, g, 2))
                    b = mask.unsqueeze(1).broadcast_to([P, 2, 2 * T])
                else:
                    dve.wait_ge(bias_in[p % 2], up(((p - 8) // 2 + 1) * 16, g, 16))
                    b = bias[:, p % 2, :].rearrange("p (h n) -> p h n", h=2)
                ins = dve.scalar_tensor_tensor(out=s[:, :, :].rearrange("p (h t) k -> p h (t k)", h=2),
                                               in0=ps[:, 4:6, :], scalar=HD ** -0.5, in1=b,
                                               op0=ALU.mult, op1=ALU.add)
                ins.then_inc(s_ready, 1)
                dve.wait_ge(s_ready, up(p + 1, g, 2))
                dve.tensor_reduce(mx, s[:, :, :], AX_X, ALU.max).then_inc(mx_ready, 1)
                dve.wait_ge(mx_ready, up(p + 1, g, 2))
                if sinks:
                    sink = tiles(sinkb, p, g, 2)
                    dve.tensor_tensor(mx.unsqueeze(1), mx.unsqueeze(1), sink, ALU.max).then_inc(mxs_ready, 1)
                    dve.wait_ge(mxs_ready, up(p + 1, g, 2))
                dve.tensor_scalar(negm, mx, -1.0, None, ALU.mult).then_inc(negm_ready, 1)
                dve.wait_ge(negm_ready, up(p + 1, g, 2))
                if sinks:
                    dve.tensor_tensor(dsk.unsqueeze(1), negm.unsqueeze(1), sink, ALU.add).then_inc(dsk_ready, 1)

            def soft_sum(p, g, sinks):
                par = p % 2
                dve.wait_ge(p_ready, up(4 * p + 4, g, 8))
                if sinks:
                    dve.wait_ge(es_ready, up(p + 1, g, 2))
                    dve.tensor_tensor(small_den[:, par, :], small_den[:, par, :], small_es[:, par, :],
                                      ALU.add).then_inc(den_ready, 1)
                    dve.wait_ge(den_ready, up(p + 1, g, 2))
                dve.reciprocal(small_rc[:, par, :], small_den[:, par, :]).then_inc(rc_ready, 1)

            def o_out(p, g):
                dve.wait_ge(o_mm, up(p + 1, g, 2))
                dve.wait_ge(rc_ready, up(p + 1, g, 2))
                if g is not None or p >= 1:
                    dve.wait_ge(ot_mm, up(p, g, 2))
                r = small_rc[:, p % 2, :].rearrange("p (h t) -> p t h", h=2).unsqueeze(3).broadcast_to([P, NT, 2, HD])
                dve.tensor_tensor(on[:, :, :].rearrange("p t (h d) -> p t h d", h=2),
                                  ps[:, 2 + (p + 1) % 2, T:2 * T].rearrange("p (t h d) -> p t h d", t=NT, h=2),
                                  r, ALU.mult).then_inc(on_ready, 1)

            def swa_step(m, g=None):
                if m < 8:
                    lo(69 + 2 * m, g)
                    dve.wait_ge(chunk_done, up(67 + 2 * m, g, 4))
                    rope_in(m + 1, m % 2, column(vec[:, V_BQ:V_BQ + 8], m, g, 2), g)
                if 1 <= m <= 8:
                    soft_in(m - 1, g, True)
                    dve.wait_ge(gate_ready, up(m, g, 2))
                    k = (m - 1) % 2
                    dve.scalar_tensor_tensor(out=tiles(sgate, m - 1, g, 2), in0=th[:, k:k + 1, :], scalar=1.0,
                                             in1=gr2[:, k:k + 1, :], op0=ALU.add, op1=ALU.mult).then_inc(th_ready, 1)
                if m >= 2:
                    o_out(m - 2, g)
                if m < 8:
                    ada_tile(32 + m, g)
                    lo(70 + 2 * m, g)
                    dve.wait_ge(chunk_done, up(68 + 2 * m, g, 4))
                    dve.scalar_tensor_tensor(out=gr2[:, m % 2, :], in0=ps[:, 2 + m % 2, 0:T], scalar=0.5,
                                             in1=R[:, 1, :], op0=ALU.mult, op1=ALU.mult).then_inc(gr_ready, 1)
                    rope_out(m + 1, m % 2, g)
                if 1 <= m <= 8:
                    soft_sum(m - 1, g, True)
                if m >= 2:
                    dve.wait_ge(ot_mm, up(m - 1, g, 2))
                    dve.wait_ge(th_ready, up(m - 1, g, 2))
                    y = tmp[4 + m % 2][:, :].unsqueeze(1)
                    dve.tensor_tensor(y, ps[:, 2 + (m + 1) % 2:3 + (m + 1) % 2, T:2 * T], tiles(sgate, m - 2, g, 2),
                                      ALU.mult).then_inc(yf_ready, 1)
                    y_low(m - 2, AG + m - 2, y, g, 2)

            def steps(eng, step):
                for m in range(4):
                    step(m)
                with eng.Fori(1, 3) as g:
                    step(2, g)
                    step(3, g)
                step(8)
                step(9)

            steps(dve, swa_step)

            def bout_step(n, g):
                lo(85 + n, g)
                dve.wait_ge(chunk_done, up(C_BOUT + n + 1, g, 4))
                dve.tensor_tensor(tiles(x, n, g, 4), tiles(x, n, g, 4), ps[:, n % 2:n % 2 + 1, 0:T],
                                  ALU.add).then_inc(x_ready, 1)

            with dve.Fori(0, 2) as g:
                for n in range(4):
                    bout_step(n, g)
            rms(2, D, EPS_A, ps[:, 7, 0:T])
            dve.wait_ge(psn_ready, 4)
            link(dve.tensor_tensor(tmp[0][:, :], R[:, 0, :], R[:, 0, :], ALU.mult))
            link(dve.tensor_tensor(tmp[0][:, :], tmp[0][:, :], ps[:, 7, T:2 * T], ALU.mult))
            rms(3, D, EPS_B, tmp[0][:, :])
            for kc in range(KC):
                dve.scalar_tensor_tensor(out=x[:, kc, :], in0=x[:, kc, :], scalar=vec[:, V_FG + kc:V_FG + kc + 1],
                                         in1=R[:, 0, :], op0=ALU.mult, op1=ALU.mult).then_inc(x_ready, 1)

            def modulated(k, gains, shifts):
                for kc in range(KC):
                    if k == 0:
                        dve.wait_ge(x_ready, 16 + kc + 1)
                    dve.scalar_tensor_tensor(out=F[:, kc, :], in0=x[:, kc, :], scalar=gains[:, kc:kc + 1],
                                             in1=R[:, 1 - k, :], op0=ALU.mult, op1=ALU.mult).then_inc(mt_ready, 1)
                for kc in range(KC):
                    dve.wait_ge(mt_ready, k * KC + kc + 1)
                    dve.tensor_scalar(F[:, kc, :], F[:, kc, :], shifts[:, kc:kc + 1], None, ALU.add).then_inc(xg_ready, 1)
                for kc in range(KC):
                    dve.wait_ge(xh_ready, (3 + k) * KC + kc + 1)
                    dve.tensor_tensor(X1L[:, kc, :], F[:, kc, :], X1H[:, kc, :].bitcast(F32),
                                      ALU.subtract).then_inc(xl_ready, 1)

            modulated(0, s1, mod[:, 0:8])

            def v2_step(q, g):
                lo(C_V2 + 2 * q + 3, g)
                lo(C_V2 + 2 * q + 4, g)

            with dve.Fori(0, 2) as g:
                for q in range(2):
                    v2_step(q, g)

            def mix_step(m, g=None):
                if m < 8:
                    lo(C_QK + 2 * m + 3, g)
                if 1 <= m <= 8:
                    soft_in(8 + m - 1, g, False)
                if m >= 2:
                    o_out(8 + m - 2, g)
                if m < 8:
                    ada_tile(40 + m, g)
                    lo(C_QK + 2 * m + 4, g)
                    dve.wait_ge(chunk_done, up(C_QK + 2 * m + 2, g, 4))
                    if g is not None or m >= 2:
                        dve.wait_ge(s_mm, up(8 + m - 1, g, 2))
                    dve.tensor_copy(ks[:, m % 2, :], ps[:, 2 + m % 2, 0:T]).then_inc(k_ready, 1)
                if 1 <= m <= 8:
                    soft_sum(8 + m - 1, g, False)
                if m >= 2:
                    dve.wait_ge(ot_mm, up(8 + m - 1, g, 2))
                    dve.tensor_copy(tiles(oT, m - 2, g, 2),
                                    ps[:, 2 + (m + 1) % 2:3 + (m + 1) % 2, T:2 * T]).then_inc(ot_done, 1)
                if m == 8:
                    rms(4, D // 2, EPS_B, ps[:, 0, T:2 * T])

            steps(dve, mix_step)
            dve.wait_ge(ada_used, NMOD)
            link(dve.tensor_tensor(mod[:, 32:48], modT[:, 32:48], vec[:, V_ADAB + 32:V_ADAB + 48], ALU.add))
            link(dve.tensor_scalar(s2, mod[:, 32:40], 1.0, None, ALU.add))
            link(dve.tensor_tensor(s2, s2, vec[:, V_N2:V_N2 + 8], ALU.mult))
            dve.wait_ge(ot_done, NPAIR)

            def normed(k):
                for n in range(4 * k, 4 * k + 4):
                    dve.scalar_tensor_tensor(out=FY[:, n, :], in0=oT[:, n, :], scalar=vec[:, V_OG + n:V_OG + n + 1],
                                             in1=R[:, k, :], op0=ALU.mult, op1=ALU.mult).then_inc(yf_ready, 1)

            def normed_low(k):
                for n in range(4 * k, 4 * k + 4):
                    y_low(n, AG + 8 + n, FY[:, n:n + 1, :], None, 1)

            normed(0)
            rms(5, D // 2, EPS_B, ps[:, 7, 0:T])
            normed(1)
            normed_low(0)
            normed_low(1)

            def cout_step(n, g):
                lo(117 + n, g)
                dve.wait_ge(chunk_done, up(C_COUT + n + 1, g, 4))
                dve.scalar_tensor_tensor(out=tiles(x, n, g, 4), in0=ps[:, n % 2:n % 2 + 1, 0:T],
                                         scalar=column(mod[:, 16:24], n, g, 4), in1=tiles(x, n, g, 4),
                                         op0=ALU.mult, op1=ALU.add).then_inc(x_ready, 1)

            with dve.Fori(0, 2) as g:
                for n in range(4):
                    cout_step(n, g)
            rms(6, D, EPS_B, ps[:, 7, 0:T])
            modulated(1, s2, mod[:, 24:32])
            dve.wait_ge(c_in, 32)
            dve.wait_ge(bias_in[0], (NPAIR // 2 + 1) * 16)
            dve.tensor_tensor(diags[:, :, :], ident.unsqueeze(1).broadcast_to([P, KC, P]),
                              mod[:, 40:48].unsqueeze(2).broadcast_to([P, KC, P]), ALU.mult).then_inc(diag_ready, 1)

            for n in range(2 * PH):
                lo(125 + n)
                dve.wait_ge(sc_ready, n + 1)
                for t in range(NT):
                    row, b8 = sc[:, n % 2, t, :], v16[:, t, n, :]
                    link(dve.max(b8[:, 0:8], row))
                    link(dve.max_index(ix8[:, 0:8], b8[:, 0:8], row))
                    link(dve.match_replace(sc2[:, :], b8[:, 0:8], row, NEG))
                    link(dve.max(b8[:, 8:16], sc2[:, :]))
                    link(dve.max_index(ix8[:, 8:16], b8[:, 8:16], sc2[:, :]))
                    ins = dve.tensor_copy(i16[:, t, n, :], ix8[:, :])
                    if t == NT - 1:
                        ins.then_inc(sc_used, 1)
                        dve.wait_ge(sc_used, n + 1)
                    else:
                        link(ins)

            vr = v16[:, :, :, :].rearrange("p t (h q) k -> p (t h) q k", q=2)
            ir = i16[:, :, :, :].rearrange("p t (h q) k -> p (t h) q k", q=2)
            steps_ = [(a, a + 1, ROWS[a], STARTS[a]) for a in range(8)] + [(8, TOPK, 1, STARTS[8])]
            R16 = NT * PH
            for a, b, n, at0 in steps_:
                w = n * (b - a)
                va, ia = vr[:, :, 0, a:b], ir[:, :, 0, a:b]
                vb, ib = vr[:, :, 1, 0:n], ir[:, :, 1, 0:n]
                if n > 1:
                    va, ia = va.broadcast_to([P, R16, n]), ia.broadcast_to([P, R16, n])
                elif b - a > 1:
                    vb, ib = vb.broadcast_to([P, R16, b - a]), ib.broadcast_to([P, R16, b - a])
                link(dve.tensor_tensor(cand[:, :, at0:at0 + w], va, vb, ALU.add))
                link(dve.scalar_tensor_tensor(out=cid[:, :, at0:at0 + w], in0=ia, scalar=float(NK), in1=ib,
                                              op0=ALU.mult, op1=ALU.add))
            for r in range(R16):
                row, b8, c2 = cand[:, r, :], best[:, r, :], sc2[:, 0:NCAND]
                link(dve.max(b8[:, 0:8], row))
                link(dve.max_index(pos[:, r, 0:8], b8[:, 0:8], row))
                link(dve.match_replace(c2, b8[:, 0:8], row, NEG))
                link(dve.max(b8[:, 8:16], c2))
                link(dve.max_index(pos[:, r, 8:16], b8[:, 8:16], c2))
                if r == POOL_ROWS - 1:
                    link(dve.tensor_copy(posf[:, 0:POOL_ROWS, :], pos[:, 0:POOL_ROWS, :]))
                    spot(dve, slice(0, POOL_ROWS)).then_inc(pos_ready, 1)
            link(dve.tensor_copy(zsum[:, :], best[:, :, 0]))
            dve.tensor_tensor(best[:, :, :], best[:, :, :], zsum[:, :].unsqueeze(2).broadcast_to([P, R16, TOPK]),
                              ALU.subtract).then_inc(exp_in, 1)
            link(dve.tensor_copy(posf[:, POOL_ROWS:, :], pos[:, POOL_ROWS:, :]))
            own, theirs = slice(POOL_ROWS, R16), slice(0, POOL_ROWS)
            link(spot(dve, own))
            link(number(dve, own))
            link(dve.tensor_reduce(sid[:, own, :], eq[:, own, :, :], AX_X, ALU.add))
            dve.wait_ge(part_ready, 1)
            link(dve.tensor_reduce(sid[:, theirs, :], eq[:, theirs, :, :], AX_X, ALU.add))
            link(dve.tensor_copy(pos[:, :, :], sid[:, :, :]))
            link(dve.tensor_scalar(posi[:, :, :], pos[:, :, :], 7, None, ALU.logical_shift_right))
            link(dve.tensor_scalar(pos[:, :, :], pos[:, :, :], NK - 1, None, ALU.bitwise_and))
            link(dve.tensor_copy(i1[:, :, :], posi[:, :, :]))
            link(dve.tensor_copy(i2[:, :, :], pos[:, :, :]))
            dve.wait_ge(exp_ready, 1)
            link(dve.tensor_reduce(zsum[:, :], best[:, :, :], AX_X, ALU.add))
            link(dve.reciprocal(zsum[:, :], zsum[:, :]))
            dve.tensor_tensor(best[:, :, :], best[:, :, :], zsum[:, :].unsqueeze(2).broadcast_to([P, R16, TOPK]),
                              ALU.mult).then_inc(lists_ready, 1)
            dve.wait_ge(lt_ready, 3)

            def eight_step(e, g=None):
                if g is not None or e >= 2:
                    dve.wait_ge(gate_mm, up(8 * e - 12, g, 16))
                dve.tensor_tensor(O2[0][:, e, :, :], *hot2_in(e, 0, g), ALU.is_equal).then_inc(hot2_ready[0], 1)
                for n in range(8):
                    if g is not None or e >= 1:
                        dve.wait_ge(gate_mm, up(8 * e + n - 7, g, 16))
                    dve.tensor_scalar(O1[:, n, :], iota, column(tmp[1], 8 * e + n, g, 16),
                                      column(tmp[0], 8 * e + n, g, 16), ALU.is_equal, ALU.mult).then_inc(hot_ready, 1)

            rounds(dve, eight_step)

            def gated(j, g=None):
                dve.wait_ge(gelu_ready, up(j + 1, g, 2))
                if g is not None or j >= 2:
                    dve.wait_ge(wl_ready, up(j - 1, g, 2))
                gj = G[:, :, j:j + 1] if g is None else \
                    G[:, :, 1:NK - 1].rearrange("p t (g j) -> p j t g", j=2)[:, j - 1, :, bass.ds(g, 1)]
                dve.tensor_tensor(tmp[2 + j % 2][:, :].unsqueeze(2), tmp[j % 2][:, :].unsqueeze(2), gj,
                                  ALU.mult).then_inc(w_ready, 1)

            def w_low(j, g=None):
                dve.wait_ge(wh_ready, up(j + 1, g, 2))
                if g is not None or j >= 2:
                    dve.wait_ge(chunk_done, up(C_UV + 2 * j - 1, g, 4))
                dve.tensor_tensor(wvL[:, j % 2, :], tmp[2 + j % 2][:, :], wvH[:, j % 2, :].bitcast(F32),
                                  ALU.subtract).then_inc(wl_ready, 1)

            dve.wait_ge(gate_out, T // 4)
            lo(141)
            gated(0)
            w_low(0)
            lo(142)
            lo(143)
            def column_step(j, g=None):
                gated(j, g)
                w_low(j, g)
                lo(C_UV + 4 + 2 * j, g)
                lo(C_UV + 5 + 2 * j, g)

            column_step(1)
            column_step(2)
            with dve.Fori(1, (NK - 4) // 2) as g:
                column_step(1, g)
                column_step(2, g)
            for j in (NK - 3, NK - 2, NK - 1):
                gated(j)
                w_low(j)
                if j == NK - 3:
                    lo(142 + 2 * j)
                    lo(143 + 2 * j)

            dve.wait_ge(fin_in, 48)
            dve.wait_ge(chunk_done, NCHUNK)
            for t in range(NT):
                for h in range(2):
                    cols = slice(h * 512, h * 512 + 512)
                    link(dve.tensor_tensor(yo[:, t, cols], ps[:, 4 + 2 * t + h, :], g2r[:, cols], ALU.mult))
                dve.tensor_tensor(yo[:, t, :], yo[:, t, :], xt2[:, t, :], ALU.add).then_inc(fy_ready, 1)
            dve.wait_ge(fsum_ready, NT)
            dve.tensor_scalar(st0, fsum, 1.0 / D, EPS_B, ALU.mult, ALU.add).then_inc(ln_m, 1)
            dve.wait_ge(ln_root, 2)
            link(dve.reciprocal(rstd, st1))
            newton(rstd, st0, st1, ln_r)
            dve.wait_ge(ln_r, 2)
            for t in range(NT):
                dve.scalar_tensor_tensor(out=yo[:, t, :], in0=yo[:, t, :], scalar=rstd[:, t:t + 1],
                                         in1=fgr[:, :], op0=ALU.mult, op1=ALU.mult).then_inc(out_ready, 1)

        @block.gpsimd
        def _(pool):
            pool.wait_ge(a_in, 64)
            pool.affine_select(out=ws[:, :, :], in_=ws[:, :, :], compare_op=ALU.is_ge, fill=0.0, base=0,
                               pattern=[[0, AG], [1, P]], channel_multiplier=-1).then_inc(ws_ready, 1)
            pool.wait_ge(xhat_ready, 2)
            Vg = V[:, :, :].rearrange("p c (n d) -> p n c d", d=P)

            def v_affine(n, g=None):
                if g is not None or n >= 2:
                    pool.wait_ge(sv_mm, up(n - 1, g, 2))
                src = Vg[:, n] if g is None else \
                    Vg.rearrange("p (g j) c d -> p j g c d", j=2)[:, n % 2, bass.ds(g + n // 2, 1)].rearrange(
                        "p a c d -> p (a c) d")
                dst = vs[:, n % 2, :].rearrange("p (c d) -> p c d", c=NT)
                pool.tensor_tensor(dst, src, tiles(lng, n, g, 2).broadcast_to([P, NT, P]), ALU.mult)\
                    .then_inc(vg_ready, 1)
                pool.wait_ge(vg_ready, up(n + 1, g, 2))
                pool.tensor_tensor(dst, dst, tiles(lnb, n, g, 2).broadcast_to([P, NT, P]), ALU.add)\
                    .then_inc(vs_ready, 1)

            def gate_product(n, g=None):
                m = tmp[4 + n % 2][:, :]
                pool.wait_ge(sg_ready, up(n + 1, g, 2))
                pool.wait_ge(svb_ready, up(n + 1, g, 2))
                if g is not None or n >= 2:
                    pool.wait_ge(yl_ready, up(n - 1, g, 2))
                pool.tensor_tensor(m, tmp[n % 2][:, :], tmp[2 + n % 2][:, :], ALU.mult).then_inc(mg_ready, 1)
                pool.wait_ge(mg_ready, up(n + 1, g, 2))
                pool.wait_ge(ur_ready, up(n + 1, g, 2))
                pool.tensor_tensor(m, m, uR[:, n % 2, :], ALU.mult).then_inc(yf_ready, 1)

            v_affine(0)
            v_affine(1)
            for n in range(2):
                gate_product(n)
                v_affine(n + 2)
            with pool.Fori(1, 7) as g:
                for n in range(2):
                    gate_product(n, g)
                    v_affine(n + 2, g)
            for n in range(14, 16):
                gate_product(n)

            pool.wait_ge(yl_ready, AG)
            pool.memset(tmp[5][:, :], 0.0).then_inc(acc_clear, 1)
            pool.wait_ge(acc_clear, 1)

            def add_square(k, acc, g=None):
                pool.wait_ge(sq_ready, up(k + 2, g, 1))
                if g is not None or k >= 1:
                    pool.wait_ge(sacc_done, up(k, g, 1))
                pool.tensor_tensor(acc, acc, tmp[4][:, :], ALU.add).then_inc(sacc_done, 1)

            add_square(0, tmp[5][:, :])
            with pool.Fori(0, KC - 1) as g:
                add_square(1, tmp[5][:, :], g)

            def rope(i, dst, waits, g=None):
                k = i % 2
                pool.wait_ge(qb_ready, up(i + 1, g, 2))
                pool.tensor_tensor(t3[:, k, :], qb[:, k, :], cosT, ALU.mult).then_inc(rope_c, 1)
                pool.wait_ge(rope_c, up(i + 1, g, 2))
                pool.wait_ge(rope_s, up(i + 1, g, 2))
                if waits is not None:
                    pool.wait_ge(s_mm, waits)
                pool.tensor_tensor(dst, t3[:, k, :], tmp[2 + k][:, :], ALU.add).then_inc(q_ready, 1)

            rope(0, ks[:, 0, :], None)
            for m in range(2):
                rope(m + 1, qs[:, m, :], None)
            with pool.Fori(0, 3) as g:
                for m in range(2, 4):
                    rope(m + 1, qs[:, m % 2, :], up(m - 1, g, 2), g)

            def clear(acc, n):
                pool.memset(acc, 0.0).then_inc(acc_clear, 1)
                pool.wait_ge(acc_clear, n)

            pool.wait_ge(yl_ready, AG + 8)
            clear(tmp[5][:, :], 2)
            clear(tmp[2][:, :], 3)
            with pool.Fori(0, KC) as g:
                for k, (acc, square) in enumerate(((tmp[5], tmp[4]), (tmp[2], tmp[3]))):
                    pool.wait_ge(sq_ready, up(8 + k + 2, g, 2))
                    pool.wait_ge(sacc_done, up(8 + k, g, 2))
                    pool.tensor_tensor(acc[:, :], acc[:, :], square[:, :], ALU.add).then_inc(sacc_done, 1)
            pool.wait_ge(psn_ready, 4)
            clear(tmp[5][:, :], 4)
            with pool.Fori(0, 4) as g:
                add_square(24, tmp[5][:, :], g)
            clear(qb[:, 0, :], 5)
            with pool.Fori(0, 4) as g:
                add_square(28, qb[:, 0, :], g)
            pool.wait_ge(psn_ready, 6)
            clear(tmp[5][:, :], 6)
            with pool.Fori(0, KC) as g:
                add_square(32, tmp[5][:, :], g)

            pool.wait_ge(pos_ready, 1)
            number(pool, slice(0, POOL_ROWS)).then_inc(part_ready, 1)

            pool.wait_ge(lt_ready, 3)

            def eight_step(e, g=None):
                if g is not None:
                    pool.wait_ge(gate_mm, up(8 * e - 8, g, 16))
                pool.tensor_tensor(O2[1][:, e, :, :], *hot2_in(e, 1, g), ALU.subtract).then_inc(dist_ready, 1)

            rounds(pool, eight_step)

        @block.tensor
        def _(pe):
            pe.wait_ge(ones_ready, 1)
            pe.wait_ge(c_in, 32)

            def product(out_ap, stat, mov, k0=0, first=True, last=True):
                sH, sL, mH, mL = (*stat, *mov)
                for kc in range(KC):
                    for i, (a, b) in enumerate(((sH, mH), (sH, mL), (sL, mH))):
                        mm = pe.matmul(out_ap, a(kc), b(kc), start=(first and kc == 0 and i == 0),
                                       stop=(last and kc == KC - 1 and i == 2))
                return mm

            def weight(W, slot, n=1):
                if n == 1:
                    return lambda kc: W[:, slot, kc * P:(kc + 1) * P]
                return lambda kc: W[:, slot:slot + n, kc * P:(kc + 1) * P]

            def acts(X, k0=0):
                return lambda kc: X[:, k0 + kc, :]

            def feature_tile(c, g, bank, XH, XL, k0=0, first=True, last=True):
                pe.wait_ge(l_done, up(c + 1, g, RING))
                mm = product(ps[:, bank, 0:T], (weight(WH, c % RING), weight(WL, c % RING)),
                             (acts(XH, k0), acts(XL, k0)), first=first, last=last)
                mm.then_inc(chunk_done, 1)

            def token_tiles(c, g, bank, XH, XL, n):
                pe.wait_ge(l_done, up(c + n, g, RING))
                for t in range(NT):
                    def x_tile(X):
                        return lambda kc: X[:, kc, t * P:(t + 1) * P]
                    o = ps[:, bank + t, 0:n * P] if n > 1 else ps[:, bank, t * P:(t + 1) * P]
                    if n > 1:
                        o = o.rearrange("p (a n) -> p a n", a=n)
                    mm = product(o, (x_tile(XH), x_tile(XL)),
                                 (weight(WH, c % RING, n), weight(WL, c % RING, n)))
                mm.then_inc(chunk_done, n)

            def spread(k, ready, count, acc, bank=7, at0=0):
                pe.wait_ge(ready, count)
                pe.matmul(ps[:, bank, at0:at0 + T], ones[:, :], acc, start=True, stop=True).then_inc(psn_ready, 1)

            def turn_rms(k):
                pe.wait_ge(r_ready, k + 1)
                for t in range(NT):
                    mm = pe.transpose(ps[:, 7, T + t * P:T + (t + 1) * P], R[:, k % 2, t * P:(t + 1) * P], ident)
                mm.then_inc(rt_ready, 1)

            spread(0, sum_ready, 1, tmp[5][:, :])
            pe.wait_ge(xl_ready, KC)
            for q in range(2):
                token_tiles(2 * q, None, 2 * q, X1H, X1L, 2)
                if q == 0:
                    turn_rms(0)
            with pe.Fori(1, 4) as g:
                for q in range(2):
                    pe.wait_ge(v_out, up(2 * q - 2, g, 4))
                    token_tiles(2 * q, g, 2 * q, X1H, X1L, 2)
            pe.wait_ge(v_out, 16)

            def ug_step(n, g=None):
                later = g is not None or n >= 2
                if later:
                    pe.wait_ge(ur_ready, up(n - 1, g, 2))
                feature_tile(16 + 2 * n, g, n % 2, X1H, X1L)
                if later:
                    pe.wait_ge(gr_ready, up(n - 1, g, 2))
                feature_tile(17 + 2 * n, g, 2 + n % 2, X1H, X1L)
                if later:
                    pe.wait_ge(svb_ready, up(n - 1, g, 2))
                pe.wait_ge(vs_ready, up(n + 1, g, 2))
                pe.wait_ge(ws_ready, 1)
                w = tiles(ws, n, g, 2)
                for c in range(NT):
                    mm = pe.matmul(ps[:, 4 + n % 2, c * P:(c + 1) * P], vs[:, n % 2, c * P:(c + 1) * P],
                                   w.rearrange("p a t -> p (a t)"), start=True, stop=True)
                mm.then_inc(sv_mm, 1)

            ug_step(0)
            ug_step(1)
            with pe.Fori(1, AG // 2) as g:
                for n in range(2):
                    ug_step(n, g)
            pe.wait_ge(ur_ready, AG)
            pe.wait_ge(yl_ready, KC)

            def aout_step(n, g=None):
                if g is not None or n >= 2:
                    pe.wait_ge(x_ready, up(n - 1, g, 2))
                feature_tile(C_AOUT + 2 * n, g, n % 2, YH, YL, 0, True, False)
                if g is None and n == 0:
                    pe.wait_ge(yl_ready, AG)
                feature_tile(C_AOUT + 2 * n + 1, g, n % 2, YH, YL, KC, False, True)

            aout_step(0)
            aout_step(1)
            with pe.Fori(1, 4) as g:
                for n in range(2):
                    aout_step(n, g)
            pe.wait_ge(xl_ready, 3 * KC)
            feature_tile(C_KV, None, 6, X1H, X1L)
            spread(1, sacc_done, KC, tmp[5][:, :])
            token_tiles(C_KV + 1, None, 5, X1H, X1L, 1)
            pe.wait_ge(b_in, 48)

            def rope_turn(i, bank, g=None):
                pe.wait_ge(qb_ready, up(i + 1, g, 2))
                pe.matmul(ps[:, bank, T:2 * T], perm, qb[:, i % 2, :], start=True, stop=True).then_inc(rope_mm, 1)

            def scores(p, g, kslot):
                for h in range(2):
                    hs = slice(h * HD, (h + 1) * HD)
                    for t in range(NT):
                        mm = pe.matmul(ps[:, 4 + h, t * T:(t + 1) * T], qs[hs, p % 2, t * P:(t + 1) * P],
                                       ks[hs, kslot, :], start=True, stop=True)
                mm.then_inc(s_mm, 1)

            def turn_probs(p, g):
                pe.wait_ge(p_ready, up(4 * p + 4, g, 8))
                if g is not None or p >= 1:
                    pe.wait_ge(pt_ready, up(2 * p, g, 4))
                for h in range(2):
                    for kt in range(NT):
                        for t in range(NT):
                            k = kt * NT + t
                            mm = pe.transpose(ps[:, 6 + h, k * P:(k + 1) * P],
                                              pr[:, 2 * h + t, kt * P:(kt + 1) * P], ident)
                mm.then_inc(pt_mm, 1)

            def values(p, g, v_of):
                pe.wait_ge(pt_ready, up(2 * p + 2, g, 4))
                for t in range(NT):
                    for h in range(2):
                        for kt in range(NT):
                            mm = pe.matmul(ps[:, 2 + (p + 1) % 2, T + t * P + h * HD:T + t * P + (h + 1) * HD],
                                           pT[:, h, kt * NT + t, :], v_of(kt, h),
                                           start=(kt == 0), stop=(kt == NT - 1))
                mm.then_inc(o_mm, 1)

            def turn_out(p, g):
                pe.wait_ge(on_ready, up(p + 1, g, 2))
                for t in range(NT):
                    mm = pe.transpose(ps[:, 2 + (p + 1) % 2, T + t * P:T + (t + 1) * P], on[:, t, :], ident)
                mm.then_inc(ot_mm, 1)

            rope_turn(0, 6)
            turn_rms(1)
            pe.wait_ge(v_ready, 2)

            def swa_step(m, g=None):
                if m < 8:
                    if g is not None or m >= 2:
                        pe.wait_ge(rope_s, up(m, g, 2))
                    feature_tile(C_QG + 2 * m, g, m % 2, X2H, X2L)
                if 1 <= m <= 8:
                    pe.wait_ge(q_ready, up(m + 1, g, 2))
                    if g is not None or m >= 2:
                        pe.wait_ge(s_ready, up(m - 1, g, 2))
                    scores(m - 1, g, 0)
                if m >= 2:
                    pe.wait_ge(gr_ready, up(AG + min(m, 8), g, 2))
                    if m == 9:
                        pe.wait_ge(yf_ready, AG + 6)
                    values(m - 2, g, lambda kt, h: vB[:, kt, h * HD:(h + 1) * HD])
                if m < 8:
                    if g is not None or m >= 3:
                        pe.wait_ge(yf_ready, up(AG + m - 2, g, 2))
                    feature_tile(C_QG + 2 * m + 1, g, 2 + m % 2, X2H, X2L)
                    rope_turn(m + 1, m % 2, g)
                if 1 <= m <= 8:
                    turn_probs(m - 1, g)
                if m >= 2:
                    turn_out(m - 2, g)

            def steps(eng, step):
                for m in range(4):
                    step(m)
                with eng.Fori(1, 3) as g:
                    step(2, g)
                    step(3, g)
                step(8)
                step(9)

            steps(pe, swa_step)

            def out_steps(c, count, x0):
                pe.wait_ge(yl_ready, count)
                with pe.Fori(0, 2) as g:
                    for n in range(4):
                        pe.wait_ge(x_ready, up(x0 + n - 1, g, 4))
                        feature_tile(c + n, g, n % 2, YH, YL)

            out_steps(C_BOUT, AG + 8, 8)
            spread(2, sacc_done, 24, tmp[5][:, :])
            pe.wait_ge(m_ready, 3)
            spread(3, sacc_done, 24, tmp[2][:, :], at0=T)
            pe.wait_ge(xl_ready, 4 * KC)
            with pe.Fori(0, 2) as g:
                for q in range(2):
                    pe.wait_ge(v_out, up(16 + 2 * q - 2, g, 4))
                    token_tiles(C_V2 + 2 * q, g, 2 * q, X1H, X1L, 2)
            vCv = vC[:, :, :].rearrange("p t (m n) -> p t m n", n=P)

            def mix_step(m, g=None):
                if m < 8:
                    pe.wait_ge(v_out, 24) if g is None and m < 2 else pe.wait_ge(qt_ready, up(m - 1, g, 2))
                    feature_tile(C_QK + 2 * m, g, m % 2, X1H, X1L)
                if 1 <= m <= 8:
                    p = m - 1
                    pe.wait_ge(qt_ready, up(p + 1, g, 2))
                    pe.wait_ge(k_ready, up(p + 1, g, 2))
                    pe.wait_ge(s_ready, up(8 + p, g, 2))
                    scores(8 + p, g, p % 2)
                if m >= 2:
                    p = m - 2
                    pe.wait_ge(k_ready, up(min(m, 8), g, 2))
                    if m == 9:
                        pe.wait_ge(ot_done, 6)

                    def v_of(kt, h):
                        v = tiles(vCv[:, kt], p, g, 2)[:, :, h * HD:(h + 1) * HD]
                        return v.rearrange("p a n -> p (a n)")
                    values(8 + p, g, v_of)
                if m < 8:
                    if g is not None or m >= 3:
                        pe.wait_ge(ot_done, up(m - 2, g, 2))
                    feature_tile(C_QK + 2 * m + 1, g, 2 + m % 2, X1H, X1L)
                if 1 <= m <= 8:
                    turn_probs(8 + m - 1, g)
                if m >= 2:
                    turn_out(8 + m - 2, g)
                if m == 8:
                    spread(4, sacc_done, 28, tmp[5][:, :], bank=0, at0=T)

            steps(pe, mix_step)
            spread(5, sacc_done, 32, qb[:, 0, :])
            out_steps(C_COUT, AG + 16, 24)
            spread(6, sacc_done, 40, tmp[5][:, :])
            pe.wait_ge(m_ready, 7)
            for t in range(NT):
                for kc in range(KC):
                    mm = pe.transpose(ps[:, 4 + 2 * t + kc // 4, kc % 4 * P:(kc % 4 + 1) * P],
                                      x[:, kc, t * P:(t + 1) * P], ident)
            mm.then_inc(tr_mm, 1)
            pe.wait_ge(diag_ready, 1)
            pe.wait_ge(act_link, 5)
            for i in range(2):
                mm = pe.matmul(ps[:, 6 + i, :], ones[:, :],
                               diags[:, 4 * i:4 * i + 4, :].rearrange("p k n -> p (k n)"), start=True, stop=True)
            mm.then_inc(tr_mm, 1)
            pe.wait_ge(xl_ready, 5 * KC)
            pe.wait_ge(sk_in, 16)

            def wq_step(n, g=None):
                pe.wait_ge(qt_ready, up(8 + n - 1, g, 4))
                feature_tile(C_WQ + n, g, n % 2, X1H, X1L)
                pe.wait_ge(qt_ready, up(8 + n + 1, g, 4))
                if g is not None or n >= 2:
                    pe.wait_ge(sc_ready, up(n - 1, g, 4))
                for t in range(NT):
                    mm = pe.matmul(ps[:, 2 + n % 2, t * P:(t + 1) * P], qt[:, n % 2, t * P:(t + 1) * P],
                                   sk[:, n % 2, :], start=True, stop=True)
                mm.then_inc(sc_mm, 1)

            for n in range(4):
                wq_step(n)
            with pe.Fori(1, 4) as g:
                for n in range(4):
                    wq_step(n, g)
            pe.wait_ge(lists_ready, 1)
            pe.wait_ge(act_link, 7)
            for i, src in enumerate((best, i1, i2)):
                for t in range(NT):
                    mm = pe.transpose(ps[:, 4 + i, t * P:(t + 1) * P],
                                      src[:, t * PH:(t + 1) * PH, :].rearrange("p h k -> p (h k)"), ident)
            mm.then_inc(lt_mm, 1)

            def eight_step(e, g=None):
                for n in range(8):
                    half, k = n // 4, n % 4
                    if k == 0:
                        if g is not None:
                            pe.wait_ge(gate_out, up(2 * e + half - 3, g, 4))
                        pe.wait_ge(hot2_ready[half], up(e + 1, g, 2))
                    pe.wait_ge(hot_ready, up(8 * e + n + 1, g, 16))
                    pe.matmul(ps[:, 2 * e + half, k * P:(k + 1) * P], O1[:, n, :], O2[half][:, e, k, :],
                              start=True, stop=True).then_inc(gate_mm, 1)

            rounds(pe, eight_step)

            def down(j, c, g=None, first=False, last=False):
                pe.wait_ge(l_done, up(c + 1, g, RING))
                pe.wait_ge(wl_ready, up(j + 1, g, 2))
                slot = c % RING
                for t in range(NT):
                    ts_ = slice(t * P, (t + 1) * P)
                    for h in range(2):
                        hs = slice(h * 512, (h + 1) * 512)
                        for i, (a, b) in enumerate(((wvH, WH), (wvH, WL), (wvL, WH))):
                            mm = pe.matmul(ps[:, 4 + 2 * t + h, :], a[:, j % 2, ts_], b[:, slot, hs],
                                           start=(first and i == 0), stop=(last and i == 2),
                                           skip_group_check=True)
                mm.then_inc(chunk_done, 1)

            def up_tile(j, c, g=None):
                if g is not None or j >= 2:
                    pe.wait_ge(gelu_ready, up(j - 1, g, 2))
                feature_tile(c, g, j % 2, X1H, X1L)

            pe.wait_ge(gate_out, T // 4)
            pe.wait_ge(lt_ready, 3)
            up_tile(0, C_UV)
            up_tile(1, C_UV + 1)
            down(0, C_UV + 2, first=True)
            with pe.Fori(0, (NK - 2) // 2) as g:
                for j in (1, 2):
                    up_tile(j + 1, C_UV + 1 + 2 * j, g)
                    down(j, C_UV + 2 + 2 * j, g)
            down(NK - 1, NCHUNK - 1, last=True)


def _constants():
    ident = np.eye(P, dtype=np.float32)
    iota = np.tile(np.arange(P, dtype=np.float32), (P, 1))
    half = HD // 2
    perm = np.zeros((P, P), np.float32)
    for f in range(P):
        if f % HD < half:
            perm[f + half, f] = -1.0
        else:
            perm[f - half, f] = 1.0
    inv = np.float32(10000.0) ** (-np.arange(0, HD, 2, dtype=np.float32) / np.float32(HD))
    ang = np.arange(T, dtype=np.float32)[:, None] * inv[None, :]
    f = np.arange(P) % half
    cosT, sinT = np.cos(ang).astype(np.float32).T[f], np.sin(ang).astype(np.float32).T[f]
    q, k = np.arange(T)[:, None], np.arange(T)[None, :]
    window = np.where((k <= q) & (k > q - 128), 0.0, NEG).astype(np.float32)
    mask = window.reshape(NT, P, T).transpose(1, 0, 2).reshape(P, NT * T)
    d = np.abs(q - k)
    count = np.zeros((T, T))
    for span, step in ((128, 1), (512, 4), (2048, 16)):
        count += (d % step == 0) & (d <= span // 2)
    slopes = 2.0 ** (-8.0 * (np.arange(8) + 1) / 8)
    logc = np.where(count > 0, np.log(np.maximum(count, 1)), NEG)
    dil = (-slopes[:, None, None] * d[None] + logc[None]).astype(np.float32)
    return np.concatenate([ident, iota], 1), np.concatenate([perm, cosT, sinT, mask], 1), dil


def _window_index():
    grid, wr, wc = 64, 4, 16
    t = np.arange(T)
    r, c = t // grid, t % grid
    c0 = np.clip(c - wc // 2, 0, grid - wc)
    dr = r[None, :] - r[:, None] + 7
    dc = c[None, :] - c[:, None] + 15
    near = (c[None, :] >= c0[:, None]) & (c[None, :] < c0[:, None] + wc)
    assert T // grid == wr
    return dr, np.clip(dc, 0, 30), near


def kernel(**inputs):
    import concourse.bacc as _bacc
    from concourse.bass_utils import run_bass_kernel_spmd as _run

    a = {k: np.asarray(v) for k, v in inputs.items()}
    cI, cB, dil = _constants()

    def tiles_of(w):
        k, n = w.shape
        return w.reshape(k // D, KC, P, n // P, P).transpose(3, 0, 2, 1, 4).reshape(-1, P, CW)

    def weave(x, y):
        return np.stack([x, y], 1).reshape(-1, P, CW)

    pair = np.arange(D).reshape(2, 8, HD).transpose(1, 0, 2).reshape(-1)
    w = a["a_w_in"][0]
    parts = [tiles_of(w[:, AW:2 * AW]), weave(tiles_of(w[:, 0:AW]), tiles_of(w[:, 2 * AW:])),
             tiles_of(a["a_w_out"][0]), tiles_of(a["w_kv"])]
    w = a["b_w_in"][0]
    parts += [weave(tiles_of(w[:, 0:D][:, pair]), tiles_of(w[:, D:][:, pair])), tiles_of(a["b_w_out"][0][pair])]
    w = tiles_of(a["w_in_2"][0])
    parts += [w[8:12], w[20:24], weave(w[0:4], w[4:8]), weave(w[12:16], w[16:20]),
              tiles_of(a["w_out_2"][0]), tiles_of(a["peer_wq_2"][0])]
    u = a["peer_u_2"][0].reshape(NK, NK, KC, P).transpose(1, 3, 2, 0).reshape(NK, P, CW)
    v = a["peer_v_2"][0].reshape(NK, NK, D).transpose(1, 0, 2)
    parts += [u[0:1], weave(u[1:], v[:-1]), v[-1:]]
    stream = np.concatenate(parts)
    assert stream.shape == (NCHUNK, P, CW)

    def cols(x):
        return x.reshape(-1, P).T

    vecs = np.concatenate([cols(x) for x in (
        a["a_norm_g"][0], a["kv_norm_g"], a["b_norm_g"][0], a["b_bq"][0][pair], a["b_kv"][0:P],
        a["norm1_g_2"][0], a["norm2_g_2"][0], a["ada_b_2"][0], a["out_norm_na_g_2"][0], a["out_norm_dil_g_2"][0],
        a["final_norm_g"])], 1)
    sinks = np.repeat(a["b_sinks"][0].reshape(2, 8).T.reshape(-1), NT)
    rows = np.concatenate([a["c_2"][0], a["a_ln_g"][0], a["a_ln_b"][0], a["a_bs"][0].reshape(-1), a["b_kv"][P:],
                           sinks, a["final_g_2"]])
    dr, dc, near = _window_index()
    na = np.where(near[None], a["na_rpb_2"][0][:, dr, dc], np.float32(NEG))
    bias = np.concatenate([na, dil]).reshape(NPAIR, 2, NT, P, T).transpose(0, 3, 1, 2, 4).reshape(NPAIR, P, 4 * T)
    def past_end(x):
        return np.concatenate([x, x[-2:]])

    arrays = {
        "stream": stream,
        "xT": a["x"][0].T.reshape(KC, P, T).transpose(1, 0, 2),
        "vecs": vecs, "cI": cI, "cB": cB, "rows": rows,
        "wsT": a["a_ws"][0].transpose(2, 0, 1),
        "adaT": past_end(a["ada_w_2"][0].T.reshape(NMOD, P, D)),
        "att_bias": past_end(bias),
        "skT": a["peer_subkeys_2"][0].transpose(2, 0, 1),
    }
    arrays = {k: np.ascontiguousarray(x) for k, x in arrays.items()}
    nc = _bacc.Bacc("TRN2", target_bir_lowering=False, num_devices=1)
    aps = [nc.dram_tensor(k, x.shape, F32, kind="ExternalInput").ap() for k, x in arrays.items()]
    spill = nc.dram_tensor("spill", [P, 3 * D], F32, kind="Internal").ap()
    out = nc.dram_tensor("out", [T, D], F32, kind="ExternalOutput").ap()
    two_block_kernel(nc, *aps, spill, out)
    got = _run(nc, [arrays], core_ids=[0]).results[0]["out"]
    return got.reshape(1, T, D)
```

```python
from contextlib import ExitStack

import numpy as np

import concourse.bass as bass
from concourse import mybir

F32 = mybir.dt.float32
F32R = mybir.dt.float32r
U32 = mybir.dt.uint32
ALU = mybir.AluOpType
ACT = mybir.ActivationFunctionType
AX_X = mybir.AxisListType.X

P = 128
T = 256
NT = T // P
D = 1024
KC = D // P
CW = KC * P
AW = 2048
AG = AW // P
HD = 64
NPAIR = 8
NMOD = 6 * D // P
NK = 128
PH = 8
TOPK = 16
NEG = -1e30
EPS_A = 1e-5
EPS_B = 1e-6

RING = 4
C_V, C_UG = 0, AG
C_AOUT = C_UG + 2 * AG
C_KV = C_AOUT + 2 * KC
C_QG = C_KV + 2
C_BOUT = C_QG + 2 * NPAIR
C_V2 = C_BOUT + KC
C_QK = C_V2 + KC
C_COUT = C_QK + 2 * NPAIR
C_WQ = C_COUT + KC
EARLY = 20
C_U = C_WQ + 2 * PH
C_V1 = C_U + EARLY
C_UV = C_V1 + EARLY
LATE = NK - EARLY
NCHUNK = C_UV + 2 * LATE
assert C_WQ % RING == 2 and EARLY % RING == 0 and C_UV % RING == 2

V_AG, V_KG, V_BG, V_BQ, V_BK, V_N1, V_N2 = 0, 8, 16, 24, 32, 33, 41
V_ADAB, V_OG = 49, 49 + NMOD
V_FG = V_OG + 8
NVEC = V_FG + 8

ROWS = [TOPK // (a + 1) for a in range(TOPK)]
STARTS = [sum(ROWS[:a]) for a in range(TOPK)]
NCAND = sum(ROWS)


class Chain:

    def __init__(self, eng, sem):
        self.eng, self.sem, self.n = eng, sem, 0

    def mark(self, ins):
        self.n += 1
        ins.then_inc(self.sem, 1)
        return self.n

    def after(self, n):
        self.eng.wait_ge(self.sem, n)

    def __call__(self, ins):
        self.after(self.mark(ins))


def up(c, g=None, per=1):
    return c if g is None else g * per + c


def tiles(view, c, g=None, per=1, width=1):
    if g is None:
        return view[:, c:c + width]
    n = view.shape[1] // per * per
    grouped = view[:, 0:n].rearrange("p (g j) n -> p g j n", j=per)
    return grouped[:, bass.ds(g + c // per, 1), c % per:c % per + width].rearrange("p a j n -> p (a j) n")


def column(view, c, g=None, per=1):
    if g is None:
        return view[:, c:c + 1]
    n = view.shape[1] // per * per
    return view[:, 0:n].rearrange("p (g j) -> p g j", j=per)[:, bass.ds(g + c // per, 1), c % per]


def two_block_kernel(nc, stream, xT, vecs, cI, cB, rows, wsT, adaT, att_bias, skT, spill, out):
    with ExitStack() as ctx:
        def sb(name, shape, dt=F32):
            return ctx.enter_context(nc.sbuf_tensor(name, shape, dt))

        def sem(name):
            return ctx.enter_context(nc.semaphore(name))

        raw = sb("raw", [P, RING, CW])
        WH = sb("WH", [P, RING, CW], F32R)
        WL = sb("WL", [P, RING, CW], F32R)
        X1H = sb("X1H", [P, KC, T], F32R)
        X1L = sb("X1L", [P, KC, T], F32R)
        idio = sb("idio", [P, 2 * P])
        ident, iota = idio[:, 0:P], idio[:, P:2 * P]
        ones = sb("ones", [P, P])
        vec = sb("vec", [P, NVEC])
        small = sb("small", [P, 168])
        tmp = [sb(f"tmp{i}", [P, T]) for i in range(6)]
        base_wv = nc.sbuf_base
        wvH = sb("wvH", [P, 2, T], F32R)
        wvL = sb("wvL", [P, 2, T], F32R)
        base = nc.sbuf_base
        W = sb("W", [P, EARLY, T])
        G = sb("G", [P, T, LATE])
        assert nc.lookup_mloc(W).addr == base and nc.lookup_mloc(wvH).addr == base_wv
        base_hot = nc.lookup_mloc(tmp[3]).addr
        free_slot = (C_V1 + 3) % RING * CW * 4
        O1 = nc.alloc_sbuf_tensor_at("O1", [P, 8, NK], F32, offset=nc.lookup_mloc(WH).addr + free_slot)
        O2 = [nc.alloc_sbuf_tensor_at("O2a", [P, 2, 4, NK], F32, offset=base_hot),
              nc.alloc_sbuf_tensor_at("O2b", [P, 2, 4, NK], F32, offset=nc.lookup_mloc(WL).addr + free_slot)]
        assert base_hot + 8 * NK * 4 <= base

        def at(name, kib, shape, dt=F32):
            off = int(kib * 1024)
            assert off + int(np.prod(shape[1:])) * 4 <= T * NK * 4, name
            return nc.alloc_sbuf_tensor_at(name, shape, dt, offset=base + off)

        x = at("x", 0, [P, KC, T])
        uR = at("uR", 8, [P, 2, T])
        X2H = at("X2H", 8, [P, KC, T], F32R)
        X2L = at("X2L", 16, [P, KC, T], F32R)
        YH = at("YH", 24, [P, AG, T], F32R)
        YL = at("YL", 40, [P, AG, T], F32R)
        ada = at("ada", 56, [P, 2, D])
        cb = at("cb", 64, [P, D])
        V = at("V", 68, [P, NT, AW])
        sq0 = at("sq0", 68, [P, KC, T])
        xg0 = at("xg0", 76, [P, KC, T])
        lng = at("lng", 84, [P, AG, P])
        lnb = at("lnb", 92, [P, AG, P])
        ws = at("ws", 100, [P, AG, P])
        bsb = at("bsb", 108, [P, AG, P])
        cBt = at("cBt", 116, [P, 9 * P])
        perm, cosT, sinT = cBt[:, 0:P], cBt[:, P:3 * P], cBt[:, 3 * P:5 * P]
        mask = cBt[:, 5 * P:9 * P]
        R = at("R", 120.5, [P, 2, T])
        nm = at("nm", 122.5, [P, T])
        nt = at("nt", 123.5, [P, T])
        vst = at("vst", 124.5, [P, NT, 8, 6])
        sinkb = at("sinkb", 125, [P, NPAIR, 4])
        bvb = at("bvb", 125.25, [P, P])
        vs = at("vs", 125.75, [P, 2, T])
        sgate = at("sgate", 68, [P, NPAIR, T])
        oT = at("oT", 68, [P, NPAIR, T])
        s = at("s", 76, [P, 4, T])
        pr = at("pr", 80, [P, 4, T])
        pT = at("pT", 84, [P, 2, 4, P])
        qs = at("qs", 88, [P, 2, T])
        qb = at("qb", 90, [P, 2, T])
        ks = at("ks", 92, [P, 2, T])
        vB = at("vB", 94, [P, NT, P])
        on = at("on", 95, [P, NT, P])
        t3 = at("t3", 96, [P, 2, T])
        gr2 = at("gr2", 98, [P, 2, T])
        th = at("th", 100, [P, 2, T])
        F = at("F", 68, [P, KC, T])
        FY = at("FY", 76, [P, KC, T])
        bias = at("bias", 100, [P, 2, 4 * T])
        vC = at("vC", 108, [P, NT, D])
        eq = at("eq", EARLY, [P, NT * PH, TOPK, NCAND])
        qt = at("qt", 68, [P, 2, T])
        sc = at("sc", 70, [P, 2, NT, NK])
        v16 = at("v16", 72, [P, NT, 2 * PH, TOPK])
        i16 = at("i16", 74, [P, NT, 2 * PH, TOPK])
        cand = at("cand", 76, [P, NT * PH, NCAND])
        cid = at("cid", 79.5, [P, NT * PH, NCAND])
        best = at("best", 83, [P, NT * PH, TOPK])
        pos = at("pos", 84, [P, NT * PH, TOPK], U32)
        posf = at("posf", 85, [P, NT * PH, TOPK])
        sid = at("sid", 86, [P, NT * PH, TOPK])
        i1 = at("i1", 87, [P, NT * PH, TOPK])
        i2 = at("i2", 88, [P, NT * PH, TOPK])
        sk = at("sk", 99, [P, 2, NK])
        sc2 = at("sc2", 90, [P, NT, NK])
        ix8 = at("ix8", 91, [P, NT, TOPK], U32)
        g2b = at("g2b", 92, [P, D])
        diags = at("diags", 100, [P, KC, P])
        zsum = at("zsum", 91.5, [P, NT * PH])
        posi = at("posi", 104, [P, NT * PH, TOPK], U32)
        xtok = at("xtok", 108, [P, NT, D])
        xt2 = at("xt2", 0, [P, NT, D])
        g2r = at("g2r", 8, [P, D])
        fgr = at("fgr", 12, [P, D])
        yo = at("yo", 16, [P, NT, D])
        sqf = at("sqf", 24, [P, NT, D])

        modT, mod = small[:, 0:NMOD], small[:, NMOD:2 * NMOD]
        s1, s2 = small[:, 96:104], small[:, 104:112]
        rtok = small[:, 112:116]
        mx, negm, dsk = small[:, 116:120], small[:, 120:124], small[:, 124:128]
        small_es = small[:, 128:136].rearrange("p (a k) -> p a k", a=2)
        small_den = small[:, 136:144].rearrange("p (a k) -> p a k", a=2)
        small_rc = small[:, 144:152].rearrange("p (a k) -> p a k", a=2)
        mv = small[:, 152:156]
        rstd, st0, st1 = small[:, 156:158], small[:, 158:160], small[:, 160:162]
        st2, fsum = small[:, 162:163], small[:, 164:166]

        ps = ctx.enter_context(nc.psum_tensor("ps", [P, 8, 512], F32))

        raw_in = [sem(f"raw_in{i}") for i in range(RING)]
        h_done, l_done, chunk_done = sem("h_done"), sem("l_done"), sem("chunk_done")
        x_in, c_in, a_in, b_in, sk_in = sem("x_in"), sem("c_in"), sem("a_in"), sem("b_in"), sem("sk_in")
        ada_in = [sem(f"ada_in{i}") for i in range(2)]
        bias_in = [sem(f"bias_in{i}") for i in range(2)]
        ada_used = sem("ada_used")
        dve_link, act_link = sem("dve_link"), sem("act_link")
        sum_ready, psn_ready, m_ready, root_ready, r_ready = (
            sem("sum_ready"), sem("psn_ready"), sem("m_ready"), sem("root_ready"), sem("r_ready"))
        rt_ready, rtok_ready = sem("rt_ready"), sem("rtok_ready")
        ones_ready, cb_ready = sem("ones_ready"), sem("cb_ready")
        sq_ready, sacc_done, x_ready = sem("sq_ready"), sem("sacc_done"), sem("x_ready")
        xg_ready, xh_ready, xl_ready = sem("xg_ready"), sem("xh_ready"), sem("xl_ready")
        yf_ready, yh_ready, yl_ready = sem("yf_ready"), sem("yh_ready"), sem("yl_ready")
        v_out, st_done = sem("v_out"), sem("st_done")
        ln_m, ln_root, xhat_ready = sem("ln_m"), sem("ln_root"), sem("xhat_ready")
        ws_ready, vs_ready, sv_mm = sem("ws_ready"), sem("vs_ready"), sem("sv_mm")
        ur_ready, th_ready = sem("ur_ready"), sem("th_ready")
        gr_ready, sg_ready, svb_ready = sem("gr_ready"), sem("sg_ready"), sem("svb_ready")
        k_ready, v_ready = sem("k_ready"), sem("v_ready")
        qb_ready, rope_mm, rope_s, rope_c, q_ready = (
            sem("qb_ready"), sem("rope_mm"), sem("rope_s"), sem("rope_c"), sem("q_ready"))
        s_mm, s_ready, mx_ready, negm_ready, dsk_ready = (
            sem("s_mm"), sem("s_ready"), sem("mx_ready"), sem("negm_ready"), sem("dsk_ready"))
        p_ready, es_ready, den_ready, rc_ready = sem("p_ready"), sem("es_ready"), sem("den_ready"), sem("rc_ready")
        pt_mm, pt_ready, o_mm, on_ready, ot_mm, ot_done = (
            sem("pt_mm"), sem("pt_ready"), sem("o_mm"), sem("on_ready"), sem("ot_mm"), sem("ot_done"))
        gate_ready = sem("gate_ready")
        qt_ready, sc_mm, sc_ready, sc_used = sem("qt_ready"), sem("sc_mm"), sem("sc_ready"), sem("sc_used")
        tr_mm, spill_done = sem("tr_mm"), sem("spill_done")
        lists_ready, lt_mm, lt_ready, exp_in, exp_ready = (
            sem("lists_ready"), sem("lt_mm"), sem("lt_ready"), sem("exp_in"), sem("exp_ready"))
        hot2_ready = [sem(f"hot2_ready{i}") for i in range(2)]
        gm_ready = sem("gm_ready")
        dist_ready, dist2_ready = sem("dist_ready"), sem("dist2_ready")
        hot_ready, gate_mm, gate_out = sem("hot_ready"), sem("gate_mm"), sem("gate_out")
        gelu_ready, w_ready, wh_ready, wl_ready = (
            sem("gelu_ready"), sem("w_ready"), sem("wh_ready"), sem("wl_ready"))
        fin_in, fy_ready, fsum_ready, out_ready, out_done = (
            sem("fin_in"), sem("fy_ready"), sem("fsum_ready"), sem("out_ready"), sem("out_done"))

        ada_sum, ln_r, t_ready, mxs_ready, mt_ready = (
            sem("ada_sum"), sem("ln_r"), sem("t_ready"), sem("mxs_ready"), sem("mt_ready"))
        vg_ready, mg_ready, acc_clear, diag_ready = (
            sem("vg_ready"), sem("mg_ready"), sem("acc_clear"), sem("diag_ready"))

        block = ctx.enter_context(nc.Block())

        @block.sync
        def _(sp):
            def load(c, g=None, group=None, j=0):
                if g is not None or c >= RING:
                    sp.wait_ge(l_done, up(c - RING + 1, g, RING))
                slot = c % RING
                if g is None:
                    sp.dma_start(raw[:, slot, :], stream[c]).then_inc(raw_in[slot], 16)
                else:
                    sp.dma_start(raw[:, slot:slot + 1, :], group[j][:, bass.ds(g, 1), :]).then_inc(raw_in[slot], 16)

            def groups(c, n):
                return stream[c:c + RING * n].rearrange("(g j) p n -> j p g n", j=RING)

            def row(lo, n):
                return rows[lo:lo + n].partition_broadcast(P)

            sp.dma_start(x[:, :, :], xT).then_inc(x_in, 16)
            sp.dma_start(vec[:, :], vecs).then_inc(x_in, 16)
            load(0)
            load(1)
            sp.dma_start(idio[:, :], cI).then_inc(c_in, 16)
            sp.dma_start(cb[:, :], row(0, D)).then_inc(c_in, 16)
            load(2)
            load(3)
            sp.dma_start(ada[:, 0, :], adaT[0]).then_inc(ada_in[0], 16)
            later = ([(ws[:, :, :], wsT, a_in)], [(lng[:, :, :].rearrange("p g n -> p (g n)"), row(D, AW), a_in)],
                     [(lnb[:, :, :].rearrange("p g n -> p (g n)"), row(D + AW, AW), a_in)],
                     [(bsb[:, :, :].rearrange("p g n -> p (g n)"), row(D + 2 * AW, AW), a_in)],
                     [(cBt[:, :], cB, b_in), (bvb[:, :], row(D + 3 * AW, P), b_in),
                      (sinkb[:, :, :].rearrange("p m k -> p (m k)"), row(D + 3 * AW + P, 32), b_in)])
            for k, loads in enumerate(later):
                for j in range(RING):
                    load(RING * (k + 1) + j)
                    if j == 1:
                        for dst, src, done in loads:
                            sp.dma_start(dst, src).then_inc(done, 16)
            first = len(later) + 1
            rounds = NCHUNK // RING
            cs = groups(RING * first, rounds - first)
            with sp.Fori(0, rounds - first) as g:
                for j in range(RING):
                    load(RING * first + j, g, cs, j)
            for c in range(RING * rounds, NCHUNK):
                load(c)
            sp.wait_ge(w_ready, LATE)
            sp.wait_ge(spill_done, 32)
            sp.dma_start(xt2[:, :, :].rearrange("p t n -> p (t n)"), spill[:, 0:NT * D]).then_inc(fin_in, 16)
            sp.dma_start(g2r[:, :], spill[:, NT * D:NT * D + D]).then_inc(fin_in, 16)
            sp.dma_start(fgr[:, :], row(D + 3 * AW + P + 32, D)).then_inc(fin_in, 16)
            for t in range(NT):
                sp.wait_ge(out_ready, t + 1)
                sp.dma_start(out[t * P:(t + 1) * P, :], yo[:, t, :]).then_inc(out_done, 16)
            sp.wait_ge(out_done, 16 * NT)

        def fours(eng, n, step):
            for j in range(4):
                step(j)
            with eng.Fori(1, n // 4) as g:
                for j in range(4):
                    step(j, g)

        def hot2_in(e, half, g=None):
            i2s = tmp[2][:, :].rearrange("p (g j) -> p g j", j=4)
            k = 2 * e + half
            i2s = i2s[:, k] if g is None else \
                i2s.rearrange("p (g k) j -> p k g j", k=4)[:, k, bass.ds(g, 1), :].rearrange("p a j -> p (a j)")
            return iota.unsqueeze(1).broadcast_to([P, 4, NK]), i2s.unsqueeze(2).broadcast_to([P, 4, NK])

        def rounds(eng, step):
            step(0)
            step(1)
            with eng.Fori(1, T // 16) as g:
                step(0, g)
                step(1, g)

        @block.scalar
        def _(act):
            link = Chain(act, act_link)
            ada_pairs = adaT.rearrange("(g j) p n -> j p g n", j=2)
            bias_pairs = att_bias.rearrange("(g j) p n -> j p g n", j=2)

            def load_ada(n, g=None):
                act.wait_ge(ada_used, up(n - 1, g, 2))
                src = adaT[n:n + 1].rearrange("a p n -> p a n") if g is None else ada_pairs[n % 2][:, bass.ds(g + n // 2, 1), :]
                act.dma_start(ada[:, n % 2:n % 2 + 1, :], src).then_inc(ada_in[n % 2], 16)

            def load_bias(m, g=None):
                act.wait_ge(s_ready, up(8 + m - 1, g, 2))
                src = att_bias[m:m + 1].rearrange("a p n -> p a n") if g is None else bias_pairs[m % 2][:, bass.ds(g + m // 2, 1), :]
                act.dma_start(bias[:, m % 2:m % 2 + 1, :], src).then_inc(bias_in[m % 2], 16)

            def hi(c, g=None):
                slot = c % RING
                act.wait_ge(raw_in[slot], up((c // RING + 1) * 16, g, 16))
                if g is not None or c >= RING:
                    act.wait_ge(chunk_done, up(c - RING + 1, g, RING))
                act.activation(WH[:, slot, :], raw[:, slot, :], ACT.Copy).then_inc(h_done, 1)

            def root(k):
                act.wait_ge(m_ready, k + 1)
                act.activation(nt[:, :], nm[:, :], ACT.Sqrt).then_inc(root_ready, 1)

            act.wait_ge(x_in, 32)
            act.activation(sq0[:, :, :], x[:, :, :], ACT.Square).then_inc(sq_ready, 1)
            for kc in range(KC):
                act.wait_ge(xg_ready, kc + 1)
                act.activation(X1H[:, kc, :], xg0[:, kc, :], ACT.Copy).then_inc(xh_ready, 1)
            for c in range(RING):
                hi(c)
            root(0)
            act.wait_ge(c_in, 32)
            act.activation(cb[:, :], cb[:, :], ACT.Silu).then_inc(cb_ready, 1)

            def v_step(q, g=None):
                if g is not None or q >= 1:
                    hi(2 * q + 3, g)
                act.wait_ge(chunk_done, up(2 * q + 2, g, 4))
                act.wait_ge(rtok_ready, 1)
                for t in range(NT):
                    act.activation(tiles(V[:, t, :].rearrange("p (q n) -> p q n", n=T), q, g, 2),
                                   ps[:, q % 2 * 2 + t:q % 2 * 2 + t + 1, 0:T], ACT.Copy,
                                   scale=rtok[:, t:t + 1]).then_inc(v_out, 1)
                if g is None and q == 0:
                    act.dma_start(ada[:, 1, :], adaT[1]).then_inc(ada_in[1], 16)
                else:
                    load_ada(q + 1, g)
                hi(2 * q + 4, g)

            for q in range(2):
                v_step(q)
            with act.Fori(1, 4) as g:
                for q in range(2):
                    v_step(q, g)
            act.wait_ge(ln_m, 1)
            act.activation(st1, st0, ACT.Sqrt).then_inc(ln_root, 1)
            act.activation(small[:, 166:167], vec[:, 0:1], ACT.Silu).then_inc(act_link, 1)

            def y_high(n, g=None):
                act.wait_ge(yf_ready, up(n + 1, g, 2))
                act.activation(tiles(YH, n, g, 2), tmp[4 + n % 2][:, :].unsqueeze(1), ACT.Copy).then_inc(yh_ready, 1)

            def ug_step(n, g=None):
                hi(C_UG + 3 + 2 * n, g)
                hi(C_UG + 4 + 2 * n, g)
                load_ada(9 + n, g)
                if g is not None or n >= 1:
                    y_high(n - 1, g)
                act.wait_ge(gr_ready, up(n + 1, g, 2))
                act.activation(tmp[n % 2][:, :], tmp[n % 2][:, :], ACT.Silu).then_inc(sg_ready, 1)

            for n in range(2):
                ug_step(n)
            with act.Fori(1, AG // 2) as g:
                for n in range(2):
                    ug_step(n, g)
            y_high(AG - 1)

            def sq_gained(n, g=None):
                act.wait_ge(x_ready, up(8 + n + 1, g, 4))
                act.wait_ge(sacc_done, up(8 + 2 * n - 1, g, 8))
                act.activation(tmp[4][:, :].unsqueeze(1), tiles(x, n, g, 4), ACT.Square).then_inc(sq_ready, 1)
                act.wait_ge(sacc_done, up(8 + 2 * n, g, 8))
                act.activation(tmp[3][:, :].unsqueeze(1), tiles(x, n, g, 4), ACT.Square,
                               scale=column(vec[:, V_FG:V_FG + 8], n, g, 4)).then_inc(sq_ready, 1)

            def sq_tile(k, src, ready, value, n, g, per):
                act.wait_ge(ready, up(value, g, per))
                if g is not None or k >= 1:
                    act.wait_ge(sacc_done, up(k, g, per))
                act.activation(tmp[4][:, :].unsqueeze(1), tiles(src, n, g, per), ACT.Square).then_inc(sq_ready, 1)

            def aout_after(n, g=None):
                for i, XH in enumerate((X1H, X2H)):
                    act.wait_ge(xg_ready, up(KC + 2 * n + i + 1, g, 4))
                    act.activation(tiles(XH, n, g, 2), tmp[2 * i + n % 2][:, :].unsqueeze(1),
                                   ACT.Copy).then_inc(xh_ready, 1)
                sq_tile(n, x, x_ready, n + 1, n, g, 2)

            def aout_step(n, g=None):
                hi(C_AOUT + 3 + 2 * n, g)
                load_ada(25 + n, g)
                hi(C_AOUT + 4 + 2 * n, g)
                if g is not None or n >= 1:
                    aout_after(n - 1, g)

            for n in range(2):
                aout_step(n)
            with act.Fori(1, 4) as g:
                for n in range(2):
                    aout_step(n, g)
            aout_after(KC - 1)
            hi(C_KV + 3)
            root(1)
            hi(C_KV + 4)

            def exps(p, g, sinks):
                par = p % 2
                act.wait_ge(dsk_ready if sinks else negm_ready, up(p + 1, g, 2))
                if g is not None or p >= 1:
                    act.wait_ge(pt_mm, up(p, g, 2))
                if g is not None or p >= 2:
                    act.wait_ge(rc_ready, up(p - 1, g, 2))
                for k in range(4):
                    act.activation(pr[:, k, :], s[:, k, :], ACT.Exp, bias=negm[:, k:k + 1],
                                   accum_out=small_den[:, par, k:k + 1]).then_inc(p_ready, 1)
                if sinks:
                    act.activation(small_es[:, par, :], dsk, ACT.Exp).then_inc(es_ready, 1)

            def pt_out(p, g):
                act.wait_ge(pt_mm, up(p + 1, g, 2))
                if g is not None or p >= 1:
                    act.wait_ge(o_mm, up(p, g, 2))
                for h in range(2):
                    act.activation(pT[:, h, :, :].rearrange("p k t -> p (k t)"), ps[:, 6 + h, :],
                                   ACT.Copy).then_inc(pt_ready, 1)

            def swa_step(m, g=None):
                if m < 8:
                    hi(C_QG + 3 + 2 * m, g)
                    hi(C_QG + 4 + 2 * m, g)
                if g is not None or m >= 3:
                    act.wait_ge(yf_ready, up(AG + m - 2, g, 2))
                    act.activation(tiles(YH, m - 3, g, 2), tmp[4 + (m + 1) % 2][:, :].unsqueeze(1),
                                   ACT.Copy).then_inc(yh_ready, 1)
                if 1 <= m <= 8:
                    exps(m - 1, g, True)
                if m < 8:
                    load_ada(33 + m, g)
                    act.wait_ge(gr_ready, up(AG + m + 1, g, 2))
                    if g is not None or m >= 2:
                        act.wait_ge(th_ready, up(m - 1, g, 2))
                    act.activation(th[:, m % 2, :], gr2[:, m % 2, :], ACT.Tanh).then_inc(gate_ready, 1)
                if 1 <= m <= 8:
                    pt_out(m - 1, g)

            def steps(eng, step):
                for m in range(4):
                    step(m)
                with eng.Fori(1, 3) as g:
                    step(2, g)
                    step(3, g)
                for m in range(8, 11):
                    step(m)

            steps(act, swa_step)

            def bout_step(n, g=None):
                hi(C_BOUT + 3 + n, g)
                if g is not None or n >= 1:
                    sq_gained(n - 1, g)

            for n in range(4):
                bout_step(n)
            with act.Fori(1, 2) as g:
                for n in range(4):
                    bout_step(n, g)
            sq_gained(KC - 1)
            root(2)
            root(3)

            def x1_high(n0):
                for kc in range(KC):
                    act.wait_ge(xg_ready, n0 + kc + 1)
                    act.activation(X1H[:, kc, :], F[:, kc, :], ACT.Copy).then_inc(xh_ready, 1)

            x1_high(3 * KC)

            act.wait_ge(th_ready, NPAIR)
            for m in range(2):
                act.dma_start(bias[:, m:m + 1, :], att_bias[m:m + 1].rearrange("a p n -> p a n")).then_inc(bias_in[m], 16)
            act.dma_start(sk[:, :, :], skT).then_inc(sk_in, 16)

            def v2_step(q, g):
                hi(C_V2 + 2 * q + 3, g)
                act.wait_ge(chunk_done, up(C_V2 + 2 * q + 2, g, 4))
                for t in range(NT):
                    act.activation(tiles(vC[:, t, :].rearrange("p (q n) -> p q n", n=T), q, g, 2),
                                   ps[:, q % 2 * 2 + t:q % 2 * 2 + t + 1, 0:T], ACT.Copy).then_inc(v_out, 1)
                hi(C_V2 + 2 * q + 4, g)

            with act.Fori(0, 2) as g:
                for q in range(2):
                    v2_step(q, g)

            def mix_step(m, g=None):
                if m < 8:
                    hi(C_QK + 2 * m + 3, g)
                    act.wait_ge(chunk_done, up(C_QK + 2 * m + 1, g, 4))
                    act.wait_ge(s_mm, up(8 + m - 1, g, 2))
                    act.activation(qs[:, m % 2, :], ps[:, m % 2, 0:T], ACT.Copy).then_inc(qt_ready, 1)
                    hi(C_QK + 2 * m + 4, g)
                if g is not None or m >= 3:
                    sq_tile(24 + m - 3, oT, ot_done, m - 2, m - 3, g, 2)
                if 1 <= m <= 8:
                    exps(8 + m - 1, g, False)
                if m < 8:
                    load_ada(41 + m, g)
                if 1 <= m <= 8:
                    pt_out(8 + m - 1, g)
                    if m < 8:
                        load_bias(m + 1, g)

            steps(act, mix_step)

            def norm_high(k):
                for n in range(4 * k, 4 * k + 4):
                    act.wait_ge(yf_ready, AG + 8 + n + 1)
                    act.activation(YH[:, n, :], FY[:, n, :], ACT.Copy).then_inc(yh_ready, 1)

            root(4)
            norm_high(0)
            root(5)
            norm_high(1)

            def cout_square(n, g=None):
                sq_tile(32 + n, x, x_ready, 24 + n + 1, n, g, 4)

            def cout_step(n, g=None):
                hi(C_COUT + 3 + n, g)
                if g is not None or n >= 1:
                    cout_square(n - 1, g)

            for n in range(4):
                cout_step(n)
            with act.Fori(1, 2) as g:
                for n in range(4):
                    cout_step(n, g)
            cout_square(KC - 1)
            root(6)
            x1_high(4 * KC)
            act.wait_ge(tr_mm, 1)
            act.wait_ge(act_link, 1)
            link.n = 1
            for i in range(4):
                link(act.activation(xtok[:, i // 2, i % 2 * 512:i % 2 * 512 + 512], ps[:, 4 + i, :], ACT.Copy))
            act.dma_start(spill[:, 0:NT * D], xtok[:, :, :].rearrange("p t n -> p (t n)")).then_inc(spill_done, 16)
            act.wait_ge(tr_mm, 2)
            for i in range(2):
                link(act.activation(g2b[:, i * 512:i * 512 + 512], ps[:, 2 + i, :], ACT.Copy))
            act.dma_start(spill[:, NT * D:NT * D + D], g2b[:, :]).then_inc(spill_done, 16)

            def wq_step(n, g=None):
                hi(C_WQ + 3 + n, g)
                act.wait_ge(chunk_done, up(C_WQ + 1 + n, g, 4))
                if g is not None or n >= 2:
                    act.wait_ge(sc_mm, up(n - 1, g, 4))
                act.activation(qt[:, n % 2, :], ps[:, n % 2, 0:T], ACT.Copy).then_inc(qt_ready, 1)
                act.wait_ge(sc_mm, up(n + 1, g, 4))
                if g is not None or n >= 2:
                    act.wait_ge(sc_used, up(n - 1, g, 4))
                act.activation(sc[:, n % 2, :, :].rearrange("p t n -> p (t n)"), ps[:, 2 + n % 2, 0:T],
                               ACT.Copy).then_inc(sc_ready, 1)

            for n in range(4):
                wq_step(n)
            with act.Fori(1, 4) as g:
                for n in range(4):
                    wq_step(n, g)
            def early_step(j, g=None):
                hi(C_U + 3 + j, g)
                act.wait_ge(chunk_done, up(C_U + j + 1, g, 4))
                act.activation(tiles(W, j, g, 4), ps[:, j % 2:j % 2 + 1, 0:T], ACT.Gelu).then_inc(gelu_ready, 1)

            fours(act, EARLY, early_step)
            act.wait_ge(exp_in, 1)
            act.activation(best[:, :, :], best[:, :, :], ACT.Exp).then_inc(exp_ready, 1)
            act.wait_ge(lt_mm, 1)
            for i in range(3):
                act.activation(tmp[i][:, :], ps[:, 4 + i, 0:T], ACT.Copy).then_inc(lt_ready, 1)
            act.wait_ge(spill_done, 32)

            def eight_step(e, g=None):
                o = O2[1][:, e, :, :].rearrange("p k n -> p (k n)")
                act.wait_ge(dist_ready, up(e + 1, g, 2))
                act.activation(o, o, ACT.Square).then_inc(dist2_ready, 1)
                act.wait_ge(dist2_ready, up(e + 1, g, 2))
                act.activation(o, o, ACT.Relu, bias=ones[:, 0:1], scale=-1.0).then_inc(hot2_ready[1], 1)
                if g is not None or e >= 1:
                    gates_out(e - 1, g)

            def gates_out(e, g=None):
                for n in range(2):
                    act.wait_ge(gate_mm, up(8 * e + 4 * n + 4, g, 16))
                    late = tiles(G[:, :, :].rearrange("p (q t) n -> p q (t n)", t=4), 2 * e + n, g, 4)
                    act.activation(late.rearrange("p a (t n) -> p (a t) n", t=4),
                                   ps[:, 2 * (e % 2) + n, :].rearrange("p (t n) -> p t n", t=4)[:, :, EARLY:NK],
                                   ACT.Copy).then_inc(gate_out, 1)

            rounds(act, eight_step)
            gates_out(T // 8 - 1)

            act.wait_ge(gm_ready, T // 8)

            def early_down(j, g=None):
                if g is not None or j >= 2:
                    act.wait_ge(chunk_done, up(C_V1 + j - 1, g, 4))
                act.activation(wvH[:, j % 2:j % 2 + 1, :], tiles(W, j, g, 4), ACT.Copy).then_inc(wh_ready, 1)
                hi(C_V1 + 3 + j, g)

            fours(act, EARLY, early_down)

            def gelu(i, g=None):
                act.wait_ge(chunk_done, C_UV + 1 if g is None and i == 0 else up(C_UV + 2 * i, g, 4))
                if g is not None or i >= 2:
                    act.wait_ge(wl_ready, up(EARLY + i - 1, g, 2))
                act.activation(tmp[i % 2][:, :], ps[:, i % 2, 0:T], ACT.Gelu).then_inc(gelu_ready, 1)

            def w_high(i, g=None):
                act.wait_ge(w_ready, up(i + 1, g, 2))
                act.wait_ge(chunk_done, up(C_UV + 2 * i - 1, g, 4))
                act.activation(wvH[:, i % 2, :], tmp[2 + i % 2][:, :], ACT.Copy).then_inc(wh_ready, 1)

            hi(C_UV + 3)
            gelu(0)
            w_high(0)
            hi(C_UV + 4)
            hi(C_UV + 5)

            def column_step(i, g=None):
                gelu(i, g)
                w_high(i, g)
                hi(C_UV + 4 + 2 * i, g)
                hi(C_UV + 5 + 2 * i, g)

            column_step(1)
            column_step(2)
            with act.Fori(1, (LATE - 4) // 2) as g:
                column_step(1, g)
                column_step(2, g)
            column_step(LATE - 3)
            for i in (LATE - 2, LATE - 1):
                gelu(i)
                w_high(i)
            for t in range(NT):
                act.wait_ge(fy_ready, t + 1)
                act.activation(sqf[:, t, :], yo[:, t, :], ACT.Square, accum_out=fsum[:, t:t + 1]).then_inc(fsum_ready, 1)
            act.wait_ge(ln_m, 2)
            act.activation(st1, st0, ACT.Sqrt).then_inc(ln_root, 1)

        @block.vector
        def _(dve):
            link = Chain(dve, dve_link)

            def lo(c, g=None):
                slot = c % RING
                dve.wait_ge(h_done, up(c + 1, g, RING))
                if g is not None or c >= RING:
                    dve.wait_ge(chunk_done, up(c - RING + 1, g, RING))
                dve.tensor_tensor(WL[:, slot, :], raw[:, slot, :], WH[:, slot, :].bitcast(F32),
                                  ALU.subtract).then_inc(l_done, 1)

            def ada_tile(n, g=None):
                dve.wait_ge(ada_in[n % 2], up((n // 2 + 1) * 16, g, 16))
                if g is not None or n >= 1:
                    dve.wait_ge(ada_used, up(n, g, 2))
                dve.tensor_tensor_reduce(ada[:, n % 2, :], ada[:, n % 2, :], cb[:, :], 1.0, 0.0,
                                         ALU.mult, ALU.add, st2).then_inc(ada_sum, 1)
                dve.wait_ge(ada_sum, up(n + 1, g, 2))
                dve.tensor_copy(column(modT, n, g, 2), st2).then_inc(ada_used, 1)

            def newton(y, m, t, last):
                link(dve.tensor_tensor(t, y, y, ALU.mult))
                link(dve.tensor_tensor(t, t, m, ALU.mult))
                link(dve.tensor_scalar(t, t, -0.5, 1.5, ALU.mult, ALU.add))
                dve.tensor_tensor(y, y, t, ALU.mult).then_inc(last, 1)

            def rms(k, width, eps, sums):
                dve.wait_ge(psn_ready, k + 1)
                dve.tensor_scalar(nm[:, :], sums, 1.0 / width, eps, ALU.mult, ALU.add).then_inc(m_ready, 1)
                dve.wait_ge(root_ready, k + 1)
                link(dve.reciprocal(R[:, k % 2, :], nt[:, :]))
                newton(R[:, k % 2, :], nm[:, :], nt[:, :], r_ready)
                dve.wait_ge(r_ready, k + 1)

            def rms_tokens(k):
                dve.wait_ge(rt_ready, k + 1)
                dve.tensor_copy(rtok[:, 2 * k:2 * k + 2],
                                ps[:, 7, T:2 * T].rearrange("p (t c) -> p t c", c=P)[:, :, 0]).then_inc(rtok_ready, 1)

            dve.memset(ones[:, :], 1.0).then_inc(ones_ready, 1)
            dve.wait_ge(x_in, 32)
            for kc in range(KC):
                dve.tensor_scalar(xg0[:, kc, :], x[:, kc, :], vec[:, V_AG + kc:V_AG + kc + 1], None,
                                  ALU.mult).then_inc(xg_ready, 1)
            dve.wait_ge(sq_ready, 1)
            dve.tensor_reduce(tmp[5][:, :], sq0[:, :, :].rearrange("p k t -> p t k"), AX_X, ALU.add).then_inc(sum_ready, 1)
            for kc in range(KC):
                dve.wait_ge(xh_ready, kc + 1)
                dve.tensor_tensor(X1L[:, kc, :], xg0[:, kc, :], X1H[:, kc, :].bitcast(F32),
                                  ALU.subtract).then_inc(xl_ready, 1)
            for c in range(RING):
                lo(c)
            rms(0, D, EPS_A, ps[:, 7, 0:T])
            dve.wait_ge(cb_ready, 1)

            def v_step(q, g=None):
                if g is not None or q >= 1:
                    lo(2 * q + 3, g)
                ada_tile(q, g)
                if g is None and q == 0:
                    rms_tokens(0)
                lo(2 * q + 4, g)
                for t in range(NT):
                    dve.wait_ge(v_out, up(2 * q + t + 1, g, 4))
                    dve.bn_stats(tiles(vst[:, t, :, :], q, g, 2),
                                 tiles(V[:, t, :].rearrange("p (q n) -> p q n", n=T), q, g, 2)).then_inc(st_done, 1)

            for q in range(2):
                v_step(q)
            with dve.Fori(1, 4) as g:
                for q in range(2):
                    v_step(q, g)
            dve.wait_ge(st_done, 16)
            for t in range(NT):
                link(dve.bn_aggr(mv[:, 2 * t:2 * t + 2], vst[:, t, :, :]))
            dve.tensor_scalar(st0, mv[:, 1:4:2], 1.0, EPS_A, ALU.mult, ALU.add).then_inc(ln_m, 1)
            dve.wait_ge(ln_root, 1)
            link(dve.reciprocal(rstd, st1))
            newton(rstd, st0, st1, ln_r)
            dve.wait_ge(ln_r, 1)
            for t in range(NT):
                dve.tensor_scalar(V[:, t, :], V[:, t, :], mv[:, 2 * t:2 * t + 1], rstd[:, t:t + 1],
                                  ALU.subtract, ALU.mult).then_inc(xhat_ready, 1)

            def y_low(n, count, src, g, per):
                dve.wait_ge(yh_ready, up(count + 1, g, per))
                dve.tensor_tensor(tiles(YL, n, g, per), src, tiles(YH, n, g, per).bitcast(F32),
                                  ALU.subtract).then_inc(yl_ready, 1)

            def ug_step(n, g=None):
                lo(C_UG + 3 + 2 * n, g)
                dve.wait_ge(chunk_done, up(C_UG + 1 + 2 * n, g, 4))
                if g is not None or n >= 2:
                    dve.wait_ge(yf_ready, up(n - 1, g, 2))
                dve.tensor_tensor(uR[:, n % 2, :], ps[:, n % 2, 0:T], R[:, 0, :], ALU.mult).then_inc(ur_ready, 1)
                lo(C_UG + 4 + 2 * n, g)
                dve.wait_ge(chunk_done, up(C_UG + 2 + 2 * n, g, 4))
                dve.tensor_tensor(tmp[n % 2][:, :], ps[:, 2 + n % 2, 0:T], R[:, 0, :], ALU.mult).then_inc(gr_ready, 1)
                dve.wait_ge(sv_mm, up(n + 1, g, 2))
                dve.tensor_tensor(tmp[2 + n % 2][:, :].rearrange("p (c t) -> p c t", c=NT),
                                  ps[:, 4 + n % 2, 0:T].rearrange("p (c t) -> p c t", c=NT),
                                  tiles(bsb, n, g, 2).broadcast_to([P, NT, P]), ALU.add).then_inc(svb_ready, 1)
                ada_tile(8 + n, g)
                if g is not None or n >= 1:
                    y_low(n - 1, n - 1, tmp[4 + (n - 1) % 2][:, :].unsqueeze(1), g, 2)

            for n in range(2):
                ug_step(n)
            with dve.Fori(1, AG // 2) as g:
                for n in range(2):
                    ug_step(n, g)
            y_low(AG - 1, AG - 1, tmp[5][:, :].unsqueeze(1), None, 2)

            def x_low(XL, XH, n, count, src, g, per, cper):
                dve.wait_ge(xh_ready, up(count + 1, g, cper))
                dve.tensor_tensor(tiles(XL, n, g, per), src, tiles(XH, n, g, per).bitcast(F32),
                                  ALU.subtract).then_inc(xl_ready, 1)

            def aout_low(n, g=None):
                for i, (XH, XL) in enumerate(((X1H, X1L), (X2H, X2L))):
                    x_low(XL, XH, n, KC + 2 * n + i, tmp[2 * i + n % 2][:, :].unsqueeze(1), g, 2, 4)

            def aout_step(n, g=None):
                lo(C_AOUT + 3 + 2 * n, g)
                lo(C_AOUT + 4 + 2 * n, g)
                dve.wait_ge(chunk_done, up(C_AOUT + 2 + 2 * n, g, 4))
                dve.tensor_tensor(tiles(x, n, g, 2), tiles(x, n, g, 2), ps[:, n % 2:n % 2 + 1, 0:T],
                                  ALU.add).then_inc(x_ready, 1)
                ada_tile(24 + n, g)
                dve.wait_ge(x_ready, up(n + 1, g, 2))
                for i, gain in enumerate((V_KG, V_BG)):
                    dve.tensor_scalar(tmp[2 * i + n % 2][:, :].unsqueeze(1), tiles(x, n, g, 2),
                                      column(vec[:, gain:gain + 8], n, g, 2), None, ALU.mult).then_inc(xg_ready, 1)
                if g is not None or n >= 1:
                    aout_low(n - 1, g)

            for n in range(2):
                aout_step(n)
            with dve.Fori(1, 4) as g:
                for n in range(2):
                    aout_step(n, g)
            aout_low(KC - 1)
            dve.wait_ge(ada_used, 32)
            link(dve.tensor_tensor(mod[:, 0:32], modT[:, 0:32], vec[:, V_ADAB:V_ADAB + 32], ALU.add))
            link(dve.tensor_scalar(s1, mod[:, 8:16], 1.0, None, ALU.add))
            link(dve.tensor_tensor(s1, s1, vec[:, V_N1:V_N1 + 8], ALU.mult))
            lo(C_KV + 3)
            rms(1, D, EPS_A, ps[:, 7, 0:T])

            def rope_in(i, bank, bcol, g=None):
                dve.tensor_tensor(tmp[0][:, :], ps[:, bank, 0:T], R[:, 1, :], ALU.mult).then_inc(t_ready, 1)
                dve.wait_ge(t_ready, up(i + 1, g, 2))
                if g is not None or i >= 2:
                    dve.wait_ge(q_ready, up(i - 1, g, 2))
                dve.tensor_scalar(qb[:, i % 2, :], tmp[0][:, :], bcol, None, ALU.add).then_inc(qb_ready, 1)

            def rope_out(i, bank, g=None):
                dve.wait_ge(rope_mm, up(i + 1, g, 2))
                if g is not None or i >= 2:
                    dve.wait_ge(q_ready, up(i - 1, g, 2))
                dve.tensor_tensor(tmp[2 + i % 2][:, :], ps[:, bank, T:2 * T], sinT, ALU.mult).then_inc(rope_s, 1)

            dve.wait_ge(b_in, 48)
            dve.wait_ge(chunk_done, C_KV + 1)
            rope_in(0, 6, vec[:, V_BK:V_BK + 1])
            lo(C_KV + 4)
            rope_out(0, 6)
            rms_tokens(1)
            dve.wait_ge(rtok_ready, 2)
            dve.wait_ge(chunk_done, C_KV + 2)
            for t in range(NT):
                dve.scalar_tensor_tensor(out=vB[:, t, :], in0=ps[:, 5, t * P:(t + 1) * P],
                                         scalar=rtok[:, 2 + t:3 + t], in1=bvb[:, :],
                                         op0=ALU.mult, op1=ALU.add).then_inc(v_ready, 1)

            def soft_in(p, g, sinks):
                dve.wait_ge(s_mm, up(p + 1, g, 2))
                if g is not None or p >= 1:
                    dve.wait_ge(p_ready, up(4 * p, g, 8))
                if sinks:
                    if g is not None or p >= 1:
                        dve.wait_ge(es_ready, up(p, g, 2))
                    b = mask.unsqueeze(1).broadcast_to([P, 2, 2 * T])
                else:
                    dve.wait_ge(bias_in[p % 2], up(((p - 8) // 2 + 1) * 16, g, 16))
                    b = bias[:, p % 2, :].rearrange("p (h n) -> p h n", h=2)
                ins = dve.scalar_tensor_tensor(out=s[:, :, :].rearrange("p (h t) k -> p h (t k)", h=2),
                                               in0=ps[:, 4:6, :], scalar=HD ** -0.5, in1=b,
                                               op0=ALU.mult, op1=ALU.add)
                ins.then_inc(s_ready, 1)
                dve.wait_ge(s_ready, up(p + 1, g, 2))
                dve.tensor_reduce(mx, s[:, :, :], AX_X, ALU.max).then_inc(mx_ready, 1)
                dve.wait_ge(mx_ready, up(p + 1, g, 2))
                if sinks:
                    sink = tiles(sinkb, p, g, 2)
                    dve.tensor_tensor(mx.unsqueeze(1), mx.unsqueeze(1), sink, ALU.max).then_inc(mxs_ready, 1)
                    dve.wait_ge(mxs_ready, up(p + 1, g, 2))
                dve.tensor_scalar(negm, mx, -1.0, None, ALU.mult).then_inc(negm_ready, 1)
                dve.wait_ge(negm_ready, up(p + 1, g, 2))
                if sinks:
                    dve.tensor_tensor(dsk.unsqueeze(1), negm.unsqueeze(1), sink, ALU.add).then_inc(dsk_ready, 1)

            def soft_sum(p, g, sinks):
                par = p % 2
                dve.wait_ge(p_ready, up(4 * p + 4, g, 8))
                if sinks:
                    dve.wait_ge(es_ready, up(p + 1, g, 2))
                    dve.tensor_tensor(small_den[:, par, :], small_den[:, par, :], small_es[:, par, :],
                                      ALU.add).then_inc(den_ready, 1)
                    dve.wait_ge(den_ready, up(p + 1, g, 2))
                dve.reciprocal(small_rc[:, par, :], small_den[:, par, :]).then_inc(rc_ready, 1)

            def o_out(p, g):
                dve.wait_ge(o_mm, up(p + 1, g, 2))
                dve.wait_ge(rc_ready, up(p + 1, g, 2))
                if g is not None or p >= 1:
                    dve.wait_ge(ot_mm, up(p, g, 2))
                r = small_rc[:, p % 2, :].rearrange("p (h t) -> p t h", h=2).unsqueeze(3).broadcast_to([P, NT, 2, HD])
                dve.tensor_tensor(on[:, :, :].rearrange("p t (h d) -> p t h d", h=2),
                                  ps[:, 2 + (p + 1) % 2, T:2 * T].rearrange("p (t h d) -> p t h d", t=NT, h=2),
                                  r, ALU.mult).then_inc(on_ready, 1)

            def swa_step(m, g=None):
                later = g is not None or m >= 3
                y = tmp[4 + (m + 1) % 2][:, :].unsqueeze(1)
                if m < 8:
                    lo(C_QG + 3 + 2 * m, g)
                if later:
                    dve.wait_ge(ot_mm, up(m - 2, g, 2))
                    dve.wait_ge(th_ready, up(m - 2, g, 2))
                    dve.tensor_tensor(y, ps[:, 2 + m % 2:3 + m % 2, T:2 * T], tiles(sgate, m - 3, g, 2),
                                      ALU.mult).then_inc(yf_ready, 1)
                if m < 8:
                    dve.wait_ge(chunk_done, up(C_QG + 1 + 2 * m, g, 4))
                    rope_in(m + 1, m % 2, column(vec[:, V_BQ:V_BQ + 8], m, g, 2), g)
                if 1 <= m <= 8:
                    soft_in(m - 1, g, True)
                    dve.wait_ge(gate_ready, up(m, g, 2))
                    k = (m - 1) % 2
                    dve.scalar_tensor_tensor(out=tiles(sgate, m - 1, g, 2), in0=th[:, k:k + 1, :], scalar=1.0,
                                             in1=gr2[:, k:k + 1, :], op0=ALU.add, op1=ALU.mult).then_inc(th_ready, 1)
                if 2 <= m <= 9:
                    o_out(m - 2, g)
                if m < 8:
                    lo(C_QG + 4 + 2 * m, g)
                if later:
                    y_low(m - 3, AG + m - 3, y, g, 2)
                if m < 8:
                    dve.wait_ge(chunk_done, up(C_QG + 2 + 2 * m, g, 4))
                    dve.scalar_tensor_tensor(out=gr2[:, m % 2, :], in0=ps[:, 2 + m % 2, 0:T], scalar=0.5,
                                             in1=R[:, 1, :], op0=ALU.mult, op1=ALU.mult).then_inc(gr_ready, 1)
                    rope_out(m + 1, m % 2, g)
                if 1 <= m <= 8:
                    soft_sum(m - 1, g, True)
                if m < 8:
                    ada_tile(32 + m, g)

            def steps(eng, step):
                for m in range(4):
                    step(m)
                with eng.Fori(1, 3) as g:
                    step(2, g)
                    step(3, g)
                for m in range(8, 11):
                    step(m)

            steps(dve, swa_step)

            def bout_step(n, g):
                lo(C_BOUT + 3 + n, g)
                dve.wait_ge(chunk_done, up(C_BOUT + n + 1, g, 4))
                dve.tensor_tensor(tiles(x, n, g, 4), tiles(x, n, g, 4), ps[:, n % 2:n % 2 + 1, 0:T],
                                  ALU.add).then_inc(x_ready, 1)

            with dve.Fori(0, 2) as g:
                for n in range(4):
                    bout_step(n, g)
            rms(2, D, EPS_A, ps[:, 7, 0:T])
            dve.wait_ge(psn_ready, 4)
            link(dve.tensor_tensor(tmp[0][:, :], R[:, 0, :], R[:, 0, :], ALU.mult))
            link(dve.tensor_tensor(tmp[0][:, :], tmp[0][:, :], ps[:, 7, T:2 * T], ALU.mult))
            rms(3, D, EPS_B, tmp[0][:, :])
            for kc in range(KC):
                dve.scalar_tensor_tensor(out=x[:, kc, :], in0=x[:, kc, :], scalar=vec[:, V_FG + kc:V_FG + kc + 1],
                                         in1=R[:, 0, :], op0=ALU.mult, op1=ALU.mult).then_inc(x_ready, 1)

            def modulated(k, gains, shifts):
                for kc in range(KC):
                    if k == 0:
                        dve.wait_ge(x_ready, 16 + kc + 1)
                    dve.scalar_tensor_tensor(out=F[:, kc, :], in0=x[:, kc, :], scalar=gains[:, kc:kc + 1],
                                             in1=R[:, 1 - k, :], op0=ALU.mult, op1=ALU.mult).then_inc(mt_ready, 1)
                for kc in range(KC):
                    dve.wait_ge(mt_ready, k * KC + kc + 1)
                    dve.tensor_scalar(F[:, kc, :], F[:, kc, :], shifts[:, kc:kc + 1], None, ALU.add).then_inc(xg_ready, 1)
                for kc in range(KC):
                    dve.wait_ge(xh_ready, (3 + k) * KC + kc + 1)
                    dve.tensor_tensor(X1L[:, kc, :], F[:, kc, :], X1H[:, kc, :].bitcast(F32),
                                      ALU.subtract).then_inc(xl_ready, 1)

            modulated(0, s1, mod[:, 0:8])

            def v2_step(q, g):
                lo(C_V2 + 2 * q + 3, g)
                lo(C_V2 + 2 * q + 4, g)

            with dve.Fori(0, 2) as g:
                for q in range(2):
                    v2_step(q, g)

            def mix_step(m, g=None):
                if m < 8:
                    lo(C_QK + 2 * m + 3, g)
                if g is not None or m >= 3:
                    dve.wait_ge(ot_mm, up(8 + m - 2, g, 2))
                    dve.tensor_copy(tiles(oT, m - 3, g, 2), ps[:, 2 + m % 2:3 + m % 2, T:2 * T]).then_inc(ot_done, 1)
                if 1 <= m <= 8:
                    soft_in(8 + m - 1, g, False)
                if 2 <= m <= 9:
                    o_out(8 + m - 2, g)
                if m < 8:
                    lo(C_QK + 2 * m + 4, g)
                    dve.wait_ge(chunk_done, up(C_QK + 2 * m + 2, g, 4))
                    if g is not None or m >= 2:
                        dve.wait_ge(s_mm, up(8 + m - 1, g, 2))
                    dve.tensor_copy(ks[:, m % 2, :], ps[:, 2 + m % 2, 0:T]).then_inc(k_ready, 1)
                if 1 <= m <= 8:
                    soft_sum(8 + m - 1, g, False)
                if m < 8:
                    ada_tile(40 + m, g)

            steps(dve, mix_step)
            rms(4, D // 2, EPS_B, ps[:, 0, T:2 * T])
            dve.wait_ge(ada_used, NMOD)
            link(dve.tensor_tensor(mod[:, 32:48], modT[:, 32:48], vec[:, V_ADAB + 32:V_ADAB + 48], ALU.add))
            link(dve.tensor_scalar(s2, mod[:, 32:40], 1.0, None, ALU.add))
            link(dve.tensor_tensor(s2, s2, vec[:, V_N2:V_N2 + 8], ALU.mult))
            dve.wait_ge(ot_done, NPAIR)

            def normed(k):
                for n in range(4 * k, 4 * k + 4):
                    dve.scalar_tensor_tensor(out=FY[:, n, :], in0=oT[:, n, :], scalar=vec[:, V_OG + n:V_OG + n + 1],
                                             in1=R[:, k, :], op0=ALU.mult, op1=ALU.mult).then_inc(yf_ready, 1)

            def normed_low(k):
                for n in range(4 * k, 4 * k + 4):
                    y_low(n, AG + 8 + n, FY[:, n:n + 1, :], None, 1)

            normed(0)
            rms(5, D // 2, EPS_B, ps[:, 7, 0:T])
            normed(1)
            normed_low(0)
            normed_low(1)

            def cout_step(n, g):
                lo(C_COUT + 3 + n, g)
                dve.wait_ge(chunk_done, up(C_COUT + n + 1, g, 4))
                dve.scalar_tensor_tensor(out=tiles(x, n, g, 4), in0=ps[:, n % 2:n % 2 + 1, 0:T],
                                         scalar=column(mod[:, 16:24], n, g, 4), in1=tiles(x, n, g, 4),
                                         op0=ALU.mult, op1=ALU.add).then_inc(x_ready, 1)

            with dve.Fori(0, 2) as g:
                for n in range(4):
                    cout_step(n, g)
            dve.wait_ge(bias_in[0], (NPAIR // 2 + 1) * 16)
            dve.tensor_tensor(diags[:, :, :], ident.unsqueeze(1).broadcast_to([P, KC, P]),
                              mod[:, 40:48].unsqueeze(2).broadcast_to([P, KC, P]), ALU.mult).then_inc(diag_ready, 1)

            rms(6, D, EPS_B, ps[:, 7, 0:T])
            modulated(1, s2, mod[:, 24:32])
            def top16(rows, firsts, bests, places):
                a = [link.mark(dve.max(b[:, 0:8], row)) for row, b in zip(rows, bests)]
                for row, b, place, first in zip(rows, bests, places, a):
                    link.after(first)
                    link.mark(dve.max_index(place[:, 0:8], b[:, 0:8], row))
                c = [link.mark(dve.match_replace(rest, b[:, 0:8], row, NEG)) for row, rest, b in zip(rows, firsts, bests)]
                d = []
                for rest, b, replaced in zip(firsts, bests, c):
                    link.after(replaced)
                    d.append(link.mark(dve.max(b[:, 8:16], rest)))
                for rest, b, place, second in zip(firsts, bests, places, d):
                    link.after(second)
                    last = link.mark(dve.max_index(place[:, 8:16], b[:, 8:16], rest))
                return last

            for n in range(2 * PH):
                lo(C_WQ + 3 + n)
                dve.wait_ge(sc_ready, n + 1)
                last = top16([sc[:, n % 2, t, :] for t in range(NT)], [sc2[:, t, :] for t in range(NT)],
                             [v16[:, t, n, :] for t in range(NT)], [ix8[:, t, :] for t in range(NT)])
                link.after(last)
                dve.tensor_copy(i16[:, :, n, :], ix8[:, :, :]).then_inc(sc_used, 1)
            dve.wait_ge(sc_used, 2 * PH)

            vr = v16[:, :, :, :].rearrange("p t (h q) k -> p (t h) q k", q=2)
            ir = i16[:, :, :, :].rearrange("p t (h q) k -> p (t h) q k", q=2)
            steps_ = [(a, a + 1, ROWS[a], STARTS[a]) for a in range(8)] + [(8, TOPK, 1, STARTS[8])]
            R16 = NT * PH
            for a, b, n, at0 in steps_:
                w = n * (b - a)
                va, ia = vr[:, :, 0, a:b], ir[:, :, 0, a:b]
                vb, ib = vr[:, :, 1, 0:n], ir[:, :, 1, 0:n]
                if n > 1:
                    va, ia = va.broadcast_to([P, R16, n]), ia.broadcast_to([P, R16, n])
                elif b - a > 1:
                    vb, ib = vb.broadcast_to([P, R16, b - a]), ib.broadcast_to([P, R16, b - a])
                link.mark(dve.tensor_tensor(cand[:, :, at0:at0 + w], va, vb, ALU.add))
                link.mark(dve.scalar_tensor_tensor(out=cid[:, :, at0:at0 + w], in0=ia, scalar=float(NK), in1=ib,
                                                   op0=ALU.mult, op1=ALU.add))
            link.after(link.n)
            for r in range(1, R16, 2):
                rs = (r - 1, r)
                last = top16([cand[:, k, :] for k in rs], [sc2[:, k % 2, 0:NCAND] for k in rs],
                             [best[:, k, :] for k in rs], [pos[:, k, :] for k in rs])
            link.after(last)
            link(dve.tensor_copy(zsum[:, :], best[:, :, 0]))
            dve.tensor_tensor(best[:, :, :], best[:, :, :], zsum[:, :].unsqueeze(2).broadcast_to([P, R16, TOPK]),
                              ALU.subtract).then_inc(exp_in, 1)
            link(dve.tensor_copy(posf[:, :, :], pos[:, :, :]))
            link(dve.tensor_tensor(eq[:, :, :, :].rearrange("p r k c -> p (r k) c"),
                                   posf[:, :, :].rearrange("p r k -> p (r k)").unsqueeze(2)
                                   .broadcast_to([P, R16 * TOPK, NCAND]),
                                   iota[:, 0:NCAND].unsqueeze(1).broadcast_to([P, R16 * TOPK, NCAND]), ALU.is_equal))
            link(dve.tensor_tensor(eq[:, :, :, :], eq[:, :, :, :],
                                   cid[:, :, :].unsqueeze(2).broadcast_to([P, R16, TOPK, NCAND]), ALU.mult))
            link(dve.tensor_reduce(sid[:, :, :], eq[:, :, :, :], AX_X, ALU.add))
            link(dve.tensor_copy(pos[:, :, :], sid[:, :, :]))
            link(dve.tensor_scalar(posi[:, :, :], pos[:, :, :], 7, None, ALU.logical_shift_right))
            link(dve.tensor_scalar(pos[:, :, :], pos[:, :, :], NK - 1, None, ALU.bitwise_and))
            link(dve.tensor_copy(i1[:, :, :], posi[:, :, :]))
            link(dve.tensor_copy(i2[:, :, :], pos[:, :, :]))
            dve.wait_ge(exp_ready, 1)
            link(dve.tensor_reduce(zsum[:, :], best[:, :, :], AX_X, ALU.add))
            link(dve.reciprocal(zsum[:, :], zsum[:, :]))
            dve.tensor_tensor(best[:, :, :], best[:, :, :], zsum[:, :].unsqueeze(2).broadcast_to([P, R16, TOPK]),
                              ALU.mult).then_inc(lists_ready, 1)
            dve.wait_ge(lt_ready, 3)

            dve.wait_ge(gelu_ready, EARLY)
            by_eights = W[:, :, :].rearrange("p j (e t) -> p e t j", t=8)

            def early_gated(e, g=None):
                dve.wait_ge(gate_out, up(2 * e + 2, g, 4))
                if g is None:
                    w8 = by_eights[:, e]
                else:
                    w8 = by_eights.rearrange("p (g k) t j -> p k g t j", k=2)[:, e % 2, bass.ds(g + e // 2, 1)]\
                        .rearrange("p a t j -> p (a t) j")
                gates = ps[:, 2 * (e % 2):2 * (e % 2) + 2, :].rearrange("p b (t n) -> p (b t) n", t=4)[:, :, 0:EARLY]
                dve.tensor_tensor(w8, w8, gates, ALU.mult).then_inc(gm_ready, 1)

            def eight_step(e, g=None):
                if g is not None or e >= 2:
                    early_gated(e - 2, g)
                    dve.wait_ge(gate_mm, up(8 * e - 12, g, 16))
                dve.tensor_tensor(O2[0][:, e, :, :], *hot2_in(e, 0, g), ALU.is_equal).then_inc(hot2_ready[0], 1)
                for n in range(8):
                    if g is not None or e >= 1:
                        dve.wait_ge(gate_mm, up(8 * e + n - 7, g, 16))
                    dve.tensor_scalar(O1[:, n, :], iota, column(tmp[1], 8 * e + n, g, 16),
                                      column(tmp[0], 8 * e + n, g, 16), ALU.is_equal, ALU.mult).then_inc(hot_ready, 1)

            rounds(dve, eight_step)
            early_gated(T // 8 - 2)
            early_gated(T // 8 - 1)

            dve.wait_ge(gm_ready, T // 8)

            def early_down(j, g=None):
                dve.wait_ge(wh_ready, up(j + 1, g, 4))
                if g is not None or j >= 2:
                    dve.wait_ge(chunk_done, up(C_V1 + j - 1, g, 4))
                dve.tensor_tensor(wvL[:, j % 2:j % 2 + 1, :], tiles(W, j, g, 4),
                                  wvH[:, j % 2:j % 2 + 1, :].bitcast(F32), ALU.subtract).then_inc(wl_ready, 1)
                lo(C_V1 + 3 + j, g)

            fours(dve, EARLY, early_down)

            def gated(i, g=None):
                dve.wait_ge(gelu_ready, up(EARLY + i + 1, g, 2))
                if g is not None or i >= 2:
                    dve.wait_ge(wl_ready, up(EARLY + i - 1, g, 2))
                gi = G[:, :, i:i + 1] if g is None else \
                    G[:, :, 1:LATE - 1].rearrange("p t (g j) -> p j t g", j=2)[:, i - 1, :, bass.ds(g, 1)]
                dve.tensor_tensor(tmp[2 + i % 2][:, :].unsqueeze(2), tmp[i % 2][:, :].unsqueeze(2), gi,
                                  ALU.mult).then_inc(w_ready, 1)

            def w_low(i, g=None):
                dve.wait_ge(wh_ready, up(EARLY + i + 1, g, 2))
                dve.wait_ge(chunk_done, up(C_UV + 2 * i - 1, g, 4))
                dve.tensor_tensor(wvL[:, i % 2, :], tmp[2 + i % 2][:, :], wvH[:, i % 2, :].bitcast(F32),
                                  ALU.subtract).then_inc(wl_ready, 1)

            lo(C_UV + 3)
            gated(0)
            w_low(0)
            lo(C_UV + 4)
            lo(C_UV + 5)

            def column_step(i, g=None):
                gated(i, g)
                w_low(i, g)
                lo(C_UV + 4 + 2 * i, g)
                lo(C_UV + 5 + 2 * i, g)

            column_step(1)
            column_step(2)
            with dve.Fori(1, (LATE - 4) // 2) as g:
                column_step(1, g)
                column_step(2, g)
            column_step(LATE - 3)
            for i in (LATE - 2, LATE - 1):
                gated(i)
                w_low(i)

            dve.wait_ge(fin_in, 48)
            dve.wait_ge(chunk_done, NCHUNK)
            for t in range(NT):
                for h in range(2):
                    cols = slice(h * 512, h * 512 + 512)
                    link(dve.tensor_tensor(yo[:, t, cols], ps[:, 4 + 2 * t + h, :], g2r[:, cols], ALU.mult))
                dve.tensor_tensor(yo[:, t, :], yo[:, t, :], xt2[:, t, :], ALU.add).then_inc(fy_ready, 1)
            dve.wait_ge(fsum_ready, NT)
            dve.tensor_scalar(st0, fsum, 1.0 / D, EPS_B, ALU.mult, ALU.add).then_inc(ln_m, 1)
            dve.wait_ge(ln_root, 2)
            link(dve.reciprocal(rstd, st1))
            newton(rstd, st0, st1, ln_r)
            dve.wait_ge(ln_r, 2)
            for t in range(NT):
                dve.scalar_tensor_tensor(out=yo[:, t, :], in0=yo[:, t, :], scalar=rstd[:, t:t + 1],
                                         in1=fgr[:, :], op0=ALU.mult, op1=ALU.mult).then_inc(out_ready, 1)

        @block.gpsimd
        def _(pool):
            pool.wait_ge(a_in, 64)
            pool.affine_select(out=ws[:, :, :], in_=ws[:, :, :], compare_op=ALU.is_ge, fill=0.0, base=0,
                               pattern=[[0, AG], [1, P]], channel_multiplier=-1).then_inc(ws_ready, 1)
            pool.wait_ge(xhat_ready, 2)
            Vg = V[:, :, :].rearrange("p c (n d) -> p n c d", d=P)

            def v_affine(n, g=None):
                if g is not None or n >= 2:
                    pool.wait_ge(sv_mm, up(n - 1, g, 2))
                src = Vg[:, n] if g is None else \
                    Vg.rearrange("p (g j) c d -> p j g c d", j=2)[:, n % 2, bass.ds(g + n // 2, 1)].rearrange(
                        "p a c d -> p (a c) d")
                dst = vs[:, n % 2, :].rearrange("p (c d) -> p c d", c=NT)
                pool.tensor_tensor(dst, src, tiles(lng, n, g, 2).broadcast_to([P, NT, P]), ALU.mult)\
                    .then_inc(vg_ready, 1)
                pool.wait_ge(vg_ready, up(n + 1, g, 2))
                pool.tensor_tensor(dst, dst, tiles(lnb, n, g, 2).broadcast_to([P, NT, P]), ALU.add)\
                    .then_inc(vs_ready, 1)

            def gate_product(n, g=None):
                m = tmp[4 + n % 2][:, :]
                pool.wait_ge(sg_ready, up(n + 1, g, 2))
                pool.wait_ge(svb_ready, up(n + 1, g, 2))
                if g is not None or n >= 2:
                    pool.wait_ge(yl_ready, up(n - 1, g, 2))
                pool.tensor_tensor(m, tmp[n % 2][:, :], tmp[2 + n % 2][:, :], ALU.mult).then_inc(mg_ready, 1)
                pool.wait_ge(mg_ready, up(n + 1, g, 2))
                pool.wait_ge(ur_ready, up(n + 1, g, 2))
                pool.tensor_tensor(m, m, uR[:, n % 2, :], ALU.mult).then_inc(yf_ready, 1)

            v_affine(0)
            v_affine(1)
            for n in range(2):
                gate_product(n)
                v_affine(n + 2)
            with pool.Fori(1, 7) as g:
                for n in range(2):
                    gate_product(n, g)
                    v_affine(n + 2, g)
            for n in range(14, 16):
                gate_product(n)

            pool.wait_ge(yl_ready, AG)
            pool.memset(tmp[5][:, :], 0.0).then_inc(acc_clear, 1)
            pool.wait_ge(acc_clear, 1)

            def add_square(k, acc, g=None):
                pool.wait_ge(sq_ready, up(k + 2, g, 1))
                if g is not None or k >= 1:
                    pool.wait_ge(sacc_done, up(k, g, 1))
                pool.tensor_tensor(acc, acc, tmp[4][:, :], ALU.add).then_inc(sacc_done, 1)

            add_square(0, tmp[5][:, :])
            with pool.Fori(0, KC - 1) as g:
                add_square(1, tmp[5][:, :], g)

            def rope(i, dst, waits, g=None):
                k = i % 2
                pool.wait_ge(qb_ready, up(i + 1, g, 2))
                pool.tensor_tensor(t3[:, k, :], qb[:, k, :], cosT, ALU.mult).then_inc(rope_c, 1)
                pool.wait_ge(rope_c, up(i + 1, g, 2))
                pool.wait_ge(rope_s, up(i + 1, g, 2))
                if waits is not None:
                    pool.wait_ge(s_mm, waits)
                pool.tensor_tensor(dst, t3[:, k, :], tmp[2 + k][:, :], ALU.add).then_inc(q_ready, 1)

            rope(0, ks[:, 0, :], None)
            for m in range(2):
                rope(m + 1, qs[:, m, :], None)
            with pool.Fori(0, 3) as g:
                for m in range(2, 4):
                    rope(m + 1, qs[:, m % 2, :], up(m - 1, g, 2), g)

            def clear(acc, n):
                pool.memset(acc, 0.0).then_inc(acc_clear, 1)
                pool.wait_ge(acc_clear, n)

            pool.wait_ge(yl_ready, AG + 8)
            clear(tmp[5][:, :], 2)
            clear(tmp[2][:, :], 3)
            with pool.Fori(0, KC) as g:
                for k, (acc, square) in enumerate(((tmp[5], tmp[4]), (tmp[2], tmp[3]))):
                    pool.wait_ge(sq_ready, up(8 + k + 2, g, 2))
                    pool.wait_ge(sacc_done, up(8 + k, g, 2))
                    pool.tensor_tensor(acc[:, :], acc[:, :], square[:, :], ALU.add).then_inc(sacc_done, 1)
            pool.wait_ge(psn_ready, 4)
            clear(tmp[5][:, :], 4)
            with pool.Fori(0, 4) as g:
                add_square(24, tmp[5][:, :], g)
            clear(qb[:, 0, :], 5)
            with pool.Fori(0, 4) as g:
                add_square(28, qb[:, 0, :], g)
            pool.wait_ge(psn_ready, 6)
            clear(tmp[5][:, :], 6)
            with pool.Fori(0, KC) as g:
                add_square(32, tmp[5][:, :], g)

            pool.wait_ge(l_done, C_U + 3)

            def early_low(j, g=None):
                c = C_U + 3 + j
                slot = c % RING
                pool.wait_ge(h_done, up(c + 1, g, RING))
                pool.tensor_tensor(WL[:, slot, :], raw[:, slot, :], WH[:, slot, :].bitcast(F32),
                                   ALU.subtract).then_inc(l_done, 1)

            fours(pool, EARLY, early_low)

            pool.wait_ge(lt_ready, 3)

            def eight_step(e, g=None):
                if g is not None:
                    pool.wait_ge(gate_mm, up(8 * e - 8, g, 16))
                pool.tensor_tensor(O2[1][:, e, :, :], *hot2_in(e, 1, g), ALU.subtract).then_inc(dist_ready, 1)

            rounds(pool, eight_step)

        @block.tensor
        def _(pe):
            pe.wait_ge(ones_ready, 1)
            pe.wait_ge(c_in, 32)

            def product(out_ap, stat, mov, k0=0, first=True, last=True):
                sH, sL, mH, mL = (*stat, *mov)
                for kc in range(KC):
                    for i, (a, b) in enumerate(((sH, mH), (sH, mL), (sL, mH))):
                        mm = pe.matmul(out_ap, a(kc), b(kc), start=(first and kc == 0 and i == 0),
                                       stop=(last and kc == KC - 1 and i == 2))
                return mm

            def weight(W, slot, n=1):
                if n == 1:
                    return lambda kc: W[:, slot, kc * P:(kc + 1) * P]
                return lambda kc: W[:, slot:slot + n, kc * P:(kc + 1) * P]

            def acts(X, k0=0):
                return lambda kc: X[:, k0 + kc, :]

            def feature_tile(c, g, bank, XH, XL, k0=0, first=True, last=True):
                pe.wait_ge(l_done, up(c + 1, g, RING))
                mm = product(ps[:, bank, 0:T], (weight(WH, c % RING), weight(WL, c % RING)),
                             (acts(XH, k0), acts(XL, k0)), first=first, last=last)
                mm.then_inc(chunk_done, 1)

            def token_tiles(c, g, bank, XH, XL, n):
                pe.wait_ge(l_done, up(c + n, g, RING))
                for t in range(NT):
                    def x_tile(X):
                        return lambda kc: X[:, kc, t * P:(t + 1) * P]
                    o = ps[:, bank + t, 0:n * P] if n > 1 else ps[:, bank, t * P:(t + 1) * P]
                    if n > 1:
                        o = o.rearrange("p (a n) -> p a n", a=n)
                    mm = product(o, (x_tile(XH), x_tile(XL)),
                                 (weight(WH, c % RING, n), weight(WL, c % RING, n)))
                mm.then_inc(chunk_done, n)

            def spread(k, ready, count, acc, bank=7, at0=0):
                pe.wait_ge(ready, count)
                pe.matmul(ps[:, bank, at0:at0 + T], ones[:, :], acc, start=True, stop=True).then_inc(psn_ready, 1)

            def turn_rms(k):
                pe.wait_ge(r_ready, k + 1)
                for t in range(NT):
                    mm = pe.transpose(ps[:, 7, T + t * P:T + (t + 1) * P], R[:, k % 2, t * P:(t + 1) * P], ident)
                mm.then_inc(rt_ready, 1)

            spread(0, sum_ready, 1, tmp[5][:, :])
            pe.wait_ge(xl_ready, KC)
            for q in range(2):
                token_tiles(2 * q, None, 2 * q, X1H, X1L, 2)
                if q == 0:
                    turn_rms(0)
            with pe.Fori(1, 4) as g:
                for q in range(2):
                    pe.wait_ge(v_out, up(2 * q - 2, g, 4))
                    token_tiles(2 * q, g, 2 * q, X1H, X1L, 2)
            pe.wait_ge(v_out, 16)

            def ug_step(n, g=None):
                later = g is not None or n >= 2
                if later:
                    pe.wait_ge(ur_ready, up(n - 1, g, 2))
                feature_tile(C_UG + 2 * n, g, n % 2, X1H, X1L)
                if later:
                    pe.wait_ge(gr_ready, up(n - 1, g, 2))
                feature_tile(C_UG + 1 + 2 * n, g, 2 + n % 2, X1H, X1L)
                if later:
                    pe.wait_ge(svb_ready, up(n - 1, g, 2))
                pe.wait_ge(vs_ready, up(n + 1, g, 2))
                pe.wait_ge(ws_ready, 1)
                w = tiles(ws, n, g, 2)
                for c in range(NT):
                    mm = pe.matmul(ps[:, 4 + n % 2, c * P:(c + 1) * P], vs[:, n % 2, c * P:(c + 1) * P],
                                   w.rearrange("p a t -> p (a t)"), start=True, stop=True)
                mm.then_inc(sv_mm, 1)

            ug_step(0)
            ug_step(1)
            with pe.Fori(1, AG // 2) as g:
                for n in range(2):
                    ug_step(n, g)
            pe.wait_ge(ur_ready, AG)
            pe.wait_ge(yl_ready, KC)

            def aout_step(n, g=None):
                if g is not None or n >= 2:
                    pe.wait_ge(x_ready, up(n - 1, g, 2))
                feature_tile(C_AOUT + 2 * n, g, n % 2, YH, YL, 0, True, False)
                if g is None and n == 0:
                    pe.wait_ge(yl_ready, AG)
                feature_tile(C_AOUT + 2 * n + 1, g, n % 2, YH, YL, KC, False, True)

            aout_step(0)
            aout_step(1)
            with pe.Fori(1, 4) as g:
                for n in range(2):
                    aout_step(n, g)
            pe.wait_ge(xl_ready, 3 * KC)
            feature_tile(C_KV, None, 6, X1H, X1L)
            spread(1, sacc_done, KC, tmp[5][:, :])
            token_tiles(C_KV + 1, None, 5, X1H, X1L, 1)
            pe.wait_ge(b_in, 48)

            def rope_turn(i, bank, g=None):
                pe.wait_ge(qb_ready, up(i + 1, g, 2))
                pe.matmul(ps[:, bank, T:2 * T], perm, qb[:, i % 2, :], start=True, stop=True).then_inc(rope_mm, 1)

            def scores(p, g, kslot):
                for h in range(2):
                    hs = slice(h * HD, (h + 1) * HD)
                    for t in range(NT):
                        mm = pe.matmul(ps[:, 4 + h, t * T:(t + 1) * T], qs[hs, p % 2, t * P:(t + 1) * P],
                                       ks[hs, kslot, :], start=True, stop=True)
                mm.then_inc(s_mm, 1)

            def turn_probs(p, g):
                pe.wait_ge(p_ready, up(4 * p + 4, g, 8))
                if g is not None or p >= 1:
                    pe.wait_ge(pt_ready, up(2 * p, g, 4))
                for h in range(2):
                    for kt in range(NT):
                        for t in range(NT):
                            k = kt * NT + t
                            mm = pe.transpose(ps[:, 6 + h, k * P:(k + 1) * P],
                                              pr[:, 2 * h + t, kt * P:(kt + 1) * P], ident)
                mm.then_inc(pt_mm, 1)

            def values(p, g, v_of):
                pe.wait_ge(pt_ready, up(2 * p + 2, g, 4))
                for t in range(NT):
                    for h in range(2):
                        for kt in range(NT):
                            mm = pe.matmul(ps[:, 2 + (p + 1) % 2, T + t * P + h * HD:T + t * P + (h + 1) * HD],
                                           pT[:, h, kt * NT + t, :], v_of(kt, h),
                                           start=(kt == 0), stop=(kt == NT - 1))
                mm.then_inc(o_mm, 1)

            def turn_out(p, g):
                pe.wait_ge(on_ready, up(p + 1, g, 2))
                for t in range(NT):
                    mm = pe.transpose(ps[:, 2 + (p + 1) % 2, T + t * P:T + (t + 1) * P], on[:, t, :], ident)
                mm.then_inc(ot_mm, 1)

            rope_turn(0, 6)
            turn_rms(1)
            pe.wait_ge(v_ready, 2)

            def swa_step(m, g=None):
                if m < 8:
                    if g is not None or m >= 2:
                        pe.wait_ge(rope_s, up(m, g, 2))
                    feature_tile(C_QG + 2 * m, g, m % 2, X2H, X2L)
                if 1 <= m <= 8:
                    pe.wait_ge(q_ready, up(m + 1, g, 2))
                    if g is not None or m >= 2:
                        pe.wait_ge(s_ready, up(m - 1, g, 2))
                    scores(m - 1, g, 0)
                if m >= 2:
                    pe.wait_ge(gr_ready, up(AG + min(m, 8), g, 2))
                    if m == 9:
                        pe.wait_ge(yf_ready, AG + 6)
                    values(m - 2, g, lambda kt, h: vB[:, kt, h * HD:(h + 1) * HD])
                if m < 8:
                    if g is not None or m >= 3:
                        pe.wait_ge(yf_ready, up(AG + m - 2, g, 2))
                    feature_tile(C_QG + 2 * m + 1, g, 2 + m % 2, X2H, X2L)
                    rope_turn(m + 1, m % 2, g)
                if 1 <= m <= 8:
                    turn_probs(m - 1, g)
                if m >= 2:
                    turn_out(m - 2, g)

            def steps(eng, step):
                for m in range(4):
                    step(m)
                with eng.Fori(1, 3) as g:
                    step(2, g)
                    step(3, g)
                for m in range(8, 10):
                    step(m)

            steps(pe, swa_step)

            def out_steps(c, count, x0):
                pe.wait_ge(yl_ready, count)
                with pe.Fori(0, 2) as g:
                    for n in range(4):
                        pe.wait_ge(x_ready, up(x0 + n - 1, g, 4))
                        feature_tile(c + n, g, n % 2, YH, YL)

            out_steps(C_BOUT, AG + 8, 8)
            spread(2, sacc_done, 24, tmp[5][:, :])
            pe.wait_ge(m_ready, 3)
            spread(3, sacc_done, 24, tmp[2][:, :], at0=T)
            pe.wait_ge(xl_ready, 4 * KC)
            with pe.Fori(0, 2) as g:
                for q in range(2):
                    pe.wait_ge(v_out, up(16 + 2 * q - 2, g, 4))
                    token_tiles(C_V2 + 2 * q, g, 2 * q, X1H, X1L, 2)
            vCv = vC[:, :, :].rearrange("p t (m n) -> p t m n", n=P)

            def mix_step(m, g=None):
                if m < 8:
                    pe.wait_ge(v_out, 24) if g is None and m < 2 else pe.wait_ge(qt_ready, up(m - 1, g, 2))
                    feature_tile(C_QK + 2 * m, g, m % 2, X1H, X1L)
                if 1 <= m <= 8:
                    p = m - 1
                    pe.wait_ge(qt_ready, up(p + 1, g, 2))
                    pe.wait_ge(k_ready, up(p + 1, g, 2))
                    pe.wait_ge(s_ready, up(8 + p, g, 2))
                    scores(8 + p, g, p % 2)
                if m >= 2:
                    p = m - 2
                    pe.wait_ge(k_ready, up(min(m, 8), g, 2))
                    if m == 9:
                        pe.wait_ge(ot_done, 6)

                    def v_of(kt, h):
                        v = tiles(vCv[:, kt], p, g, 2)[:, :, h * HD:(h + 1) * HD]
                        return v.rearrange("p a n -> p (a n)")
                    values(8 + p, g, v_of)
                if m < 8:
                    if g is not None or m >= 3:
                        pe.wait_ge(ot_done, up(m - 2, g, 2))
                    feature_tile(C_QK + 2 * m + 1, g, 2 + m % 2, X1H, X1L)
                if 1 <= m <= 8:
                    turn_probs(8 + m - 1, g)
                if m >= 2:
                    turn_out(8 + m - 2, g)
                if m == 8:
                    spread(4, sacc_done, 28, tmp[5][:, :], bank=0, at0=T)

            steps(pe, mix_step)
            spread(5, sacc_done, 32, qb[:, 0, :])
            out_steps(C_COUT, AG + 16, 24)
            spread(6, sacc_done, 40, tmp[5][:, :])
            pe.wait_ge(m_ready, 7)
            for t in range(NT):
                for kc in range(KC):
                    mm = pe.transpose(ps[:, 4 + 2 * t + kc // 4, kc % 4 * P:(kc % 4 + 1) * P],
                                      x[:, kc, t * P:(t + 1) * P], ident)
            mm.then_inc(tr_mm, 1)
            pe.wait_ge(diag_ready, 1)
            for i in range(2):
                mm = pe.matmul(ps[:, 2 + i, :], ones[:, :],
                               diags[:, 4 * i:4 * i + 4, :].rearrange("p k n -> p (k n)"), start=True, stop=True)
            mm.then_inc(tr_mm, 1)
            pe.wait_ge(xl_ready, 5 * KC)
            pe.wait_ge(sk_in, 16)

            def wq_step(n, g=None):
                pe.wait_ge(qt_ready, up(8 + n - 1, g, 4))
                feature_tile(C_WQ + n, g, n % 2, X1H, X1L)
                pe.wait_ge(qt_ready, up(8 + n + 1, g, 4))
                if g is None and n == 0:
                    pe.wait_ge(act_link, 7)
                if g is not None or n >= 2:
                    pe.wait_ge(sc_ready, up(n - 1, g, 4))
                for t in range(NT):
                    mm = pe.matmul(ps[:, 2 + n % 2, t * P:(t + 1) * P], qt[:, n % 2, t * P:(t + 1) * P],
                                   sk[:, n % 2, :], start=True, stop=True)
                mm.then_inc(sc_mm, 1)

            for n in range(4):
                wq_step(n)
            with pe.Fori(1, 4) as g:
                for n in range(4):
                    wq_step(n, g)
            def early_up(j, g=None):
                if g is not None or j >= 2:
                    pe.wait_ge(gelu_ready, up(j - 1, g, 4))
                feature_tile(C_U + j, g, j % 2, X1H, X1L)

            fours(pe, EARLY, early_up)
            pe.wait_ge(lists_ready, 1)
            for i, src in enumerate((best, i1, i2)):
                for t in range(NT):
                    mm = pe.transpose(ps[:, 4 + i, t * P:(t + 1) * P],
                                      src[:, t * PH:(t + 1) * PH, :].rearrange("p h k -> p (h k)"), ident)
            mm.then_inc(lt_mm, 1)

            def eight_step(e, g=None):
                for n in range(8):
                    half, k = n // 4, n % 4
                    if k == 0:
                        if g is not None:
                            pe.wait_ge(gm_ready, up(e - 1, g, 2))
                        pe.wait_ge(hot2_ready[half], up(e + 1, g, 2))
                    pe.wait_ge(hot_ready, up(8 * e + n + 1, g, 16))
                    pe.matmul(ps[:, 2 * e + half, k * P:(k + 1) * P], O1[:, n, :], O2[half][:, e, k, :],
                              start=True, stop=True).then_inc(gate_mm, 1)

            rounds(pe, eight_step)

            def down(j, c, g=None, per=2, first=False, last=False):
                pe.wait_ge(l_done, up(c + 1, g, RING))
                pe.wait_ge(wl_ready, up(j + 1, g, per))
                slot = c % RING
                for t in range(NT):
                    ts_ = slice(t * P, (t + 1) * P)
                    for h in range(2):
                        hs = slice(h * 512, (h + 1) * 512)
                        for i, (a, b) in enumerate(((wvH, WH), (wvH, WL), (wvL, WH))):
                            mm = pe.matmul(ps[:, 4 + 2 * t + h, :], a[:, j % 2, ts_], b[:, slot, hs],
                                           start=(first and i == 0), stop=(last and i == 2),
                                           skip_group_check=True)
                mm.then_inc(chunk_done, 1)

            def up_tile(i, c, g=None):
                if g is not None or i >= 2:
                    pe.wait_ge(gelu_ready, up(EARLY + i - 1, g, 2))
                feature_tile(c, g, i % 2, X1H, X1L)

            pe.wait_ge(lt_ready, 3)
            fours(pe, EARLY, lambda j, g=None: down(j, C_V1 + j, g, per=4, first=(g is None and j == 0)))
            pe.wait_ge(gm_ready, T // 8)
            up_tile(0, C_UV)
            up_tile(1, C_UV + 1)
            down(EARLY, C_UV + 2)
            with pe.Fori(0, (LATE - 2) // 2) as g:
                for i in (1, 2):
                    up_tile(i + 1, C_UV + 1 + 2 * i, g)
                    down(EARLY + i, C_UV + 2 + 2 * i, g)
            down(NK - 1, NCHUNK - 1, last=True)


def _constants():
    ident = np.eye(P, dtype=np.float32)
    iota = np.tile(np.arange(P, dtype=np.float32), (P, 1))
    half = HD // 2
    perm = np.zeros((P, P), np.float32)
    for f in range(P):
        if f % HD < half:
            perm[f + half, f] = -1.0
        else:
            perm[f - half, f] = 1.0
    inv = np.float32(10000.0) ** (-np.arange(0, HD, 2, dtype=np.float32) / np.float32(HD))
    ang = np.arange(T, dtype=np.float32)[:, None] * inv[None, :]
    f = np.arange(P) % half
    cosT, sinT = np.cos(ang).astype(np.float32).T[f], np.sin(ang).astype(np.float32).T[f]
    q, k = np.arange(T)[:, None], np.arange(T)[None, :]
    window = np.where((k <= q) & (k > q - 128), 0.0, NEG).astype(np.float32)
    mask = window.reshape(NT, P, T).transpose(1, 0, 2).reshape(P, NT * T)
    d = np.abs(q - k)
    count = np.zeros((T, T))
    for span, step in ((128, 1), (512, 4), (2048, 16)):
        count += (d % step == 0) & (d <= span // 2)
    slopes = 2.0 ** (-8.0 * (np.arange(8) + 1) / 8)
    logc = np.where(count > 0, np.log(np.maximum(count, 1)), NEG)
    dil = (-slopes[:, None, None] * d[None] + logc[None]).astype(np.float32)
    return np.concatenate([ident, iota], 1), np.concatenate([perm, cosT, sinT, mask], 1), dil


def _window_index():
    grid, wr, wc = 64, 4, 16
    t = np.arange(T)
    r, c = t // grid, t % grid
    c0 = np.clip(c - wc // 2, 0, grid - wc)
    dr = r[None, :] - r[:, None] + 7
    dc = c[None, :] - c[:, None] + 15
    near = (c[None, :] >= c0[:, None]) & (c[None, :] < c0[:, None] + wc)
    assert T // grid == wr
    return dr, np.clip(dc, 0, 30), near


def kernel(**inputs):
    import concourse.bacc as _bacc
    from concourse.bass_utils import run_bass_kernel_spmd as _run

    a = {k: np.asarray(v) for k, v in inputs.items()}
    cI, cB, dil = _constants()

    def tiles_of(w):
        k, n = w.shape
        return w.reshape(k // D, KC, P, n // P, P).transpose(3, 0, 2, 1, 4).reshape(-1, P, CW)

    def weave(x, y):
        return np.stack([x, y], 1).reshape(-1, P, CW)

    pair = np.arange(D).reshape(2, 8, HD).transpose(1, 0, 2).reshape(-1)
    w = a["a_w_in"][0]
    parts = [tiles_of(w[:, AW:2 * AW]), weave(tiles_of(w[:, 0:AW]), tiles_of(w[:, 2 * AW:])),
             tiles_of(a["a_w_out"][0]), tiles_of(a["w_kv"])]
    w = a["b_w_in"][0]
    parts += [weave(tiles_of(w[:, 0:D][:, pair]), tiles_of(w[:, D:][:, pair])), tiles_of(a["b_w_out"][0][pair])]
    w = tiles_of(a["w_in_2"][0])
    parts += [w[8:12], w[20:24], weave(w[0:4], w[4:8]), weave(w[12:16], w[16:20]),
              tiles_of(a["w_out_2"][0]), tiles_of(a["peer_wq_2"][0])]
    u = a["peer_u_2"][0].reshape(NK, NK, KC, P).transpose(1, 3, 2, 0).reshape(NK, P, CW)
    v = a["peer_v_2"][0].reshape(NK, NK, D).transpose(1, 0, 2)
    parts += [u[:EARLY], v[:EARLY], u[EARLY:EARLY + 1], weave(u[EARLY + 1:], v[EARLY:-1]), v[-1:]]
    stream = np.concatenate(parts)
    assert stream.shape == (NCHUNK, P, CW)

    def cols(x):
        return x.reshape(-1, P).T

    vecs = np.concatenate([cols(x) for x in (
        a["a_norm_g"][0], a["kv_norm_g"], a["b_norm_g"][0], a["b_bq"][0][pair], a["b_kv"][0:P],
        a["norm1_g_2"][0], a["norm2_g_2"][0], a["ada_b_2"][0], a["out_norm_na_g_2"][0], a["out_norm_dil_g_2"][0],
        a["final_norm_g"])], 1)
    sinks = np.repeat(a["b_sinks"][0].reshape(2, 8).T.reshape(-1), NT)
    rows = np.concatenate([a["c_2"][0], a["a_ln_g"][0], a["a_ln_b"][0], a["a_bs"][0].reshape(-1), a["b_kv"][P:],
                           sinks, a["final_g_2"]])
    dr, dc, near = _window_index()
    na = np.where(near[None], a["na_rpb_2"][0][:, dr, dc], np.float32(NEG))
    bias = np.concatenate([na, dil]).reshape(NPAIR, 2, NT, P, T).transpose(0, 3, 1, 2, 4).reshape(NPAIR, P, 4 * T)
    def past_end(x):
        return np.concatenate([x, x[-2:]])

    arrays = {
        "stream": stream,
        "xT": a["x"][0].T.reshape(KC, P, T).transpose(1, 0, 2),
        "vecs": vecs, "cI": cI, "cB": cB, "rows": rows,
        "wsT": a["a_ws"][0].transpose(2, 0, 1),
        "adaT": past_end(a["ada_w_2"][0].T.reshape(NMOD, P, D)),
        "att_bias": past_end(bias),
        "skT": a["peer_subkeys_2"][0].transpose(2, 0, 1),
    }
    arrays = {k: np.ascontiguousarray(x) for k, x in arrays.items()}
    nc = _bacc.Bacc("TRN2", target_bir_lowering=False, num_devices=1)
    aps = [nc.dram_tensor(k, x.shape, F32, kind="ExternalInput").ap() for k, x in arrays.items()]
    spill = nc.dram_tensor("spill", [P, 3 * D], F32, kind="Internal").ap()
    out = nc.dram_tensor("out", [T, D], F32, kind="ExternalOutput").ap()
    two_block_kernel(nc, *aps, spill, out)
    got = _run(nc, [arrays], core_ids=[0]).results[0]["out"]
    return got.reshape(1, T, D)
```
